# Optimizing a Trainium2 kernel written in Bass

```python
import math
import jax, jax.numpy as jnp
from jax import lax
import numpy as np

D_MODEL = 1024
BATCH = 1
SEQ = 256
DEPTH = 2

GRID_W = 64
CTX_LEN = 256
EPS = 1e-6

A_HEADS = 4
A_HEAD_DIM = 128
A_WIDTH = A_HEADS * A_HEAD_DIM
SHORT_CONV_W = 5
DELTA_CHUNK = 64
B_Q_HEADS = 8
B_KV_HEADS = 2
B_HEAD_DIM = 64
B_GROUP = B_Q_HEADS // B_KV_HEADS
B_WIDTH = B_Q_HEADS * B_HEAD_DIM
B_KV_WIDTH = B_KV_HEADS * B_HEAD_DIM
ROPE_AXIS_PAIRS = B_HEAD_DIM // 4
ROPE_THETA = 10000.0
Q_BLOCK = 128
OFF_Z_A = 3 * A_WIDTH
OFF_BA_A = OFF_Z_A + A_WIDTH
OFF_Q_B = OFF_BA_A + 4 * A_HEADS
OFF_K_B = OFF_Q_B + B_WIDTH
OFF_V_B = OFF_K_B + B_KV_WIDTH
HYB_IN_WIDTH = OFF_V_B + B_KV_WIDTH
MIX_WIDTH = A_WIDTH + B_WIDTH
CONF_WIDTH = D_MODEL
CONF_KERNEL = 31
FFN_HIDDEN = ((8 * D_MODEL + 3 * 256 - 1) // (3 * 256)) * 256
N_EVEN = (DEPTH + 1) // 2
N_ODD = DEPTH // 2


F32 = jnp.float32

def rms_norm(x, gain):
    xf = x.astype(F32)
    y = xf * lax.rsqrt(jnp.mean(jnp.square(xf), axis=-1, keepdims=True) + EPS)
    return (y * gain.astype(F32)).astype(x.dtype)

def layer_norm(x, gain, bias):
    xf = x.astype(F32)
    mu = jnp.mean(xf, axis=-1, keepdims=True)
    var = jnp.mean(jnp.square(xf - mu), axis=-1, keepdims=True)
    return ((xf - mu) * lax.rsqrt(var + EPS) * gain.astype(F32) + bias.astype(F32)).astype(x.dtype)

def l2_normalize(x):
    return x * lax.rsqrt(jnp.sum(jnp.square(x), axis=-1, keepdims=True) + EPS)

def depthwise_conv_centred(x, w):
    pad = w.shape[0] // 2
    return lax.conv_general_dilated(
        x, w[:, None, :].astype(x.dtype), window_strides=(1,), padding=[(pad, pad)],
        dimension_numbers=("NWC", "WIO", "NWC"), feature_group_count=x.shape[-1])

def ada_terms(cond, w_mod, b_mod):
    m = jax.nn.silu(cond) @ w_mod + b_mod
    return jnp.split(m, 6, axis=-1)

def modulate(h, shift, scale):
    return h * (1.0 + scale) + shift

def axial_rope_tables(n_tokens):
    rows = n_tokens // GRID_W
    row = jnp.broadcast_to(jnp.arange(rows, dtype=F32)[:, None], (rows, GRID_W)).reshape(n_tokens)
    col = jnp.broadcast_to(jnp.arange(GRID_W, dtype=F32)[None, :], (rows, GRID_W)).reshape(n_tokens)
    inv_freq = ROPE_THETA ** (-jnp.arange(ROPE_AXIS_PAIRS, dtype=F32) / ROPE_AXIS_PAIRS)
    ang_r = row[:, None] * inv_freq
    ang_c = col[:, None] * inv_freq
    ang = jnp.concatenate([ang_r, ang_r, ang_c, ang_c], axis=-1)
    return jnp.cos(ang), jnp.sin(ang)

def apply_axial_rope(x, cos, sin):
    xf = x.astype(F32)
    xr = xf.reshape(*x.shape[:-1], 2, 2, ROPE_AXIS_PAIRS)
    rot = jnp.stack([-xr[..., 1, :], xr[..., 0, :]], axis=-2).reshape(x.shape)
    return (xf * cos[None, :, None, :] + rot * sin[None, :, None, :]).astype(x.dtype)

def gated_delta_chunked(q, k, v, g, beta, s0, need_out):
    bsz, n_tok, n_h, _ = q.shape
    dv = v.shape[-1]
    n_ch = n_tok // DELTA_CHUNK

    def chunks(t):
        return t.reshape(bsz, n_ch, DELTA_CHUNK, n_h, -1).transpose(1, 0, 3, 2, 4)

    qc, kc, vc = chunks(q), chunks(k), chunks(v)
    gcum = jnp.cumsum(chunks(g[..., None])[..., 0], axis=-1)
    bc = chunks(beta[..., None])
    idx = jnp.arange(DELTA_CHUNK)
    incl = idx[:, None] >= idx[None, :]
    strict = idx[:, None] > idx[None, :]
    decay = jnp.exp(jnp.where(incl, gcum[..., :, None] - gcum[..., None, :], -jnp.inf))
    kb = kc * bc
    lower = jnp.where(strict, jnp.einsum("nbhcd,nbhsd->nbhcs", kb, kc) * decay, 0.0)
    eye = jnp.eye(DELTA_CHUNK, dtype=F32)
    rhs = jnp.concatenate([vc * bc, kb * jnp.exp(gcum)[..., None]], axis=-1)
    sol = lax.linalg.triangular_solve(lower + eye, rhs, left_side=True, lower=True, unit_diagonal=True)
    u, w = sol[..., :dv], sol[..., dv:]
    g_last = gcum[..., -1]
    k_tail = kc * jnp.exp(g_last[..., None] - gcum)[..., None]
    xs = (u, w, k_tail, g_last)
    if need_out:
        intra = jnp.einsum("nbhcd,nbhsd->nbhcs", qc, kc) * decay
        q_dec = qc * jnp.exp(gcum)[..., None]
        xs = xs + (q_dec, intra)

    def step(state, xs_i):
        u_i, w_i, kt_i, gl_i = xs_i[:4]
        v_new = u_i - jnp.einsum("bhcd,bhde->bhce", w_i, state)
        new_state = state * jnp.exp(gl_i)[..., None, None] + jnp.einsum("bhcd,bhce->bhde", kt_i, v_new)
        if need_out:
            qd_i, a_i = xs_i[4:]
            o_i = jnp.einsum("bhcd,bhde->bhce", qd_i, state) + jnp.einsum("bhcs,bhse->bhce", a_i, v_new)
            return new_state, o_i
        return new_state, None

    s_fin, o = lax.scan(step, s0, xs)
    if need_out:
        o = o.transpose(1, 0, 3, 2, 4).reshape(bsz, n_tok, n_h, dv)
    return o, s_fin

def bidirectional_delta(q, k, v, g, beta, s0_fwd, s0_bwd, need_out):
    o_f, s_f = gated_delta_chunked(q, k, v, g[:, :, 0], beta[:, :, 0], s0_fwd, need_out)
    rev = lambda t: jnp.flip(t, axis=1)
    o_b, s_b = gated_delta_chunked(rev(q), rev(k), rev(v), rev(g[:, :, 1]), rev(beta[:, :, 1]), s0_bwd, need_out)
    o = o_f + rev(o_b) if need_out else None
    return o, s_f, s_b

def split_hybrid_projection(p, conv_w, a_log, dt_bias, q_norm, k_norm):
    bsz, n_tok, _ = p.shape
    qkv = jax.nn.silu(depthwise_conv_centred(p[..., :OFF_Z_A], conv_w))
    qkv = qkv.astype(F32).reshape(bsz, n_tok, 3, A_HEADS, A_HEAD_DIM)
    qa = l2_normalize(qkv[:, :, 0]) * (A_HEAD_DIM ** -0.5)
    ka = l2_normalize(qkv[:, :, 1])
    va = qkv[:, :, 2]
    za = p[..., OFF_Z_A:OFF_BA_A].reshape(bsz, n_tok, A_HEADS, A_HEAD_DIM)
    ba = p[..., OFF_BA_A:OFF_Q_B].astype(F32).reshape(bsz, n_tok, 2, 2, A_HEADS)
    beta = jax.nn.sigmoid(ba[:, :, 0])
    g = -jnp.exp(a_log.astype(F32)) * jax.nn.softplus(ba[:, :, 1] + dt_bias.astype(F32))
    qb = rms_norm(p[..., OFF_Q_B:OFF_K_B].reshape(bsz, n_tok, B_Q_HEADS, B_HEAD_DIM), q_norm)
    kb = rms_norm(p[..., OFF_K_B:OFF_V_B].reshape(bsz, n_tok, B_KV_HEADS, B_HEAD_DIM), k_norm)
    vb = p[..., OFF_V_B:].reshape(bsz, n_tok, B_KV_HEADS, B_HEAD_DIM)
    return qa, ka, va, za, g, beta, qb, kb, vb

def attend(q, k, v):
    s = jnp.einsum("bqkgd,bskd->bkgqs", q, k, preferred_element_type=F32) * (B_HEAD_DIM ** -0.5)
    p = jax.nn.softmax(s, axis=-1).astype(v.dtype)
    return jnp.einsum("bkgqs,bskd->bqkgd", p, v)

def latent_attention_blocks(q, k, v):
    bsz, n_tok = q.shape[:2]
    nb = n_tok // Q_BLOCK
    qb = q.reshape(bsz, nb, Q_BLOCK, *q.shape[2:]).swapaxes(0, 1)
    o = lax.map(lambda blk: attend(blk, k, v), qb)
    return o.swapaxes(0, 1).reshape(bsz, n_tok, B_WIDTH)

def hybrid_mixer(a_lat, a_ctx, w_in, conv_w, a_log, dt_bias, out_norm, q_norm, k_norm, w_out, cos, sin, ctx_out):
    bsz, n_tok, _ = a_lat.shape
    n_ctx = a_ctx.shape[1]
    qa_l, ka_l, va_l, za_l, g_l, be_l, qb_l, kb_l, vb_l = split_hybrid_projection(
        a_lat @ w_in, conv_w, a_log, dt_bias, q_norm, k_norm)
    qa_c, ka_c, va_c, za_c, g_c, be_c, qb_c, kb_c, vb_c = split_hybrid_projection(
        a_ctx @ w_in, conv_w, a_log, dt_bias, q_norm, k_norm)

    zeros = jnp.zeros((bsz, A_HEADS, A_HEAD_DIM, A_HEAD_DIM), F32)
    o_ctx_a, s_fwd, s_bwd = bidirectional_delta(qa_c, ka_c, va_c, g_c, be_c, zeros, zeros, ctx_out)
    o_lat_a, _, _ = bidirectional_delta(qa_l, ka_l, va_l, g_l, be_l, s_fwd, s_bwd, True)

    def delta_readout(o, z, n):
        y = rms_norm(o, out_norm) * jax.nn.silu(z.astype(F32))
        return y.reshape(bsz, n, A_WIDTH).astype(a_lat.dtype)

    qb_l = apply_axial_rope(qb_l, cos, sin)
    kb_l = apply_axial_rope(kb_l, cos, sin)
    k_all = jnp.concatenate([kb_c, kb_l], axis=1)
    v_all = jnp.concatenate([vb_c, vb_l], axis=1)
    group = lambda t: t.reshape(*t.shape[:2], B_KV_HEADS, B_GROUP, B_HEAD_DIM)
    o_lat_b = latent_attention_blocks(group(qb_l), k_all, v_all)

    y_lat = jnp.concatenate([delta_readout(o_lat_a, za_l, n_tok), o_lat_b.astype(a_lat.dtype)], axis=-1) @ w_out
    y_ctx = None
    if ctx_out:
        o_ctx_b = attend(group(qb_c), kb_c, vb_c).reshape(bsz, n_ctx, B_WIDTH)
        y_ctx = jnp.concatenate([delta_readout(o_ctx_a, za_c, n_ctx), o_ctx_b.astype(a_ctx.dtype)], axis=-1) @ w_out
    return y_lat, y_ctx

def conformer_conv(h, w_in, b_in, dw_w, dw_b, ln_g, ln_b, w_out, b_out):
    val, gate = jnp.split(h @ w_in + b_in, 2, axis=-1)
    u = val * jax.nn.sigmoid(gate)
    u = depthwise_conv_centred(u, dw_w) + dw_b
    u = jax.nn.silu(layer_norm(u, ln_g, ln_b))
    return u @ w_out + b_out

def swiglu_ffn(h, w_in, w_out):
    gate, up = jnp.split(h @ w_in, 2, axis=-1)
    return (jax.nn.silu(gate) * up) @ w_out

def first_inputs(seed: int = 0) -> dict:
    key = jax.random.key(seed)
    ks = iter(jax.random.split(key, 40))
    D = D_MODEL

    def nrm(shape, scale):
        return jax.random.normal(next(ks), shape, F32) * scale

    def gain(shape):
        return 1.0 + nrm(shape, 0.05)

    a_log = jnp.log(jax.random.uniform(next(ks), (N_EVEN, 2, A_HEADS), F32, 1.0, 16.0))
    dt = jnp.exp(jax.random.uniform(next(ks), (N_EVEN, 2, A_HEADS), F32, math.log(1e-3), math.log(1e-1)))
    dt_bias = dt + jnp.log(-jnp.expm1(-dt))
    return {
        "x": nrm((BATCH, SEQ, D), 1.0),
        "c": nrm((BATCH, D), 1.0),
        "ctx": nrm((BATCH, CTX_LEN, D), 1.0),
        "c_ctx": nrm((D,), 1.0),
        "w_mod": nrm((DEPTH, D, 6 * D), 0.5 * D ** -0.5),
        "b_mod": nrm((DEPTH, 6 * D), 0.02),
        "g_mix_pre": gain((DEPTH, D)),
        "g_mix_post": gain((DEPTH, D)),
        "g_ffn_pre": gain((DEPTH, D)),
        "g_ffn_post": gain((DEPTH, D)),
        "w_ffn_in": nrm((DEPTH, D, 2 * FFN_HIDDEN), D ** -0.5),
        "w_ffn_out": nrm((DEPTH, FFN_HIDDEN, D), FFN_HIDDEN ** -0.5),
        "hyb_w_in": nrm((N_EVEN, D, HYB_IN_WIDTH), D ** -0.5),
        "hyb_conv_w": nrm((N_EVEN, SHORT_CONV_W, 3 * A_WIDTH), SHORT_CONV_W ** -0.5),
        "hyb_a_log": a_log,
        "hyb_dt_bias": dt_bias,
        "hyb_out_norm": gain((N_EVEN, A_HEAD_DIM)),
        "hyb_q_norm": gain((N_EVEN, B_HEAD_DIM)),
        "hyb_k_norm": gain((N_EVEN, B_HEAD_DIM)),
        "hyb_w_out": nrm((N_EVEN, MIX_WIDTH, D), MIX_WIDTH ** -0.5),
        "conf_w_in": nrm((N_ODD, D, 2 * CONF_WIDTH), D ** -0.5),
        "conf_b_in": nrm((N_ODD, 2 * CONF_WIDTH), 0.02),
        "conf_dw_w": nrm((N_ODD, CONF_KERNEL, CONF_WIDTH), CONF_KERNEL ** -0.5),
        "conf_dw_b": nrm((N_ODD, CONF_WIDTH), 0.02),
        "conf_ln_g": gain((N_ODD, CONF_WIDTH)),
        "conf_ln_b": nrm((N_ODD, CONF_WIDTH), 0.02),
        "conf_w_out": nrm((N_ODD, CONF_WIDTH, D), CONF_WIDTH ** -0.5),
        "conf_b_out": nrm((N_ODD, D), 0.02),
    }

def first_block(x, c, ctx, c_ctx, w_mod, b_mod, g_mix_pre, g_mix_post, g_ffn_pre, g_ffn_post, w_ffn_in, w_ffn_out,
              hyb_w_in, hyb_conv_w, hyb_a_log, hyb_dt_bias, hyb_out_norm, hyb_q_norm, hyb_k_norm, hyb_w_out,
              conf_w_in, conf_b_in, conf_dw_w, conf_dw_b, conf_ln_g, conf_ln_b, conf_w_out, conf_b_out):
    cos, sin = axial_rope_tables(x.shape[1])
    h, hc = x, ctx
    for layer in range(DEPTH):
        is_hybrid = layer % 2 == 0
        idx = layer // 2
        advance_ctx = any(j % 2 == 0 for j in range(layer + 1, DEPTH))
        sh1, sc1, gt1, sh2, sc2, gt2 = ada_terms(c[:, None, :], w_mod[layer], b_mod[layer])
        a = modulate(rms_norm(h, g_mix_pre[layer]), sh1, sc1)
        if is_hybrid or advance_ctx:
            csh1, csc1, cgt1, csh2, csc2, cgt2 = ada_terms(c_ctx, w_mod[layer], b_mod[layer])
            ac = modulate(rms_norm(hc, g_mix_pre[layer]), csh1, csc1)
        if is_hybrid:
            y, yc = hybrid_mixer(a, ac, hyb_w_in[idx], hyb_conv_w[idx], hyb_a_log[idx], hyb_dt_bias[idx],
                                 hyb_out_norm[idx], hyb_q_norm[idx], hyb_k_norm[idx], hyb_w_out[idx],
                                 cos, sin, advance_ctx)
        else:
            conf = (conf_w_in[idx], conf_b_in[idx], conf_dw_w[idx], conf_dw_b[idx],
                    conf_ln_g[idx], conf_ln_b[idx], conf_w_out[idx], conf_b_out[idx])
            y = conformer_conv(a, *conf)
            yc = conformer_conv(ac, *conf) if advance_ctx else None
        h = h + gt1 * rms_norm(y, g_mix_post[layer])
        f = swiglu_ffn(modulate(rms_norm(h, g_ffn_pre[layer]), sh2, sc2), w_ffn_in[layer], w_ffn_out[layer])
        h = h + gt2 * rms_norm(f, g_ffn_post[layer])
        if advance_ctx:
            hc = hc + cgt1 * rms_norm(yc, g_mix_post[layer])
            fc = swiglu_ffn(modulate(rms_norm(hc, g_ffn_pre[layer]), csh2, csc2), w_ffn_in[layer], w_ffn_out[layer])
            hc = hc + cgt2 * rms_norm(fc, g_ffn_post[layer])
    return h


DEPTH_2 = 4

N_MIXERS = 3
ALPHA = (2.0 * DEPTH_2) ** 0.25
BETA = (8.0 * DEPTH_2) ** -0.25
LN_EPS = 1e-5
HEAD_NORM_EPS = 1e-6

HGRN_EXPAND = 128
HGRN_HEADS = D_MODEL // HGRN_EXPAND
HGRN_DK = HGRN_EXPAND
HGRN_DV = D_MODEL // HGRN_HEADS
HGRN_CHUNK = 64

MLSTM_HEADS = 8
MLSTM_DV = D_MODEL // MLSTM_HEADS
MLSTM_DQK = MLSTM_DV // 2
MLSTM_CONV = 4
MLSTM_CHUNK = 64
MLSTM_QK_W = MLSTM_HEADS * MLSTM_DQK
MLSTM_IN_W = 2 * MLSTM_QK_W + 2 * D_MODEL + 2 * MLSTM_HEADS

S5_GROUP_CH = 16
S5_GROUPS = D_MODEL // S5_GROUP_CH
S5_STATE = 64
S5_CHUNK = 1024
S5_DT_MIN = 1e-3
S5_DT_MAX = 1e-1

FFN_HIDDEN_2 = -(-8 * D_MODEL // (3 * 256)) * 256

N_HGRN = (DEPTH_2 + 2) // 3
N_MLSTM = (DEPTH_2 + 1) // 3
N_S5 = DEPTH_2 // 3


def _layernorm(x, g, b):
    xf = x.astype(jnp.float32)
    mu = jnp.mean(xf, axis=-1, keepdims=True)
    xc = xf - mu
    var = jnp.mean(xc * xc, axis=-1, keepdims=True)
    return (xc * lax.rsqrt(var + LN_EPS) * g + b).astype(x.dtype)

def _head_rmsnorm(h, w):
    return h * lax.rsqrt(jnp.mean(h * h, axis=-1, keepdims=True) + HEAD_NORM_EPS) * w

def _to_chunks(t, n_heads, chunk):
    bsz, seq, width = t.shape
    return t.reshape(bsz, seq // chunk, chunk, n_heads, width // n_heads).transpose(1, 0, 3, 2, 4)

def _from_chunks(t):
    nc, bsz, h, c, d = t.shape
    return t.transpose(1, 0, 3, 2, 4).reshape(bsz, nc * c, h, d)

def _causal_conv(u, w):
    k_w = w.shape[0]
    seq = u.shape[1]
    up = jnp.pad(u, ((0, 0), (k_w - 1, 0), (0, 0)))
    out = up[:, 0:seq] * w[0]
    for j in range(1, k_w):
        out = out + up[:, j:j + seq] * w[j]
    return out

def _hgrn_lower_bounds(lb_logits):
    p = jax.nn.softmax(lb_logits.astype(jnp.float32), axis=0)
    c = jnp.cumsum(p, axis=0)
    return c - c[0:1]

def _hgrn2_mixer(x, w_in, norm_w, w_out, lb):
    bsz, seq, _ = x.shape
    q, f, v, g = jnp.split(x @ w_in, 4, axis=-1)
    f = f.astype(jnp.float32)
    log_f = jnp.logaddexp(jnp.log(lb), jnp.log1p(-lb) + jax.nn.log_sigmoid(f))
    k = (1.0 - lb) * jax.nn.sigmoid(-f)
    q = jax.nn.silu(q.astype(jnp.float32))
    qc = _to_chunks(q, HGRN_HEADS, HGRN_CHUNK)
    kc = _to_chunks(k, HGRN_HEADS, HGRN_CHUNK)
    vc = _to_chunks(v.astype(jnp.float32), HGRN_HEADS, HGRN_CHUNK)
    lfc = _to_chunks(log_f, HGRN_HEADS, HGRN_CHUNK)
    mask = jnp.tril(jnp.ones((HGRN_CHUNK, HGRN_CHUNK), dtype=bool))

    def step(s_prev, inp):
        qb, kb, vb, lfb = inp
        b = jnp.cumsum(lfb, axis=2)
        diff = b[:, :, :, None, :] - b[:, :, None, :, :]
        decay = jnp.exp(jnp.where(mask[:, :, None], diff, -jnp.inf))
        att = jnp.einsum('bhtd,bhsd,bhtsd->bhts', qb, kb, decay)
        o = jnp.einsum('bhts,bhse->bhte', att, vb) + jnp.einsum('bhtd,bhde->bhte', qb * jnp.exp(b), s_prev)
        b_last = b[:, :, -1]
        k_dec = kb * jnp.exp(b_last[:, :, None, :] - b)
        s_new = jnp.exp(b_last)[..., None] * s_prev + jnp.einsum('bhsd,bhse->bhde', k_dec, vb)
        return s_new, o

    s0 = jnp.zeros((bsz, HGRN_HEADS, HGRN_DK, HGRN_DV), jnp.float32)
    _, oc = lax.scan(step, s0, (qc, kc, vc, lfc))
    o = _head_rmsnorm(_from_chunks(oc), norm_w.astype(jnp.float32))
    o = o.reshape(bsz, seq, D_MODEL) * jax.nn.silu(g.astype(jnp.float32))
    return o.astype(x.dtype) @ w_out

def _mlstm_mixer(x, w_in, conv_w, gate_b, norm_w, w_out):
    bsz, seq, _ = x.shape
    proj = x @ w_in
    qk = proj[..., :2 * MLSTM_QK_W]
    v = proj[..., 2 * MLSTM_QK_W:2 * MLSTM_QK_W + D_MODEL]
    o_pre = proj[..., 2 * MLSTM_QK_W + D_MODEL:2 * MLSTM_QK_W + 2 * D_MODEL]
    gates = proj[..., 2 * MLSTM_QK_W + 2 * D_MODEL:].astype(jnp.float32) + gate_b.astype(jnp.float32)
    qk = jax.nn.silu(_causal_conv(qk, conv_w).astype(jnp.float32))
    q = qk[..., :MLSTM_QK_W]
    k = qk[..., MLSTM_QK_W:] * (MLSTM_DQK ** -0.5)
    log_i = gates[..., :MLSTM_HEADS]
    log_f = jax.nn.log_sigmoid(gates[..., MLSTM_HEADS:])
    qc = _to_chunks(q, MLSTM_HEADS, MLSTM_CHUNK)
    kc = _to_chunks(k, MLSTM_HEADS, MLSTM_CHUNK)
    vc = _to_chunks(v.astype(jnp.float32), MLSTM_HEADS, MLSTM_CHUNK)
    lic = _to_chunks(log_i, MLSTM_HEADS, MLSTM_CHUNK)[..., 0]
    lfc = _to_chunks(log_f, MLSTM_HEADS, MLSTM_CHUNK)[..., 0]
    mask = jnp.tril(jnp.ones((MLSTM_CHUNK, MLSTM_CHUNK), dtype=bool))

    def step(carry, inp):
        c_prev, n_prev, m_prev = carry
        qb, kb, vb, lib, lfb = inp
        b = jnp.cumsum(lfb, axis=-1)
        log_d = jnp.where(mask, b[..., :, None] - b[..., None, :] + lib[..., None, :], -jnp.inf)
        log_inter = b + m_prev[..., None]
        m_t = jnp.maximum(jnp.max(log_d, axis=-1), log_inter)
        d_mat = jnp.exp(log_d - m_t[..., None])
        w_inter = jnp.exp(log_inter - m_t)
        s = jnp.einsum('bhtd,bhsd->bhts', qb, kb) * d_mat
        num = jnp.einsum('bhts,bhse->bhte', s, vb) + w_inter[..., None] * jnp.einsum('bhtd,bhde->bhte', qb, c_prev)
        den = jnp.sum(s, axis=-1) + w_inter * jnp.einsum('bhtd,bhd->bht', qb, n_prev)
        h = num / jnp.maximum(jnp.abs(den), jnp.exp(-m_t))[..., None]
        b_last = b[..., -1]
        log_w = b_last[..., None] - b + lib
        m_new = jnp.maximum(b_last + m_prev, jnp.max(log_w, axis=-1))
        w_s = jnp.exp(log_w - m_new[..., None])
        w_prev = jnp.exp(b_last + m_prev - m_new)
        c_new = w_prev[..., None, None] * c_prev + jnp.einsum('bhs,bhsd,bhse->bhde', w_s, kb, vb)
        n_new = w_prev[..., None] * n_prev + jnp.einsum('bhs,bhsd->bhd', w_s, kb)
        return (c_new, n_new, m_new), h

    init = (jnp.zeros((bsz, MLSTM_HEADS, MLSTM_DQK, MLSTM_DV), jnp.float32),
            jnp.zeros((bsz, MLSTM_HEADS, MLSTM_DQK), jnp.float32),
            jnp.zeros((bsz, MLSTM_HEADS), jnp.float32))
    _, hc = lax.scan(step, init, (qc, kc, vc, lic, lfc))
    h = _head_rmsnorm(_from_chunks(hc), norm_w.astype(jnp.float32).reshape(MLSTM_HEADS, MLSTM_DV))
    h = h.reshape(bsz, seq, D_MODEL) * jax.nn.sigmoid(o_pre.astype(jnp.float32))
    return h.astype(x.dtype) @ w_out

def _cmul(ar, ai, br, bi):
    return ar * br - ai * bi, ar * bi + ai * br

def _s5_combine(e1, e2):
    a1r, a1i, b1r, b1i = e1
    a2r, a2i, b2r, b2i = e2
    ar, ai = _cmul(a2r, a2i, a1r, a1i)
    tr, ti = _cmul(a2r, a2i, b1r, b1i)
    return ar, ai, tr + b2r, ti + b2i

def _s5_mixer(x, w_in, a_re, a_im, log_dt, b_re, b_im, c_re, c_im, d_skip, w_out):
    bsz, seq, _ = x.shape
    f32 = jnp.float32
    u = (x @ w_in).astype(f32)
    a_re = a_re.astype(f32)
    a_im = a_im.astype(f32)
    b_re = b_re.astype(f32)
    b_im = b_im.astype(f32)
    c_re = c_re.astype(f32)
    c_im = c_im.astype(f32)
    dt = jnp.exp(log_dt.astype(f32))[:, None]
    mag = jnp.exp(a_re * dt)
    abar_re = mag * jnp.cos(a_im * dt)
    abar_im = mag * jnp.sin(a_im * dt)
    nr = abar_re - 1.0
    ni = abar_im
    den = a_re * a_re + a_im * a_im
    coef_re = (nr * a_re + ni * a_im) / den
    coef_im = (ni * a_re - nr * a_im) / den
    bbar_re = coef_re[..., None] * b_re - coef_im[..., None] * b_im
    bbar_im = coef_re[..., None] * b_im + coef_im[..., None] * b_re
    chunk = math.gcd(seq, S5_CHUNK)
    nc = seq // chunk
    ug = u.reshape(bsz, nc, chunk, S5_GROUPS, S5_GROUP_CH).transpose(1, 0, 2, 3, 4)
    a_r = jnp.broadcast_to(abar_re, (bsz, chunk, S5_GROUPS, S5_STATE))
    a_i = jnp.broadcast_to(abar_im, (bsz, chunk, S5_GROUPS, S5_STATE))

    def step(carry, ub):
        hr, hi = carry
        bu_re = jnp.einsum('blgc,gpc->blgp', ub, bbar_re)
        bu_im = jnp.einsum('blgc,gpc->blgp', ub, bbar_im)
        pr, pi, sr, si = lax.associative_scan(_s5_combine, (a_r, a_i, bu_re, bu_im), axis=1)
        cr, ci = _cmul(pr, pi, hr[:, None], hi[:, None])
        sr = sr + cr
        si = si + ci
        y = jnp.einsum('blgp,gcp->blgc', sr, c_re) - jnp.einsum('blgp,gcp->blgc', si, c_im)
        return (sr[:, -1], si[:, -1]), y

    h0 = (jnp.zeros((bsz, S5_GROUPS, S5_STATE), f32), jnp.zeros((bsz, S5_GROUPS, S5_STATE), f32))
    _, yc = lax.scan(step, h0, ug)
    y = yc.transpose(1, 0, 2, 3, 4).reshape(bsz, seq, D_MODEL)
    y = y + d_skip.astype(f32) * u
    y = jax.nn.gelu(y).astype(x.dtype)
    za, zb = jnp.split(y @ w_out, 2, axis=-1)
    return za * jax.nn.sigmoid(zb)

def _swiglu(x, w_gate_up, w_down):
    gate, up = jnp.split(x @ w_gate_up, 2, axis=-1)
    return (jax.nn.silu(gate) * up) @ w_down

def second_inputs(seed: int = 0) -> dict:
    key = jax.random.key(seed)
    ks = jax.random.split(key, 24)
    D = D_MODEL
    nrm = jax.random.normal
    x = nrm(ks[0], (BATCH, SEQ, D), jnp.float32)
    hgrn_w_in = nrm(ks[1], (N_HGRN, D, 4 * D), jnp.float32) * D ** -0.5
    hgrn_norm_w = 1.0 + 0.02 * nrm(ks[2], (N_HGRN, HGRN_DV), jnp.float32)
    hgrn_w_out = nrm(ks[3], (N_HGRN, D, D), jnp.float32) * (D ** -0.5 * BETA)
    hgrn_lb_logits = 0.5 * nrm(ks[4], (DEPTH_2, HGRN_HEADS * HGRN_DK), jnp.float32)
    mlstm_w_in = nrm(ks[5], (N_MLSTM, D, MLSTM_IN_W), jnp.float32) * D ** -0.5
    mlstm_conv_w = nrm(ks[6], (N_MLSTM, MLSTM_CONV, 2 * MLSTM_QK_W), jnp.float32) * MLSTM_CONV ** -0.5
    i_bias = 0.1 * nrm(ks[7], (N_MLSTM, MLSTM_HEADS), jnp.float32)
    f_bias = jnp.linspace(3.0, 6.0, MLSTM_HEADS, dtype=jnp.float32)[None] + 0.1 * nrm(ks[8], (N_MLSTM, MLSTM_HEADS), jnp.float32)
    mlstm_gate_b = jnp.concatenate([i_bias, f_bias], axis=-1)
    mlstm_norm_w = 1.0 + 0.02 * nrm(ks[9], (N_MLSTM, D), jnp.float32)
    mlstm_w_out = nrm(ks[10], (N_MLSTM, D, D), jnp.float32) * (D ** -0.5 * BETA)
    s5_w_in = nrm(ks[11], (N_S5, D, D), jnp.float32) * D ** -0.5
    s5_a_re = -0.5 + 0.01 * nrm(ks[12], (N_S5, S5_GROUPS, S5_STATE), jnp.float32)
    s5_a_im = (jnp.pi * jnp.arange(S5_STATE, dtype=jnp.float32))[None, None] + 0.01 * nrm(ks[13], (N_S5, S5_GROUPS, S5_STATE), jnp.float32)
    s5_log_dt = jax.random.uniform(ks[14], (N_S5, S5_GROUPS), jnp.float32, math.log(S5_DT_MIN), math.log(S5_DT_MAX))
    s5_b_re = nrm(ks[15], (N_S5, S5_GROUPS, S5_STATE, S5_GROUP_CH), jnp.float32) * (2 * S5_GROUP_CH) ** -0.5
    s5_b_im = nrm(ks[16], (N_S5, S5_GROUPS, S5_STATE, S5_GROUP_CH), jnp.float32) * (2 * S5_GROUP_CH) ** -0.5
    s5_c_re = nrm(ks[17], (N_S5, S5_GROUPS, S5_GROUP_CH, S5_STATE), jnp.float32) * S5_STATE ** -0.5
    s5_c_im = nrm(ks[18], (N_S5, S5_GROUPS, S5_GROUP_CH, S5_STATE), jnp.float32) * S5_STATE ** -0.5
    s5_d = nrm(ks[19], (N_S5, D), jnp.float32)
    s5_w_out = nrm(ks[20], (N_S5, D, 2 * D), jnp.float32) * (D ** -0.5 * BETA)
    ffn_w_gate_up = nrm(ks[21], (DEPTH_2, D, 2 * FFN_HIDDEN_2), jnp.float32) * D ** -0.5
    ffn_w_down = nrm(ks[22], (DEPTH_2, FFN_HIDDEN_2, D), jnp.float32) * (FFN_HIDDEN_2 ** -0.5 * BETA)
    kg, kb = jax.random.split(ks[23])
    ln_g = 1.0 + 0.02 * nrm(kg, (DEPTH_2, 2, D), jnp.float32)
    ln_b = 0.02 * nrm(kb, (DEPTH_2, 2, D), jnp.float32)
    return {"x": x, "hgrn_w_in": hgrn_w_in, "hgrn_norm_w": hgrn_norm_w, "hgrn_w_out": hgrn_w_out,
            "hgrn_lb_logits": hgrn_lb_logits, "mlstm_w_in": mlstm_w_in, "mlstm_conv_w": mlstm_conv_w,
            "mlstm_gate_b": mlstm_gate_b, "mlstm_norm_w": mlstm_norm_w, "mlstm_w_out": mlstm_w_out,
            "s5_w_in": s5_w_in, "s5_a_re": s5_a_re, "s5_a_im": s5_a_im, "s5_log_dt": s5_log_dt,
            "s5_b_re": s5_b_re, "s5_b_im": s5_b_im, "s5_c_re": s5_c_re, "s5_c_im": s5_c_im,
            "s5_d": s5_d, "s5_w_out": s5_w_out, "ffn_w_gate_up": ffn_w_gate_up, "ffn_w_down": ffn_w_down,
            "ln_g": ln_g, "ln_b": ln_b}

def second_block(x, hgrn_w_in, hgrn_norm_w, hgrn_w_out, hgrn_lb_logits, mlstm_w_in, mlstm_conv_w,
              mlstm_gate_b, mlstm_norm_w, mlstm_w_out, s5_w_in, s5_a_re, s5_a_im, s5_log_dt,
              s5_b_re, s5_b_im, s5_c_re, s5_c_im, s5_d, s5_w_out, ffn_w_gate_up, ffn_w_down,
              ln_g, ln_b):
    lb_all = _hgrn_lower_bounds(hgrn_lb_logits)
    for i in range(DEPTH_2):
        kind = i % N_MIXERS
        j = i // N_MIXERS
        if kind == 0:
            h = _hgrn2_mixer(x, hgrn_w_in[j], hgrn_norm_w[j], hgrn_w_out[j], lb_all[i])
        elif kind == 1:
            h = _mlstm_mixer(x, mlstm_w_in[j], mlstm_conv_w[j], mlstm_gate_b[j], mlstm_norm_w[j], mlstm_w_out[j])
        else:
            h = _s5_mixer(x, s5_w_in[j], s5_a_re[j], s5_a_im[j], s5_log_dt[j], s5_b_re[j], s5_b_im[j],
                          s5_c_re[j], s5_c_im[j], s5_d[j], s5_w_out[j])
        x = _layernorm(ALPHA * x + h, ln_g[i, 0], ln_b[i, 0])
        x = _layernorm(ALPHA * x + _swiglu(x, ffn_w_gate_up[i], ffn_w_down[i]), ln_g[i, 1], ln_b[i, 1])
    return x


def setup_inputs(seed=0):
    out = dict(first_inputs(seed))
    for name, value in second_inputs(seed + 1).items():
        if name != "x":
            out[name + "_2"] = value
    return out


def reference(
    x, c, ctx, c_ctx, w_mod, b_mod, g_mix_pre, g_mix_post, g_ffn_pre, g_ffn_post, w_ffn_in,
    w_ffn_out, hyb_w_in, hyb_conv_w, hyb_a_log, hyb_dt_bias, hyb_out_norm, hyb_q_norm,
    hyb_k_norm, hyb_w_out, conf_w_in, conf_b_in, conf_dw_w, conf_dw_b, conf_ln_g, conf_ln_b,
    conf_w_out, conf_b_out, hgrn_w_in_2, hgrn_norm_w_2, hgrn_w_out_2, hgrn_lb_logits_2,
    mlstm_w_in_2, mlstm_conv_w_2, mlstm_gate_b_2, mlstm_norm_w_2, mlstm_w_out_2, s5_w_in_2,
    s5_a_re_2, s5_a_im_2, s5_log_dt_2, s5_b_re_2, s5_b_im_2, s5_c_re_2, s5_c_im_2, s5_d_2,
    s5_w_out_2, ffn_w_gate_up_2, ffn_w_down_2, ln_g_2, ln_b_2,
):
    x = first_block(
        x, c, ctx, c_ctx, w_mod, b_mod, g_mix_pre, g_mix_post, g_ffn_pre, g_ffn_post, w_ffn_in,
        w_ffn_out, hyb_w_in, hyb_conv_w, hyb_a_log, hyb_dt_bias, hyb_out_norm, hyb_q_norm,
        hyb_k_norm, hyb_w_out, conf_w_in, conf_b_in, conf_dw_w, conf_dw_b, conf_ln_g, conf_ln_b,
        conf_w_out, conf_b_out,
    )
    return second_block(
        x, hgrn_w_in_2, hgrn_norm_w_2, hgrn_w_out_2, hgrn_lb_logits_2, mlstm_w_in_2,
        mlstm_conv_w_2, mlstm_gate_b_2, mlstm_norm_w_2, mlstm_w_out_2, s5_w_in_2, s5_a_re_2,
        s5_a_im_2, s5_log_dt_2, s5_b_re_2, s5_b_im_2, s5_c_re_2, s5_c_im_2, s5_d_2, s5_w_out_2,
        ffn_w_gate_up_2, ffn_w_down_2, ln_g_2, ln_b_2,
    )


_drawn_inputs = setup_inputs


def setup_inputs(seed=0):
    import zlib

    import numpy as np

    out = dict(_drawn_inputs(seed))
    spreads = {}
    factors = {'g_ffn_post': 2.836,
     'hyb_out_norm': 3.832,
     'hyb_q_norm': 8.0,
     'hyb_k_norm': 8.0,
     'conf_b_in': 8.0,
     'conf_dw_b': 5.493,
     'conf_ln_g': 3.162,
     'conf_ln_b': 8.0,
     'conf_b_out': 5.935,
     'hgrn_norm_w_2': 8.0,
     'hgrn_lb_logits_2': 6.299,
     'mlstm_norm_w_2': 8.0,
     's5_a_re_2': 64.0,
     's5_a_im_2': 63.272,
     's5_log_dt_2': 64.0,
     's5_b_re_2': 64.0,
     's5_b_im_2': 64.0,
     's5_c_re_2': 64.0,
     's5_c_im_2': 64.0}
    for name, (base, spread) in spreads.items():
        noise = np.random.default_rng([zlib.crc32(name.encode()), seed]).standard_normal(out[name].shape)
        drawn = base * np.exp(spread * noise) if base else spread * noise
        out[name] = __import__('jax').numpy.asarray(drawn.astype(out[name].dtype))
    for name, factor in factors.items():
        out[name] = (out[name] * factor).astype(out[name].dtype)
    return out
```

```python
from contextlib import ExitStack

import numpy as np

import concourse.bass as bass
from concourse import mybir

F32 = mybir.dt.float32
U32 = mybir.dt.uint32
ALU = mybir.AluOpType
ACT = mybir.ActivationFunctionType
AXX = mybir.AxisListType.X

P = 128
D = 1024
KC = D // P
T = 256
TT = T // P
FFN = 2816
FC = FFN // P
COND = 6 * D // P
SLAB = 2048
SLAB_TILES = SLAB // P
RING = 9
BANK = 512
BANKS = 8
A_HEADS = 4
B_PAIRS = 4
DIRS = 2
DH = DIRS * A_HEADS
CONV_A = 5
CONV_C = 31
PAD_C = CONV_C // 2
CONV_M = 4
HEADS = 8
GROUPS = 64
S5_CH = 16
S5_STATE = 64
S5_TILES = GROUPS * S5_STATE // P
EPS = 1e-6
LN_EPS = 1e-5
ALPHA = 8.0 ** 0.25
LEVELS = [1, 2, 4, 8, 16, 32, 64]
TWO_PI = 6.283185307179586
PI_1 = 6.28125
PI_2 = 0.0019350051879882812
PI_3 = 3.019916050561733e-07
ROUND = 12582912.0

VECTORS = [
    ("c", KC), ("c_ctx", KC), ("b_mod", 2 * COND),
    ("g_mix_pre", 2 * KC), ("g_mix_post", 2 * KC), ("g_ffn_pre", 2 * KC), ("g_ffn_post", 2 * KC),
    ("hyb_conv_w", CONV_A * 12), ("hyb_out_norm", 1), ("hyb_q_norm", 1), ("hyb_k_norm", 1),
    ("hyb_a_log", 1), ("hyb_dt_bias", 1), ("hyb_beta_w", KC * 8), ("hyb_g_w", KC * 8),
    ("conf_b_in", 2 * KC), ("conf_dw_w", CONV_C * KC), ("conf_dw_b", KC),
    ("conf_ln_g", KC), ("conf_ln_b", KC), ("conf_b_out", KC),
    ("hgrn_norm_w", 2), ("lb_logits", 4 * KC),
    ("mlstm_conv_w", CONV_M * KC), ("mlstm_gate_i", 1), ("mlstm_gate_f", 1), ("mlstm_norm_w", KC),
    ("mlstm_i_w", KC * 8), ("mlstm_f_w", KC * 8),
    ("s5_a_re", S5_TILES), ("s5_a_im", S5_TILES), ("s5_log_dt", S5_TILES), ("s5_d", KC),
    ("ln_g", 8 * KC), ("ln_b", 8 * KC),
]
CONSTANTS = [
    ("ident", P), ("mean", P), ("ones", P), ("ones64", P), ("rope_turn", P),
    ("upto", P), ("from_", P), ("lower_pairs", len(LEVELS) * P), ("upper_pairs", len(LEVELS) * P),
    ("cos", T), ("sin", T), ("head_rows", HEADS * P), ("one_row", T),
    ("time", T),
]


def columns_of(table):
    at, out = 0, {}
    for name, n in table:
        out[name] = (at, n)
        at += n
    return out, at


VEC_AT, VEC_N = columns_of(VECTORS)
CONST_AT, CONST_N = columns_of(CONSTANTS)


class Signal:

    def __init__(self, sem):
        self.sem, self.count = sem, 0

    def events(self, n):
        first = self.count + 1
        self.count += n
        return [(self.sem, first + i) for i in range(n)]

    def event(self):
        return self.events(1)[0]


class Chain:

    def __init__(self, eng, sem):
        self.eng, self.sem, self.count = eng, sem, 0

    def link(self, ins):
        self.count += 1
        ins.then_inc(self.sem, 1)
        self.eng.wait_ge(self.sem, self.count)


class Job:

    def __init__(self, ap, before, full, free):
        self.ap, self.before, self.full, self.free = ap, before, full, free


class Weights:

    def __init__(self, ring, loaded, used):
        self.ring, self.loaded, self.used = ring, loaded, used
        self.at, self.release = 0, False

    def next(self, pe):
        pe.wait_ge(self.loaded[self.at % RING], 16 * (self.at // RING + 1))
        self.release = self.at > 0
        slab = self.ring[:, self.at % RING, :]
        self.at += 1
        return slab

    def matmul(self, pe, *args, **kw):
        mm = pe.matmul(*args, **kw)
        if self.release:
            mm.then_inc(self.used, 1)
            self.release = False
        return mm


class Core:

    def __init__(self, nc, ctx, vec_dram, const_dram):
        self.nc = nc

        def sb(name, shape, dt=F32):
            return ctx.enter_context(nc.sbuf_tensor(name, shape, dt))

        def sem(name):
            return ctx.enter_context(nc.semaphore(name))

        self.ring = sb("weight_ring", [P, RING, SLAB])
        self.vec = sb("vectors", [P, VEC_N])
        self.const = sb("constants", [P, CONST_N])
        self.h = sb("residual", [P, KC, T])
        self.mod = sb("modulation", [P, COND, 2])
        self.coef = sb("modulation_gains", [P, 5, KC])
        self.silu_c = sb("silu_cond", [P, KC, 2])
        self.work_n = 25600
        self.work = sb("work", [P, self.work_n])
        self.cols = sb("columns", [P, 12, 32])
        self.psum = ctx.enter_context(nc.psum_tensor("psum", [P, BANKS, BANK], F32))
        self.loaded = [sem(f"slab_loaded{i}") for i in range(RING)]
        self.used = sem("slab_used")
        self.consts_loaded = sem("consts_loaded")
        self.act_chain = sem("act_chain")
        self.dve_chain = sem("dve_chain")
        self.pool_chain = sem("pool_chain")
        self.bank_full = [Signal(sem(f"bank{i}_full")) for i in range(BANKS)]
        self.bank_free = [Signal(sem(f"bank{i}_free")) for i in range(BANKS)]
        self.last_free = [None] * BANKS
        self.jobs = 0
        self.counters = {}
        self.sem = sem
        self.weights = Weights(self.ring, self.loaded, self.used)
        self.vec_dram, self.const_dram = vec_dram, const_dram
        self.root_free = None
        self.h_ready = None

    def counter(self, name):
        if name not in self.counters:
            self.counters[name] = Signal(self.sem(name))
        return self.counters[name]

    def job(self, free=None):
        b = self.jobs % BANKS
        self.jobs += 1
        job = Job(self.psum[:, b, :], self.last_free[b], self.bank_full[b].event(),
                  free or self.bank_free[b].event())
        self.last_free[b] = job.free
        return job

    def take(self, n):
        return [self.job() for _ in range(n)]

    def v(self, name, i=0, n=1, rows=P):
        at = VEC_AT[name][0] + i
        return self.vec[0:rows, at:at + n]

    def c(self, name, i=0, n=None, rows=P):
        at, size = CONST_AT[name]
        n = size if n is None else n
        return self.const[0:rows, at + i:at + i + n]

    def area(self, at, *shape):
        n = 1
        for s in shape:
            n *= s
        assert at + n <= self.work_n, (at, shape)
        flat = self.work[:, at:at + n]
        if len(shape) == 1:
            return flat
        if len(shape) == 2:
            return flat.rearrange("p (a b) -> p a b", b=shape[1])
        return flat.rearrange("p (a b c) -> p a b c", b=shape[1], c=shape[2])


def over_chunks(ap, n):
    return ap.unsqueeze(1).broadcast_to([ap.shape[0], n, ap.shape[1]])


def begin(eng, job):
    if job.before:
        eng.wait_ge(*job.before)


class Stage:
    def __init__(self, core):
        self.k = core
        self.setup()

    def setup(self):
        pass

    def tensor(self, pe):
        pass

    def scalar(self, act):
        pass

    def vector(self, dve):
        pass

    def gpsimd(self, pool):
        pass


AT_A = 0
AT_Y = AT_A + KC * T
AT_SQ = AT_Y + KC * T
AT_RS = AT_SQ + KC * T
AT_HID = AT_RS + 2 * T
AT_TMP = AT_HID + FC * T


class Start(Stage):

    def setup(self):
        self.k.h_ready = [(self.k.consts_loaded, 64)] * KC
        self.silu_ready = self.k.counter("silu_ready").events(2)
        self.k.silu_ready = self.silu_ready[1]

    def tensor(self, pe):
        pe.wait_ge(self.k.consts_loaded, 64)

    def scalar(self, act):
        act.wait_ge(self.k.consts_loaded, 64)
        for i, name in enumerate(("c", "c_ctx")):
            act.activation(self.k.silu_c[:, :, i], self.k.v(name, 0, KC), ACT.Silu)\
               .then_inc(self.silu_ready[i][0], 1)

    def vector(self, dve):
        dve.wait_ge(self.k.consts_loaded, 64)

    def gpsimd(self, pool):
        pool.wait_ge(self.k.consts_loaded, 64)


class Modulation(Stage):

    def __init__(self, core, layer):
        self.layer = layer
        super().__init__(core)

    def setup(self):
        self.job = self.k.job()
        self.ready = self.k.counter("modulation_ready").event()
        self.k.mod_ready = self.ready

    def tensor(self, pe):
        k = self.k
        pe.wait_ge(*k.silu_ready)
        begin(pe, self.job)
        for n in range(COND):
            if n % 2 == 0:
                slab = k.weights.next(pe).rearrange("p (k c) -> p k c", k=KC)
            for c in range(KC):
                mm = k.weights.matmul(pe, self.job.ap[:, 2 * n:2 * n + 2],
                                      slab[:, c, (n % 2) * P:(n % 2 + 1) * P], k.silu_c[:, c, :],
                                      start=(c == 0), stop=(c == KC - 1))
        mm.then_inc(self.job.full[0], 1)

    def vector(self, dve):
        k, chain = self.k, self.k.dve
        dve.wait_ge(*self.job.full)
        bias = k.v("b_mod", self.layer * COND, COND).unsqueeze(2).broadcast_to([P, COND, 2])
        dve.tensor_tensor(k.mod[:, :, :], self.job.ap[:, 0:2 * COND].rearrange("p (n c) -> p n c", c=2),
                          bias, ALU.add).then_inc(self.job.free[0], 1)
        dve.wait_ge(*self.job.free)

        def gain(i, part, name, cond, add):
            dve.scalar_tensor_tensor(k.coef[:, i, :], k.mod[:, part * KC:(part + 1) * KC, cond], add,
                                     k.v(name, self.layer * KC, KC), ALU.add, ALU.mult)

        gain(0, 1, "g_mix_pre", 0, 1.0)
        gain(1, 1, "g_mix_pre", 1, 1.0)
        gain(2, 2, "g_mix_post", 0, 0.0)
        gain(3, 4, "g_ffn_pre", 0, 1.0)
        dve.scalar_tensor_tensor(k.coef[:, 4, :], k.mod[:, 5 * KC:6 * KC, 0], 0.0,
                                 k.v("g_ffn_post", self.layer * KC, KC), ALU.add, ALU.mult)\
           .then_inc(self.ready[0], 1)
        dve.wait_ge(*self.ready)


def root_inverse(act, chain, out, sums, eps, free=None):
    ins = act.activation(out, sums, ACT.Ln, bias=eps)
    if free is None:
        chain.link(ins)
    else:
        ins.then_inc(free[0], 1)
        act.wait_ge(*free)
    return act.activation(out, out, ACT.Exp, scale=-0.5)


class PreNorm(Stage):

    def __init__(self, core, x, x_ready, out, gain, shift):
        self.x, self.x_ready, self.out, self.gain, self.shift = x, x_ready, out, gain, shift
        super().__init__(core)

    def setup(self):
        k = self.k
        self.sq = k.area(AT_SQ, KC, T)
        self.rs = k.area(AT_RS, T)
        self.squared = k.counter("squared").events(KC)
        self.job = k.job()
        self.root = k.counter("root_ready").event()
        self.ready = k.counter("normed_ready").events(KC)
        self.root_free, k.root_free = k.root_free, self.ready[-1]

    def scalar(self, act):
        for c in range(KC):
            act.wait_ge(*self.x_ready[c])
            act.activation(self.sq[:, c, :], self.x[:, c, :], ACT.Square).then_inc(self.squared[c][0], 1)
        act.wait_ge(*self.job.full)
        if self.root_free:
            act.wait_ge(*self.root_free)
        root_inverse(act, self.k.act, self.rs, self.job.ap[:, 0:T], self.k.eps[:, 0:1], self.job.free)\
            .then_inc(self.root[0], 1)

    def tensor(self, pe):
        begin(pe, self.job)
        for c in range(KC):
            pe.wait_ge(*self.squared[c])
            mm = pe.matmul(self.job.ap[:, 0:T], self.k.c("mean"), self.sq[:, c, :],
                           start=(c == 0), stop=(c == KC - 1))
        mm.then_inc(self.job.full[0], 1)

    def vector(self, dve):
        k = self.k
        dve.wait_ge(*self.root)
        k.dve.link(dve.tensor_tensor(self.out, self.x, over_chunks(self.rs, KC), ALU.mult))
        for c in range(KC):
            dve.tensor_scalar(self.out[:, c, :], self.out[:, c, :], self.gain[:, c:c + 1],
                              self.shift[:, c:c + 1], ALU.mult, ALU.add).then_inc(self.ready[c][0], 1)
        dve.wait_ge(*self.ready[-1])


class OutProjection(Stage):

    def __init__(self, core, x, x_ready, chunks, rms_gain=None, bias=None, ln=None, glu=False):
        self.x, self.x_ready, self.chunks = x, x_ready, chunks
        self.rms_gain, self.bias, self.ln, self.glu = rms_gain, bias, ln, glu
        super().__init__(core)

    def setup(self):
        k = self.k
        self.y = k.area(AT_Y, KC, T)
        self.sq = k.area(AT_SQ, KC, T)
        self.rs = k.area(AT_RS, T)
        self.gate = k.area(AT_RS, 2, T)
        self.y_ready = k.counter("y_ready_act" if self.ln is None else "y_ready").events(KC)
        self.y_squared = k.counter("y_squared").events(KC)
        if self.glu:
            self.gate_used = k.counter("out_gate_used").events(KC)
            self.out_jobs = [k.job(free) for free in self.gate_used]
        else:
            self.out_jobs = [k.job(free) for free in (self.y_squared if self.ln is None else self.y_ready)[1::2]]
        self.sum_job = k.job()
        if self.ln is not None:
            self.var_job = k.job()
            self.centred = k.counter("centred").event()
        if self.glu:
            self.gated = k.counter("out_gate").events(KC)
        self.root = k.counter("root_ready").event()
        self.h_new = k.counter("residual_ready").events(KC)
        k.h_ready = self.h_new
        self.root_free, k.root_free = k.root_free, self.h_new[-1]

    def columns(self, pe, job, n, tiles):
        k = self.k
        out = job.ap[:, tiles * T:(tiles + 1) * T]
        for c in range(self.chunks):
            if self.chunks == KC:
                if n % 2 == 0 and c == 0:
                    self.slab = k.weights.next(pe).rearrange("p (k c) -> p k c", k=KC)
                w = self.slab[:, c, (n % 2) * P:(n % 2 + 1) * P]
            else:
                i = n * self.chunks + c
                if i % SLAB_TILES == 0:
                    self.slab = k.weights.next(pe).rearrange("p (t c) -> p t c", c=P)
                w = self.slab[:, i % SLAB_TILES, :]
            if n == 0:
                pe.wait_ge(*self.x_ready[c])
            mm = k.weights.matmul(pe, out, w, self.x[:, c, :], start=(c == 0), stop=(c == self.chunks - 1))
        return mm

    def tensor(self, pe):
        for j, job in enumerate(self.out_jobs):
            begin(pe, job)
            self.columns(pe, job, 2 * j, 0)
            self.columns(pe, job, 2 * j + 1, 1).then_inc(job.full[0], 1)
        begin(pe, self.sum_job)
        rms = self.ln is None
        for c in range(KC):
            pe.wait_ge(*(self.y_squared if rms else self.y_ready)[c])
            mm = pe.matmul(self.sum_job.ap[:, 0:T], self.k.c("mean"), (self.sq if rms else self.y)[:, c, :],
                           start=(c == 0), stop=(c == KC - 1))
        mm.then_inc(self.sum_job.full[0], 1)
        if not rms:
            begin(pe, self.var_job)
            for c in range(KC):
                pe.wait_ge(*self.y_squared[c])
                mm = pe.matmul(self.var_job.ap[:, 0:T], self.k.c("mean"), self.sq[:, c, :],
                               start=(c == 0), stop=(c == KC - 1))
            mm.then_inc(self.var_job.full[0], 1)

    def scalar(self, act):
        k = self.k
        if self.ln is None:
            for j, job in enumerate(self.out_jobs):
                act.wait_ge(*job.full)
                for t in range(2):
                    c = 2 * j + t
                    b = self.bias[:, c:c + 1] if self.bias is not None else 0.0
                    ins = act.activation(self.y[:, c, :], job.ap[:, t * T:(t + 1) * T], ACT.Identity, bias=b)
                    ins.then_inc(self.y_ready[c][0], 1)
                    ins = act.activation(self.sq[:, c, :], job.ap[:, t * T:(t + 1) * T], ACT.Square, bias=b)
                    ins.then_inc(self.y_squared[c][0], 1)
            act.wait_ge(*self.sum_job.full)
            if self.root_free:
                act.wait_ge(*self.root_free)
            root_inverse(act, k.act, self.rs, self.sum_job.ap[:, 0:T], k.eps[:, 0:1], self.sum_job.free)\
                .then_inc(self.root[0], 1)
            return
        if self.glu:
            for c, job in enumerate(self.out_jobs):
                act.wait_ge(*job.full)
                if c >= 2:
                    act.wait_ge(*self.gate_used[c - 2])
                act.activation(self.gate[:, c % 2, :], job.ap[:, T:2 * T], ACT.Sigmoid)\
                   .then_inc(self.gated[c][0], 1)
        act.wait_ge(*self.centred)
        for c in range(KC):
            act.activation(self.sq[:, c, :], self.y[:, c, :], ACT.Square).then_inc(self.y_squared[c][0], 1)
        act.wait_ge(*self.var_job.full)
        root_inverse(act, k.act, self.rs, self.var_job.ap[:, 0:T], k.eps[:, 1:2], self.var_job.free)\
            .then_inc(self.root[0], 1)

    def vector(self, dve):
        k = self.k
        if self.ln is None:
            dve.wait_ge(*self.root)
            k.dve.link(dve.tensor_tensor(self.y, self.y, over_chunks(self.rs, KC), ALU.mult))
            for c in range(KC):
                dve.scalar_tensor_tensor(k.h[:, c, :], self.y[:, c, :], self.rms_gain[:, c:c + 1], k.h[:, c, :],
                                         ALU.mult, ALU.add).then_inc(self.h_new[c][0], 1)
            dve.wait_ge(*self.h_new[-1])
            return
        if self.glu:
            for c, job in enumerate(self.out_jobs):
                dve.wait_ge(*self.gated[c])
                dve.tensor_tensor(self.y[:, c, :], job.ap[:, 0:T], self.gate[:, c % 2, :], ALU.mult)\
                   .then_inc(self.gate_used[c][0], 1)
                dve.wait_ge(*self.gate_used[c])
                dve.scalar_tensor_tensor(self.y[:, c, :], k.h[:, c, :], ALPHA, self.y[:, c, :], ALU.mult, ALU.add)\
                   .then_inc(self.y_ready[c][0], 1)
        else:
            for j, job in enumerate(self.out_jobs):
                dve.wait_ge(*job.full)
                for t in range(2):
                    c = 2 * j + t
                    dve.scalar_tensor_tensor(self.y[:, c, :], k.h[:, c, :], ALPHA, job.ap[:, t * T:(t + 1) * T],
                                             ALU.mult, ALU.add).then_inc(self.y_ready[c][0], 1)
        dve.wait_ge(*self.sum_job.full)
        dve.tensor_copy(self.rs, self.sum_job.ap[:, 0:T]).then_inc(self.sum_job.free[0], 1)
        dve.wait_ge(*self.sum_job.free)
        dve.tensor_tensor(self.y, self.y, over_chunks(self.rs, KC), ALU.subtract).then_inc(self.centred[0], 1)
        dve.wait_ge(*self.root)
        k.dve.link(dve.tensor_tensor(self.y, self.y, over_chunks(self.rs, KC), ALU.mult))
        gain, shift = (k.v(n, self.ln * KC, KC) for n in ("ln_g", "ln_b"))
        for c in range(KC):
            dve.tensor_scalar(k.h[:, c, :], self.y[:, c, :], gain[:, c:c + 1], shift[:, c:c + 1],
                              ALU.mult, ALU.add).then_inc(self.h_new[c][0], 1)
        dve.wait_ge(*self.h_new[-1])


class GateUp(Stage):

    def __init__(self, core, x, x_ready):
        self.x, self.x_ready = x, x_ready
        super().__init__(core)

    def setup(self):
        k = self.k
        self.hid = k.area(AT_HID, FC, T)
        self.silu = k.counter("gate_ready").events(FC)
        self.ready = k.counter("hidden_ready").events(FC)
        self.jobs = [k.job(free) for free in self.ready]

    def tensor(self, pe):
        k = self.k
        for j, job in enumerate(self.jobs):
            begin(pe, job)
            slab = k.weights.next(pe).rearrange("p (k c) -> p k c", k=KC)
            for half in range(2):
                for c in range(KC):
                    if j == 0:
                        pe.wait_ge(*self.x_ready[c])
                    mm = k.weights.matmul(pe, job.ap[:, half * T:(half + 1) * T],
                                          slab[:, c, half * P:(half + 1) * P], self.x[:, c, :],
                                          start=(c == 0), stop=(c == KC - 1))
            mm.then_inc(job.full[0], 1)

    def scalar(self, act):
        for j, job in enumerate(self.jobs):
            act.wait_ge(*job.full)
            act.activation(self.hid[:, j, :], job.ap[:, 0:T], ACT.Silu).then_inc(self.silu[j][0], 1)

    def vector(self, dve):
        for j, job in enumerate(self.jobs):
            dve.wait_ge(*self.silu[j])
            dve.tensor_tensor(self.hid[:, j, :], self.hid[:, j, :], job.ap[:, T:2 * T], ALU.mult)\
               .then_inc(self.ready[j][0], 1)


def feed_forward(k, x, x_ready, **residual):
    up = GateUp(k, x, x_ready)
    return [up, OutProjection(k, up.hid, up.ready, FC, **residual)]


MIXERS = {}
T2 = 2 * T
N4 = A_HEADS * P
H_A = 0
H_Q = 6656
H_K = H_Q + A_HEADS * T
H_V = H_K + A_HEADS * T2
H_Z = H_V + A_HEADS * T2
H_QB = H_Z + A_HEADS * T
H_KB = H_QB + B_PAIRS * T
H_VB = H_KB + T2
H_PAD = H_VB + T2
H_GATE = H_PAD + 3 * 2 * (T + CONV_A - 1)
H_MIX = H_GATE + 3 * T2
H_END = H_MIX + KC * T
H_P = 0
H_PT = H_P + 2 * T2
H_VT = H_PT + 2 * 4 * T
H_GB = 0
H_L = H_GB + 16 * P
H_X = H_L + 16 * P
H_XT = H_QB
H_QS = H_XT + 16 * P
H_KT = H_END
H_VTOK = H_KT + 8 * P
H_S = H_VTOK + 8 * P
H_LM = H_S + 2 * DH * P
SEQS = 2


class HybridProjection(Stage):

    def setup(self):
        k = self.k
        self.a = k.area(H_A, KC, T2)
        self.norms = [PreNorm(k, k.area(H_END, KC, T), [(k.consts_loaded, 64)] * KC, self.a[:, :, 0:T],
                              k.coef[:, 1, :], k.mod[:, 0:KC, 1]),
                      PreNorm(k, k.h[:, :, :], k.h_ready, self.a[:, :, T:T2],
                              k.coef[:, 0, :], k.mod[:, 0:KC, 0])]
        self.gate_jobs = k.take(2)
        self.beta = k.area(H_GATE, T2)[0:8, :]
        self.g = k.area(H_GATE + T2, T2)[0:8, :]
        self.g_abs = k.area(H_GATE + 2 * T2, T2)[0:8, :]
        lat = slice(T, T2)
        q, kk, v = k.area(H_Q, A_HEADS, T), k.area(H_K, A_HEADS, T2), k.area(H_V, A_HEADS, T2)
        z, qb = k.area(H_Z, A_HEADS, T), k.area(H_QB, B_PAIRS, T)
        every = slice(0, T2)
        self.chunks = [(q[:, h, :], lat, "conv") for h in range(4)] + [(kk[:, h, :], every, "conv") for h in range(4)]
        self.chunks += [(v[:, h, :], every, "conv") for h in range(4)] + [(z[:, h, :], lat, "silu") for h in range(4)]
        self.chunks += [(qb[:, h, :], lat, "copy") for h in range(4)]
        self.chunks += [(k.area(H_KB, T2), every, "copy"), (k.area(H_VB, T2), every, "copy")]
        self.taken = k.counter("projection_taken").events(len(self.chunks))
        self.jobs = [k.job(free) for free in self.taken]
        self.pad = k.area(H_PAD, 3, SEQS, T + CONV_A - 1)
        self.pad_clear = k.counter("pad_clear").event()
        self.convolved = k.counter("convolved").events(12)
        self.conv_ready = k.counter("conv_ready").events(12)
        self.gate_exp = k.counter("gate_exp").event()
        self.gate_linear = k.counter("gate_linear").event()
        self.k.gates_ready = k.counter("gates_ready").events(2)
        self.heads = [(self.chunks[h][0], "ones", 1.0) for h in range(8)]
        self.heads += [(self.chunks[h][0], "ones64", 1.0 / 64) for h in range(16, 21)]
        self.squared = k.counter("head_squared").events(len(self.heads))
        self.sum_jobs = k.take(len(self.heads))
        self.root = k.counter("head_root").events(len(self.heads))
        self.normed = k.counter("head_normed").events(len(self.heads))
        self.turn_jobs = k.take(5)
        self.turned = k.counter("rope_done").events(5)
        self.sq = k.area(AT_SQ, 2, T2)
        self.rs = k.area(AT_SQ + 2 * T2, 2, T2)
        k.hyb = self

    def tensor(self, pe):
        k = self.k
        for norm in self.norms:
            norm.tensor(pe)
        for norm in self.norms:
            pe.wait_ge(*norm.ready[-1])
        for job, name in zip(self.gate_jobs, ("hyb_beta_w", "hyb_g_w")):
            begin(pe, job)
            w = k.v(name, 0, KC * 8).rearrange("p (k c) -> p k c", k=KC)
            for c in range(KC):
                mm = pe.matmul(job.ap[0:8, 0:T2], w[:, c, :], self.a[:, c, :], start=(c == 0), stop=(c == KC - 1))
            mm.then_inc(job.full[0], 1)
        for n, (job, (_, tokens, _)) in enumerate(zip(self.jobs, self.chunks)):
            begin(pe, job)
            if n % 2 == 0:
                slab = k.weights.next(pe).rearrange("p (k c) -> p k c", k=KC)
            out = job.ap[:, 0:tokens.stop - tokens.start]
            for c in range(KC):
                mm = k.weights.matmul(pe, out, slab[:, c, (n % 2) * P:(n % 2 + 1) * P], self.a[:, c, tokens],
                                      start=(c == 0), stop=(c == KC - 1))
            mm.then_inc(job.full[0], 1)
        for i, (x, ones, _) in enumerate(self.heads):
            n = x.shape[1]
            begin(pe, self.sum_jobs[i])
            pe.wait_ge(*self.squared[i])
            pe.matmul(self.sum_jobs[i].ap[:, 0:n], k.c(ones), self.sq[:, i % 2, 0:n], start=True, stop=True)\
              .then_inc(self.sum_jobs[i].full[0], 1)
        for i in range(5):
            x = self.heads[8 + i][0]
            x = x[:, x.shape[1] - T:]
            begin(pe, self.turn_jobs[i])
            pe.wait_ge(*self.normed[8 + i])
            pe.matmul(self.turn_jobs[i].ap[:, 0:T], k.c("rope_turn"), x, start=True, stop=True)\
              .then_inc(self.turn_jobs[i].full[0], 1)

    def scalar(self, act):
        k = self.k
        for norm in self.norms:
            norm.scalar(act)
        beta_job, g_job = self.gate_jobs
        act.wait_ge(*beta_job.full)
        act.activation(self.beta, beta_job.ap[0:8, 0:T2], ACT.Sigmoid).then_inc(beta_job.free[0], 1)
        act.wait_ge(*g_job.full)
        dt_bias = k.v("hyb_dt_bias", rows=8)
        k.act.link(act.activation(self.g_abs, g_job.ap[0:8, 0:T2], ACT.Abs, bias=dt_bias))
        act.activation(self.g, g_job.ap[0:8, 0:T2], ACT.Identity, bias=dt_bias).then_inc(g_job.free[0], 1)
        act.wait_ge(*g_job.free)
        act.activation(k.cols[0:8, 0, 0:1], k.v("hyb_a_log", rows=8), ACT.Exp).then_inc(self.gate_linear[0], 1)
        k.act.link(act.activation(self.g_abs, self.g_abs, ACT.Exp, scale=-1.0))
        act.activation(self.g_abs, self.g_abs, ACT.Ln, bias=k.eps[0:8, 2:3]).then_inc(self.gate_exp[0], 1)
        act.wait_ge(*self.pad_clear)

        def silu(n):
            act.wait_ge(*self.convolved[n])
            x = self.chunks[n][0]
            act.activation(x, x, ACT.Silu).then_inc(self.conv_ready[n][0], 1)

        for n, (job, (x, tokens, kind)) in enumerate(zip(self.jobs, self.chunks)):
            act.wait_ge(*job.full)
            seqs = (tokens.stop - tokens.start) // T
            if kind == "conv":
                if n >= 3:
                    act.wait_ge(*self.convolved[n - 3])
                act.activation(self.pad[:, n % 3, 0:seqs, 2:2 + T],
                               job.ap[:, 0:seqs * T].rearrange("p (s t) -> p s t", t=T), ACT.Identity)\
                   .then_inc(self.taken[n][0], 1)
            else:
                act.activation(x, job.ap[:, 0:seqs * T], ACT.Silu if kind == "silu" else ACT.Identity)\
                   .then_inc(self.taken[n][0], 1)
            if 1 <= n <= 12:
                silu(n - 1)
        for i, (x, _, scale) in enumerate(self.heads):
            n = x.shape[1]
            if i < 8:
                act.wait_ge(*self.conv_ready[i])
            else:
                act.wait_ge(*self.taken[8 + i])
            if i >= 2:
                act.wait_ge(*self.sum_jobs[i - 2].full)
            act.activation(self.sq[:, i % 2, 0:n], x, ACT.Square).then_inc(self.squared[i][0], 1)
            act.wait_ge(*self.sum_jobs[i].full)
            if i >= 2:
                act.wait_ge(*self.normed[i - 2])
            act.activation(self.rs[:, i % 2, 0:n], self.sum_jobs[i].ap[:, 0:n], ACT.Ln, bias=k.eps[:, 0:1],
                           scale=scale).then_inc(self.sum_jobs[i].free[0], 1)
            act.wait_ge(*self.sum_jobs[i].free)
            act.activation(self.rs[:, i % 2, 0:n], self.rs[:, i % 2, 0:n], ACT.Exp, scale=-0.5)\
               .then_inc(self.root[i][0], 1)

    def vector(self, dve):
        k = self.k
        chain = k.dve
        dve.memset(self.pad[:, :, :, 0:2], 0.0)
        dve.memset(self.pad[:, :, :, 2 + T:4 + T], 0.0).then_inc(self.pad_clear[0], 1)
        for norm in self.norms:
            norm.vector(dve)
        dve.wait_ge(*self.gate_linear)
        chain.link(dve.tensor_scalar(self.g, self.g, 0.0, None, ALU.max))
        dve.wait_ge(*self.gate_exp)
        chain.link(dve.tensor_tensor(self.g, self.g, self.g_abs, ALU.add))
        dve.tensor_scalar(self.g, self.g, k.cols[0:8, 0, 0:1], -1.0, ALU.mult, ALU.mult)\
           .then_inc(k.gates_ready[0][0], 1)
        dve.wait_ge(*k.gates_ready[0])
        for n in range(12):
            x, tokens, _ = self.chunks[n]
            seqs = (tokens.stop - tokens.start) // T
            x = x.rearrange("p (s t) -> p s t", t=T)
            dve.wait_ge(*self.taken[n])
            for j in range(CONV_A):
                w = k.v("hyb_conv_w", j * 12 + n)
                src = self.pad[:, n % 3, 0:seqs, j:j + T]
                if j == 0:
                    ins = dve.tensor_scalar(x, src, w, None, ALU.mult)
                else:
                    ins = dve.scalar_tensor_tensor(x, src, w, x, ALU.mult, ALU.add)
                if j < CONV_A - 1:
                    chain.link(ins)
            ins.then_inc(self.convolved[n][0], 1)
        for i, (x, _, _) in enumerate(self.heads):
            n = x.shape[1]
            dve.wait_ge(*self.root[i])
            gain = (P ** -0.5 if i < 4 else 1.0) if i < 8 else k.v("hyb_q_norm" if i < 12 else "hyb_k_norm")
            dve.scalar_tensor_tensor(x, x, gain, self.rs[:, i % 2, 0:n], ALU.mult, ALU.mult)\
               .then_inc(self.normed[i][0], 1)
        for i in range(5):
            x = self.heads[8 + i][0]
            x = x[:, x.shape[1] - T:]
            turned = self.sq[:, i % 2, 0:T]
            dve.wait_ge(*self.normed[8 + i])
            dve.wait_ge(*self.turn_jobs[i].full)
            dve.tensor_tensor(turned, self.turn_jobs[i].ap[:, 0:T], k.c("sin"), ALU.mult)\
               .then_inc(self.turn_jobs[i].free[0], 1)
            chain.link(dve.tensor_tensor(x, x, k.c("cos"), ALU.mult))
            dve.wait_ge(*self.turn_jobs[i].free)
            dve.tensor_tensor(x, x, turned, ALU.add).then_inc(self.turned[i][0], 1)


class HybridAttention(Stage):

    def setup(self):
        k = self.k
        self.q, self.kb, self.vb = k.area(H_QB, B_PAIRS, T), k.area(H_KB, T2), k.area(H_VB, T2)
        self.probs = k.area(H_P, 2, T2)
        self.pt = k.area(H_PT, 2, 4, T)
        self.vt = k.area(H_VT, 4, P)
        self.out = k.area(H_MIX + A_HEADS * T, B_PAIRS, T)
        self.vt_ready = k.counter("values_by_token").event()
        self.vt_job = k.job(self.vt_ready)
        self.units = [(j, half, t) for j in range(B_PAIRS) for half in range(2) for t in range(TT)]
        n = len(self.units)
        self.score_jobs, self.turn_jobs, self.pv_jobs = [], [], []
        self.peak = k.counter("score_peak").events(n)
        self.exp_done = k.counter("exp_done").events(n)
        self.probs_ready = k.counter("probs_ready").events(n)
        self.pt_ready = k.counter("probs_turned").events(n)
        self.out_ready = k.counter("attention_out").events(n // 2)
        for u in range(n + 1):
            if u < n:
                self.score_jobs.append(k.job(self.exp_done[u]))
            if u >= 1:
                self.turn_jobs.append(k.job(self.pt_ready[u - 1]))
                if u % 2 == 0:
                    self.pv_jobs.append(k.job(self.out_ready[u // 2 - 1]))
        k.attention_out = self.out_ready

    def tensor(self, pe):
        k = self.k
        begin(pe, self.vt_job)
        pe.wait_ge(*k.hyb.taken[21])
        for s in range(4):
            mm = pe.transpose(self.vt_job.ap[:, s * P:(s + 1) * P], self.vb[:, s * P:(s + 1) * P], k.c("ident"))
        mm.then_inc(self.vt_job.full[0], 1)
        pe.wait_ge(*k.hyb.turned[4])
        for u in range(len(self.units) + 1):
            if u < len(self.units):
                j, half, t = self.units[u]
                rows = slice(64 * half, 64 * half + 64)
                begin(pe, self.score_jobs[u])
                pe.matmul(self.score_jobs[u].ap[:, :], self.q[rows, j, t * P:(t + 1) * P], self.kb[rows, :],
                          start=True, stop=True).then_inc(self.score_jobs[u].full[0], 1)
            if u >= 1:
                w = u - 1
                begin(pe, self.turn_jobs[w])
                pe.wait_ge(*self.probs_ready[w])
                for s in range(4):
                    mm = pe.transpose(self.turn_jobs[w].ap[:, s * P:(s + 1) * P],
                                      self.probs[:, w % 2, s * P:(s + 1) * P], k.c("ident"))
                mm.then_inc(self.turn_jobs[w].full[0], 1)
                if w % 2 == 1:
                    m = w // 2
                    begin(pe, self.pv_jobs[m])
                    if m == 0:
                        pe.wait_ge(*self.vt_ready)
                    pe.wait_ge(*self.pt_ready[w])
                    for s in range(4):
                        mm = pe.matmul(self.pv_jobs[m].ap[:, 0:T], self.vt[:, s, :], self.pt[:, m % 2, s, :],
                                       start=(s == 0), stop=(s == 3))
                    mm.then_inc(self.pv_jobs[m].full[0], 1)

    def scalar(self, act):
        k = self.k
        act.wait_ge(*self.vt_job.full)
        act.activation(self.vt, self.vt_job.ap[:, :].rearrange("p (s c) -> p s c", s=4), ACT.Identity)\
           .then_inc(self.vt_ready[0], 1)
        for u in range(len(self.units) + 1):
            if u < len(self.units):
                act.wait_ge(*self.peak[u])
                if u >= 2:
                    act.wait_ge(*self.turn_jobs[u - 2].full)
                act.activation(self.probs[:, u % 2, :], self.score_jobs[u].ap[:, :], ACT.Exp,
                               bias=k.cols[:, 1, u:u + 1], scale=0.125, accum_out=k.cols[:, 2, u:u + 1])\
                   .then_inc(self.exp_done[u][0], 1)
            if u >= 1:
                w = u - 1
                act.wait_ge(*self.turn_jobs[w].full)
                m = w // 2
                if m >= 2:
                    act.wait_ge(*self.pv_jobs[m - 2].full)
                t = w % 2
                act.activation(self.pt[:, m % 2, :, t * P:(t + 1) * P],
                               self.turn_jobs[w].ap[:, :].rearrange("p (s c) -> p s c", s=4), ACT.Identity)\
                   .then_inc(self.pt_ready[w][0], 1)

    def vector(self, dve):
        k = self.k
        for u in range(len(self.units) + 1):
            if u < len(self.units):
                dve.wait_ge(*self.score_jobs[u].full)
                k.dve.link(dve.reduce_max(k.cols[:, 3, u:u + 1], self.score_jobs[u].ap[:, :], AXX))
                dve.tensor_scalar(k.cols[:, 1, u:u + 1], k.cols[:, 3, u:u + 1], -0.125, None, ALU.mult)\
                   .then_inc(self.peak[u][0], 1)
                dve.wait_ge(*self.exp_done[u])
                k.dve.link(dve.reciprocal(k.cols[:, 3, u:u + 1], k.cols[:, 2, u:u + 1]))
                dve.tensor_scalar(self.probs[:, u % 2, :], self.probs[:, u % 2, :], k.cols[:, 3, u:u + 1],
                                  None, ALU.mult).then_inc(self.probs_ready[u][0], 1)
            if u >= 2 and u % 2 == 0:
                m = u // 2 - 1
                j, half, _ = self.units[u - 1]
                rows = slice(64 * half, 64 * half + 64)
                dve.wait_ge(*self.pv_jobs[m].full)
                dve.tensor_copy(self.out[rows, j, :], self.pv_jobs[m].ap[rows, 0:T]).then_inc(self.out_ready[m][0], 1)


C_BETA, C_G, C_GC, C_BEG, C_TAIL, C_LAST = 4, 5, 6, 7, 8, 9


class DeltaColumns(Stage):

    def setup(self):
        k = self.k
        self.turned = k.counter("gates_by_token").event()
        self.job = k.job(self.turned)
        self.summed = k.counter("gates_summed").event()
        self.sum_job = k.job(self.summed)
        self.exp = k.counter("gates_exp").event()
        self.ready = k.counter("delta_columns").event()

    def tensor(self, pe):
        k = self.k
        begin(pe, self.job)
        pe.wait_ge(*k.gates_ready[0])
        for n in range(4):
            for i, x in enumerate((k.hyb.beta, k.hyb.g)):
                mm = pe.transpose(self.job.ap[:, i * 32 + n * 8:i * 32 + n * 8 + 8], x[:, n * P:(n + 1) * P],
                                  k.c("ident", 0, 8, rows=8))
        mm.then_inc(self.job.full[0], 1)
        begin(pe, self.sum_job)
        pe.wait_ge(*self.turned)
        for n in range(4):
            for d, tri in enumerate(("upto", "from_")):
                at = n * 8 + d * 4
                mm = pe.matmul(self.sum_job.ap[:, at:at + 4], k.c(tri), k.cols[:, C_G, at:at + 4],
                               start=True, stop=True)
        mm.then_inc(self.sum_job.full[0], 1)

    def scalar(self, act):
        k = self.k
        act.wait_ge(*self.summed)
        act.activation(k.cols[:, C_BEG, :], k.cols[:, C_GC, :], ACT.Exp).then_inc(self.exp[0], 1)

    def vector(self, dve):
        k = self.k
        dve.wait_ge(*self.job.full)
        dve.tensor_copy(k.cols[:, C_BETA:C_G + 1, :], self.job.ap[:, 0:64].rearrange("p (a b) -> p a b", a=2))\
           .then_inc(self.turned[0], 1)
        dve.wait_ge(*self.sum_job.full)
        dve.tensor_copy(k.cols[:, C_GC, :], self.sum_job.ap[:, 0:32]).then_inc(self.summed[0], 1)
        dve.wait_ge(*self.exp)
        dve.wait_ge(*self.turned)
        dve.tensor_tensor(k.cols[:, C_BEG, :], k.cols[:, C_BEG, :], k.cols[:, C_BETA, :], ALU.mult)\
           .then_inc(self.ready[0], 1)
        dve.wait_ge(*self.ready)


class Delta(Stage):

    def __init__(self, core, seq):
        self.seq = seq
        super().__init__(core)

    def setup(self):
        k = self.k
        s = self.seq
        self.gb, self.l, self.x, self.xt, self.qs = (
            k.area(at, 4, A_HEADS, P) for at in (H_GB, H_L, H_X, H_XT, H_QS))
        self.lm = k.area(H_LM, 2, A_HEADS, P)
        self.kt, self.vt = k.area(H_KT, TT, A_HEADS, P), k.area(H_VTOK, TT, A_HEADS, P)
        self.state = k.area(H_S, 2, DH, P)
        self.kf = k.area(H_K, A_HEADS, T2)
        self.vf = k.area(H_V, A_HEADS, T2)
        self.qf = k.area(H_Q, A_HEADS, T)
        self.groups = [(d, t) for d in range(DIRS) for t in range(TT)]
        self.tok_ready = k.counter("delta_by_token").events(4)
        self.tok_jobs = [k.job(e) for e in self.tok_ready]
        self.gb_ready = k.counter("decay_rows").events(4)
        self.gb_jobs = [k.job(e) for e in self.gb_ready]
        self.diff = k.counter("decay_difference").events(4)
        self.decay = k.counter("decay_ready").events(4)
        self.l_ready = k.counter("lower_ready").events(4)
        self.kk_jobs = [k.job(e) for e in self.l_ready]
        self.masked = k.counter("pairs_masked").events(4 * len(LEVELS))
        self.q_ready = k.counter("inverse_q").events(4 * len(LEVELS))
        self.x_ready = k.counter("inverse_x").events(4 * len(LEVELS))
        self.xt_ready = k.counter("inverse_xt").events(4 * len(LEVELS))
        self.level_jobs = {}
        for l in range(len(LEVELS)):
            for g in range(4):
                self.level_jobs[l, g, "q"] = k.job(self.q_ready[4 * l + g])
            for g in range(4):
                self.level_jobs[l, g, "x"] = k.job(self.x_ready[4 * l + g])
                self.level_jobs[l, g, "xt"] = k.job(self.xt_ready[4 * l + g])
        self.rhs = k.counter("delta_rhs").events(4)
        self.w_ready = k.counter("delta_w").events(4)
        self.u_ready = k.counter("delta_u").events(4)
        self.w_jobs, self.u_jobs = [], []
        for g in range(4):
            self.w_jobs.append(k.job(self.w_ready[g]))
            self.u_jobs.append(k.job(self.u_ready[g]))
        self.tail_diff = k.counter("tail_difference").event()
        self.tail_exp = k.counter("tail_exp").event()
        self.tail_ready = k.counter("tail_ready").events(4)
        if s == 1:
            self.intra_diff = k.counter("intra_difference").events(4)
            self.intra_exp = k.counter("intra_exp").events(4)
            self.intra_ready = k.counter("intra_ready").events(4)
            self.kq_jobs = [k.job(e) for e in self.intra_ready]
            self.qd_exp = k.counter("query_decay_exp").events(4)
            self.qd_ready = k.counter("query_decay").events(4)
        self.v_new = k.counter("value_new").events(4)
        self.s_new = k.counter("state_new").events(4)
        self.steps = [(0, 0, 0), (0, 1, 1), (1, 0, 1), (1, 1, 0)]
        self.ws_jobs, self.kv_jobs = [], []
        for i, (step, _, _) in enumerate(self.steps):
            zero = s == 0 and step == 0
            last = s == 1 and step == 1
            self.ws_jobs.append(None if zero else k.job(self.v_new[i]))
            self.kv_jobs.append(None if last else k.job(self.s_new[i]))
        if s == 1:
            self.out_jobs = k.take(TT)

    def tensor(self, pe):
        k, s = self.k, self.seq
        if s == 0:
            pe.wait_ge(*k.hyb.conv_ready[11])
            pe.wait_ge(*k.hyb.normed[7])
        for i, (job, src) in enumerate(zip(self.tok_jobs, (self.kf, self.kf, self.vf, self.vf))):
            begin(pe, job)
            at = s * T + (i % 2) * P
            for h in range(A_HEADS):
                mm = pe.transpose(job.ap[:, h * P:(h + 1) * P], src[:, h, at:at + P], k.c("ident"))
            mm.then_inc(job.full[0], 1)
        for g, (d, t) in enumerate(self.groups):
            begin(pe, self.gb_jobs[g])
            for h in range(A_HEADS):
                col = k.cols[:, C_G, (s * TT + t) * 8 + d * 4 + h:(s * TT + t) * 8 + d * 4 + h + 1]
                mm = pe.matmul(self.gb_jobs[g].ap[:, h * P:(h + 1) * P], col.broadcast_to([P, P]),
                               k.c(("upto", "from_")[d]), start=True, stop=True)
            mm.then_inc(self.gb_jobs[g].full[0], 1)
        for g, (d, t) in enumerate(self.groups):
            begin(pe, self.kk_jobs[g])
            for h in range(A_HEADS):
                kt = self.kf[:, h, s * T + t * P:s * T + (t + 1) * P]
                mm = pe.matmul(self.kk_jobs[g].ap[:, h * P:(h + 1) * P], kt, kt, start=True, stop=True)
            mm.then_inc(self.kk_jobs[g].full[0], 1)
        for l in range(len(LEVELS)):
            for g in range(4):
                job = self.level_jobs[l, g, "q"]
                begin(pe, job)
                pe.wait_ge(*self.masked[4 * l + g])
                if l > 0:
                    pe.wait_ge(*self.xt_ready[4 * (l - 1) + g])
                for h in range(A_HEADS):
                    mm = pe.matmul(job.ap[:, h * P:(h + 1) * P], self.lm[:, g % 2, h, :], self.xt[:, g, h, :],
                                   start=True, stop=True)
                mm.then_inc(job.full[0], 1)
            for g in range(4):
                pe.wait_ge(*self.q_ready[4 * l + g])
                if l > 0:
                    pe.wait_ge(*self.x_ready[4 * (l - 1) + g])
                for which, left, right in (("x", self.qs, self.x), ("xt", self.x, self.qs)):
                    job = self.level_jobs[l, g, which]
                    begin(pe, job)
                    for h in range(A_HEADS):
                        mm = pe.matmul(job.ap[:, h * P:(h + 1) * P], left[:, g, h, :], right[:, g, h, :],
                                       start=True, stop=True)
                    mm.then_inc(job.full[0], 1)
        for g in range(4):
            pe.wait_ge(*self.rhs[g])
            begin(pe, self.w_jobs[g])
            for h in range(A_HEADS):
                mm = pe.matmul(self.w_jobs[g].ap[:, h * P:(h + 1) * P], self.l[:, g, h, :], self.xt[:, g, h, :],
                               start=True, stop=True)
            mm.then_inc(self.w_jobs[g].full[0], 1)
            begin(pe, self.u_jobs[g])
            for h in range(A_HEADS):
                mm = pe.matmul(self.u_jobs[g].ap[:, h * P:(h + 1) * P], self.xt[:, g, h, :], self.x[:, g, h, :],
                               start=True, stop=True)
            mm.then_inc(self.u_jobs[g].full[0], 1)
        if s == 1:
            for g, (d, t) in enumerate(self.groups):
                begin(pe, self.kq_jobs[g])
                for h in range(A_HEADS):
                    mm = pe.matmul(self.kq_jobs[g].ap[:, h * P:(h + 1) * P],
                                   self.kf[:, h, T + t * P:T + (t + 1) * P], self.qf[:, h, t * P:(t + 1) * P],
                                   start=True, stop=True)
                mm.then_inc(self.kq_jobs[g].full[0], 1)
        for i, (step, d, t) in enumerate(self.steps):
            g = d * TT + t
            if self.ws_jobs[i] is not None:
                begin(pe, self.ws_jobs[i])
                pe.wait_ge(*self.w_ready[g])
                if i >= 2:
                    pe.wait_ge(*self.s_new[i - 2])
                for h in range(A_HEADS):
                    mm = pe.matmul(self.ws_jobs[i].ap[:, h * P:(h + 1) * P], self.qs[:, g, h, :],
                                   self.state[:, self.state_of(step), d * 4 + h, :], start=True, stop=True)
                mm.then_inc(self.ws_jobs[i].full[0], 1)
            if self.kv_jobs[i] is not None:
                begin(pe, self.kv_jobs[i])
                pe.wait_ge(*self.v_new[i])
                pe.wait_ge(*self.tail_ready[g])
                for h in range(A_HEADS):
                    mm = pe.matmul(self.kv_jobs[i].ap[:, h * P:(h + 1) * P], self.l[:, g, h, :], self.x[:, g, h, :],
                                   start=True, stop=True)
                mm.then_inc(self.kv_jobs[i].full[0], 1)
        if s == 1:
            pe.wait_ge(*self.v_new[3])
            for t in range(TT):
                begin(pe, self.out_jobs[t])
                for h in range(A_HEADS):
                    out = self.out_jobs[t].ap[:, h * P:(h + 1) * P]
                    for d in range(DIRS):
                        g, step = d * TT + t, (t if d == 0 else 1 - t)
                        if h == 0:
                            pe.wait_ge(*self.qd_ready[g])
                            pe.wait_ge(*self.intra_ready[g])
                        pe.matmul(out, self.state[:, step, d * 4 + h, :], self.gb[:, g, h, :],
                                  start=(d == 0), stop=False)
                        mm = pe.matmul(out, self.x[:, g, h, :], self.xt[:, g, h, :], start=False, stop=(d == 1))
                mm.then_inc(self.out_jobs[t].full[0], 1)

    def state_of(self, step):
        return step if self.seq == 1 else 0

    def scalar(self, act):
        k, s = self.k, self.seq

        def banked(job):
            return job.ap[:, :].rearrange("p (h c) -> p h c", c=P)

        for i, job in enumerate(self.tok_jobs):
            act.wait_ge(*job.full)
            dst = (self.kt, self.vt)[i // 2][:, i % 2, :, :]
            act.activation(dst, banked(job), ACT.Identity).then_inc(self.tok_ready[i][0], 1)
        for g in range(4):
            act.wait_ge(*self.gb_jobs[g].full)
            act.activation(self.gb[:, g, :, :], banked(self.gb_jobs[g]), ACT.Identity)\
               .then_inc(self.gb_ready[g][0], 1)
        for g in range(4):
            act.wait_ge(*self.diff[g])
            act.activation(self.l[:, g, :, :], self.l[:, g, :, :], ACT.Exp, scale=-1.0).then_inc(self.decay[g][0], 1)
        for l in range(len(LEVELS)):
            for g in range(4):
                n = 4 * l + g
                job = self.level_jobs[l, g, "q"]
                act.wait_ge(*job.full)
                if l > 0:
                    act.wait_ge(*self.level_jobs[l - 1, g, "xt"].full)
                act.activation(self.qs[:, g, :, :], banked(job), ACT.Identity).then_inc(self.q_ready[n][0], 1)
        for g in range(4):
            act.wait_ge(*self.w_jobs[g].full)
            act.wait_ge(*self.level_jobs[len(LEVELS) - 1, g, "xt"].full)
            act.activation(self.qs[:, g, :, :], banked(self.w_jobs[g]), ACT.Copy, scale=-1.0)\
               .then_inc(self.w_ready[g][0], 1)
            act.wait_ge(*self.u_jobs[g].full)
            act.activation(self.x[:, g, :, :], banked(self.u_jobs[g]), ACT.Identity).then_inc(self.u_ready[g][0], 1)
        act.wait_ge(*self.tail_diff)
        k.act.link(act.activation(k.cols[:, C_TAIL, 0:16], k.cols[:, C_TAIL, 0:16], ACT.Exp))
        act.activation(k.cols[:, C_LAST, 0:16], k.cols[:, C_LAST, 0:16], ACT.Exp).then_inc(self.tail_exp[0], 1)
        if s == 1:
            for g in range(4):
                act.wait_ge(*self.intra_diff[g])
                act.activation(self.xt[:, g, :, :], self.xt[:, g, :, :], ACT.Exp).then_inc(self.intra_exp[g][0], 1)
                act.activation(self.gb[:, g, :, :], self.gb[:, g, :, :], ACT.Exp).then_inc(self.qd_exp[g][0], 1)

    def vector(self, dve):
        k, s, chain = self.k, self.seq, self.k.dve

        def banked(job):
            return job.ap[:, :].rearrange("p (h c) -> p h c", c=P)

        def col(row, g, h):
            d, t = self.groups[g]
            at = (s * TT + t) * 8 + d * 4 + h
            return k.cols[:, row, at:at + 1]

        def four(mask):
            return mask.unsqueeze(1).broadcast_to([P, A_HEADS, P])

        for g in range(4):
            dve.wait_ge(*self.gb_ready[g])
            for h in range(A_HEADS):
                ins = dve.tensor_scalar(self.l[:, g, h, :], self.gb[:, g, h, :], col(C_GC, g, h), 0.0,
                                        ALU.subtract, ALU.max)
            ins.then_inc(self.diff[g][0], 1)
        for g in range(4):
            dve.wait_ge(*self.decay[g])
            dve.wait_ge(*self.kk_jobs[g].full)
            for h in range(A_HEADS):
                ins = dve.scalar_tensor_tensor(self.l[:, g, h, :], self.kk_jobs[g].ap[:, h * P:(h + 1) * P],
                                               col(C_BETA, g, h), self.l[:, g, h, :], ALU.mult, ALU.mult)
            ins.then_inc(self.l_ready[g][0], 1)
            for x in (self.x, self.xt):
                ins = dve.tensor_copy(x[:, g, :, :], four(k.c("ident")))
            chain.link(ins)
            dve.wait_ge(*self.l_ready[g])

        def mask(l, g):
            d = self.groups[g][0]
            if 4 * l + g >= 2:
                m = 4 * l + g - 2
                dve.wait_ge(*self.level_jobs[m // 4, m % 4, "q"].full)
            pairs = k.c(("lower_pairs", "upper_pairs")[d], l * P, P)
            dve.tensor_tensor(self.lm[:, g % 2, :, :], self.l[:, g, :, :], four(pairs), ALU.mult)\
               .then_inc(self.masked[4 * l + g][0], 1)

        mask(0, 0)
        mask(0, 1)
        for l in range(len(LEVELS)):
            mask(l, 2)
            mask(l, 3)
            for g in range(4):
                for which, x, ready in (("x", self.x, self.x_ready), ("xt", self.xt, self.xt_ready)):
                    job = self.level_jobs[l, g, which]
                    dve.wait_ge(*job.full)
                    if which == "x":
                        dve.wait_ge(*self.level_jobs[l, g, "xt"].full)
                    dve.tensor_tensor(x[:, g, :, :], x[:, g, :, :], banked(job), ALU.subtract)\
                       .then_inc(ready[4 * l + g][0], 1)
                if g >= 2 and l + 1 < len(LEVELS):
                    mask(l + 1, g - 2)
        dve.wait_ge(*self.xt_ready[-1])
        for i in range(4):
            dve.wait_ge(*self.tok_ready[i])
        for g, (d, t) in enumerate(self.groups):
            for h in range(A_HEADS):
                dve.tensor_scalar(self.l[:, g, h, :], self.kt[:, t, h, :], col(C_BEG, g, h), None, ALU.mult)
                ins = dve.tensor_scalar(self.x[:, g, h, :], self.vt[:, t, h, :], col(C_BETA, g, h), None, ALU.mult)
            ins.then_inc(self.rhs[g][0], 1)
        for g, (d, t) in enumerate(self.groups):
            last = (P - 1) * (1 - d)
            at = (s * TT + t) * 8 + d * 4
            dve.tensor_tensor(k.cols[:, C_TAIL, g * 4:g * 4 + 4], self.gb[:, g, :, last],
                              k.cols[:, C_GC, at:at + 4], ALU.subtract)
            ins = dve.tensor_copy(k.cols[:, C_LAST, g * 4:g * 4 + 4], self.gb[:, g, :, last])
        ins.then_inc(self.tail_diff[0], 1)
        dve.wait_ge(*self.tail_exp)
        for g, (d, t) in enumerate(self.groups):
            dve.wait_ge(*self.w_jobs[g].full)
            for h in range(A_HEADS):
                ins = dve.tensor_scalar(self.l[:, g, h, :], self.kt[:, t, h, :],
                                        k.cols[:, C_TAIL, g * 4 + h:g * 4 + h + 1], None, ALU.mult)
            ins.then_inc(self.tail_ready[g][0], 1)
        if s == 1:
            for g, (d, t) in enumerate(self.groups):
                dve.wait_ge(*self.u_jobs[g].full)
                for h in range(A_HEADS):
                    ins = dve.tensor_scalar(self.xt[:, g, h, :], self.gb[:, g, h, :], col(C_GC, g, h), 0.0,
                                            ALU.subtract, ALU.min)
                ins.then_inc(self.intra_diff[g][0], 1)
            for g, (d, t) in enumerate(self.groups):
                dve.wait_ge(*self.intra_exp[g])
                chain.link(dve.tensor_tensor(self.xt[:, g, :, :], self.xt[:, g, :, :],
                                             four(k.c(("upto", "from_")[d])), ALU.mult))
                dve.wait_ge(*self.kq_jobs[g].full)
                dve.tensor_tensor(self.xt[:, g, :, :], self.xt[:, g, :, :], banked(self.kq_jobs[g]), ALU.mult)\
                   .then_inc(self.intra_ready[g][0], 1)
                dve.wait_ge(*self.qd_exp[g])
                dve.tensor_tensor(self.gb[:, g, :, :], self.gb[:, g, :, :], self.qf[:, :, t * P:(t + 1) * P],
                                  ALU.mult).then_inc(self.qd_ready[g][0], 1)
        for i, (step, d, t) in enumerate(self.steps):
            g = d * TT + t
            dve.wait_ge(*self.u_ready[g])
            if self.ws_jobs[i] is not None:
                dve.wait_ge(*self.ws_jobs[i].full)
                ins = dve.tensor_tensor(self.x[:, g, :, :], self.x[:, g, :, :], banked(self.ws_jobs[i]), ALU.add)
            else:
                ins = dve.tensor_copy(k.cols[:, 10, 0:1], k.cols[:, C_LAST, 0:1])
            ins.then_inc(self.v_new[i][0], 1)
            dve.wait_ge(*self.v_new[i])
            if self.kv_jobs[i] is not None:
                dve.wait_ge(*self.kv_jobs[i].full)
                if i >= 2:
                    dve.wait_ge(*self.s_new[i - 2])
                src = self.state_of(step)
                dst = 0 if s == 0 else step + 1
                for h in range(A_HEADS):
                    ps = self.kv_jobs[i].ap[:, h * P:(h + 1) * P]
                    out = self.state[:, dst, d * 4 + h, :]
                    if self.ws_jobs[i] is None:
                        ins = dve.tensor_copy(out, ps)
                    else:
                        ins = dve.scalar_tensor_tensor(out, self.state[:, src, d * 4 + h, :],
                                                       k.cols[:, C_LAST, g * 4 + h:g * 4 + h + 1], ps,
                                                       ALU.mult, ALU.add)
                ins.then_inc(self.s_new[i][0], 1)


class DeltaReadout(Stage):

    def __init__(self, core, delta):
        self.delta = delta
        super().__init__(core)

    def setup(self):
        k = self.k
        self.copied = k.counter("readout_copied").events(TT)
        self.squared = k.counter("readout_squared").events(TT)
        self.o = k.area(H_K, TT, A_HEADS, P)
        self.sq = k.area(H_V, TT, A_HEADS, P)
        self.jobs = k.take(TT)
        self.root = k.counter("readout_root").events(TT)
        self.ready = k.counter("readout_ready").events(TT)

    def tensor(self, pe):
        for t in range(TT):
            begin(pe, self.jobs[t])
            pe.wait_ge(*self.squared[t])
            pe.matmul(self.jobs[t].ap[:, :], self.k.c("ones"), self.sq[:, t, :, :].rearrange("p h c -> p (h c)"),
                      start=True, stop=True).then_inc(self.jobs[t].full[0], 1)

    def scalar(self, act):
        for t in range(TT):
            job = self.delta.out_jobs[t]
            act.wait_ge(*job.full)
            act.activation(self.o[:, t, :, :].rearrange("p h c -> p (h c)"), job.ap[:, :], ACT.Identity)\
               .then_inc(self.copied[t][0], 1)
            act.activation(self.sq[:, t, :, :].rearrange("p h c -> p (h c)"), job.ap[:, :], ACT.Square)\
               .then_inc(self.squared[t][0], 1)
            act.wait_ge(*self.squared[t])
            act.wait_ge(*self.jobs[t].full)
            flat = self.sq[:, t, :, :].rearrange("p h c -> p (h c)")
            act.activation(flat, self.jobs[t].ap[:, :], ACT.Ln, bias=self.k.eps[:, 0:1], scale=1.0 / P)\
               .then_inc(self.jobs[t].free[0], 1)
            act.wait_ge(*self.jobs[t].free)
            act.activation(flat, flat, ACT.Exp, scale=-0.5).then_inc(self.root[t][0], 1)

    def vector(self, dve):
        k = self.k
        z = k.area(H_Z, A_HEADS, T)
        mix = k.area(H_MIX, KC, T)
        for t in range(TT):
            dve.wait_ge(*self.root[t])
            dve.wait_ge(*self.copied[t])
            dve.tensor_copy(k.cols[:, 10, 1:2], k.cols[:, C_LAST, 0:1]).then_inc(self.delta.out_jobs[t].free[0], 1)
            k.dve.link(dve.scalar_tensor_tensor(self.o[:, t, :, :], self.o[:, t, :, :], k.v("hyb_out_norm"),
                                                self.sq[:, t, :, :], ALU.mult, ALU.mult))
            dve.tensor_tensor(mix[:, 0:A_HEADS, t * P:(t + 1) * P], self.o[:, t, :, :],
                              z[:, :, t * P:(t + 1) * P], ALU.mult).then_inc(self.ready[t][0], 1)
        dve.wait_ge(*self.ready[-1])


def hybrid(k):
    stages = [HybridProjection(k), HybridAttention(k), DeltaColumns(k), Delta(k, 0)]
    stages.append(Delta(k, 1))
    stages.append(DeltaReadout(k, stages[-1]))
    mix_ready = [stages[-1].ready[-1]] * A_HEADS + [k.attention_out[-1]] * B_PAIRS
    return stages + [OutProjection(k, k.area(H_MIX, KC, T), mix_ready, KC, rms_gain=k.coef[:, 2, :])]


MIXERS["hybrid"] = hybrid


F_U = AT_HID
F_C = F_U + KC * (T + 2 * PAD_C)
F_G = F_C + KC * T


class ConformerIn(Stage):

    def __init__(self, core, x, x_ready):
        self.x, self.x_ready = x, x_ready
        super().__init__(core)

    def setup(self):
        k = self.k
        self.u = k.area(F_U, KC, T + 2 * PAD_C)
        self.conv = k.area(F_C, KC, T)
        self.gate = k.area(F_G, 2, T)
        self.edges = k.counter("conv_edges").event()
        self.gated = k.counter("conf_gate").events(KC)
        self.ready = k.counter("conf_u").events(KC)
        self.conv_ready = k.counter("conf_conv").events(KC)
        self.jobs = [k.job(e) for e in self.ready]

    def tensor(self, pe):
        k = self.k
        for j, job in enumerate(self.jobs):
            begin(pe, job)
            slab = k.weights.next(pe).rearrange("p (k c) -> p k c", k=KC)
            for half in range(2):
                for c in range(KC):
                    if j == 0:
                        pe.wait_ge(*self.x_ready[c])
                    mm = k.weights.matmul(pe, job.ap[:, half * T:(half + 1) * T],
                                          slab[:, c, half * P:(half + 1) * P], self.x[:, c, :],
                                          start=(c == 0), stop=(c == KC - 1))
            mm.then_inc(job.full[0], 1)

    def scalar(self, act):
        k = self.k
        for j, job in enumerate(self.jobs):
            act.wait_ge(*job.full)
            if j >= 2:
                act.wait_ge(*self.ready[j - 2])
            act.activation(self.gate[:, j % 2, :], job.ap[:, T:2 * T], ACT.Sigmoid,
                           bias=k.v("conf_b_in", KC + j)).then_inc(self.gated[j][0], 1)

    def vector(self, dve):
        k = self.k
        dve.memset(self.u[:, :, 0:PAD_C], 0.0)
        dve.memset(self.u[:, :, PAD_C + T:], 0.0).then_inc(self.edges[0], 1)
        dve.wait_ge(*self.edges)
        for c in range(KC):
            job = self.jobs[c]
            dve.wait_ge(*self.gated[c])
            dve.scalar_tensor_tensor(self.u[:, c, PAD_C:PAD_C + T], job.ap[:, 0:T], k.v("conf_b_in", c),
                                     self.gate[:, c % 2, :], ALU.add, ALU.mult).then_inc(self.ready[c][0], 1)
            dve.wait_ge(*self.ready[c])
            for j in range(CONV_C):
                w = k.v("conf_dw_w", j * KC + c)
                src = self.u[:, c, j:j + T]
                if j == 0:
                    ins = dve.tensor_scalar(self.conv[:, c, :], src, w, k.v("conf_dw_b", c), ALU.mult, ALU.add)
                else:
                    ins = dve.scalar_tensor_tensor(self.conv[:, c, :], src, w, self.conv[:, c, :],
                                                   ALU.mult, ALU.add)
                if j < CONV_C - 1:
                    k.dve.link(ins)
            ins.then_inc(self.conv_ready[c][0], 1)


class ConformerNorm(Stage):

    def __init__(self, core, x, x_ready):
        self.x, self.x_ready = x, x_ready
        super().__init__(core)

    def setup(self):
        k = self.k
        self.sq, self.rs = k.area(AT_SQ, KC, T), k.area(AT_RS, T)
        self.mean_job = k.job()
        self.var_job = k.job()
        self.centred = k.counter("centred").event()
        self.squared = k.counter("squared").events(KC)
        self.root = k.counter("root_ready").event()
        self.scaled = k.counter("conf_scaled").event()
        self.ready = k.counter("conf_act").events(KC)
        self.root_free, k.root_free = k.root_free, self.scaled

    def tensor(self, pe):
        for job, src, ready in ((self.mean_job, self.x, self.x_ready), (self.var_job, self.sq, self.squared)):
            begin(pe, job)
            for c in range(KC):
                pe.wait_ge(*ready[c])
                mm = pe.matmul(job.ap[:, 0:T], self.k.c("mean"), src[:, c, :], start=(c == 0), stop=(c == KC - 1))
            mm.then_inc(job.full[0], 1)

    def scalar(self, act):
        k = self.k
        act.wait_ge(*self.centred)
        for c in range(KC):
            act.activation(self.sq[:, c, :], self.x[:, c, :], ACT.Square).then_inc(self.squared[c][0], 1)
        act.wait_ge(*self.var_job.full)
        root_inverse(act, k.act, self.rs, self.var_job.ap[:, 0:T], k.eps[:, 0:1], self.var_job.free)\
            .then_inc(self.root[0], 1)
        act.wait_ge(*self.scaled)
        for c in range(KC):
            act.activation(self.x[:, c, :], self.x[:, c, :], ACT.Silu, bias=k.v("conf_ln_b", c),
                           scale=k.v("conf_ln_g", c)).then_inc(self.ready[c][0], 1)

    def vector(self, dve):
        dve.wait_ge(*self.mean_job.full)
        for c in range(KC):
            dve.wait_ge(*self.x_ready[c])
        dve.tensor_copy(self.rs, self.mean_job.ap[:, 0:T]).then_inc(self.mean_job.free[0], 1)
        dve.wait_ge(*self.mean_job.free)
        dve.tensor_tensor(self.x, self.x, over_chunks(self.rs, KC), ALU.subtract).then_inc(self.centred[0], 1)
        dve.wait_ge(*self.root)
        dve.tensor_tensor(self.x, self.x, over_chunks(self.rs, KC), ALU.mult).then_inc(self.scaled[0], 1)


def conformer(k):
    a = k.area(AT_A, KC, T)
    pre = PreNorm(k, k.h[:, :, :], k.h_ready, a, k.coef[:, 0, :], k.mod[:, 0:KC, 0])
    conv = ConformerIn(k, a, pre.ready)
    norm = ConformerNorm(k, conv.conv, conv.conv_ready)
    return [pre, conv, norm, OutProjection(k, conv.conv, norm.ready, KC, rms_gain=k.coef[:, 2, :],
                                           bias=k.v("conf_b_out", 0, KC))]


MIXERS["conformer"] = conformer


M_OUT = AT_A
M_Q = AT_HID
M_K = M_Q + KC * T
M_B = M_K + KC * T
M_V = M_B + KC * T
M_G = M_V + TT * D
M_E = M_G + KC * T
M_ATT = M_E + 2 * KC * T


def project_columns(k, pe, x, x_ready, jobs):
    for j, job in enumerate(jobs):
        begin(pe, job)
        slab = k.weights.next(pe).rearrange("p (k c) -> p k c", k=KC)
        for half in range(2):
            for c in range(KC):
                if j == 0:
                    pe.wait_ge(*x_ready[c])
                mm = k.weights.matmul(pe, job.ap[:, half * T:(half + 1) * T], slab[:, c, half * P:(half + 1) * P],
                                      x[:, c, :], start=(c == 0), stop=(c == KC - 1))
        mm.then_inc(job.full[0], 1)


def project_tokens(k, pe, x, jobs):
    for job in jobs:
        begin(pe, job)
        slab = k.weights.next(pe).rearrange("p (k c) -> p k c", k=KC)
        for t in range(TT):
            for c in range(KC):
                mm = k.weights.matmul(pe, job.ap[:, t * 256:(t + 1) * 256], x[:, c, t * P:(t + 1) * P],
                                      slab[:, c, :], start=(c == 0), stop=(c == KC - 1))
        mm.then_inc(job.full[0], 1)


def pair(job):
    return job.ap[:, :].rearrange("p (a t) -> p a t", a=2)


class HgrnIn(Stage):

    def __init__(self, core, layer):
        self.layer = layer
        super().__init__(core)

    def setup(self):
        k = self.k
        self.x_ready = k.h_ready
        self.q, self.kk, self.b = (k.area(at, KC, T) for at in (M_Q, M_K, M_B))
        self.v, self.g = k.area(M_V, TT, D), k.area(M_G, KC, T)
        self.raw, self.soft = k.area(M_E, KC, T), k.area(M_E + KC * T, KC, T)
        self.q_ready = k.counter("mixer_q").events(4)
        self.f_taken = k.counter("forget_taken").events(4)
        self.v_ready = k.counter("mixer_v").events(4)
        self.g_ready = k.counter("mixer_g").events(4)
        self.jobs = [k.job(e) for e in self.q_ready + self.f_taken + self.v_ready + self.g_ready]
        if self.layer:
            self.bound_shift = k.counter("bound_shift").event()
            self.bound_log = k.counter("bound_log").event()
            self.bound_sums = k.counter("bound_sums").event()
            self.bound_exp = k.counter("bound_exp").event()
            self.bound = k.counter("bound_ready").event()
            self.dist = k.counter("log_distance").event()
            self.log_sum = k.counter("log_sum").event()
        self.k_exp = k.counter("k_sigmoid").event()
        self.log1p = k.counter("log1p_ready").event()
        self.ready = k.counter("decay_cumulated").event()
        self.small = k.cols[:, :, :].rearrange("p a b -> p (a b)")

    def tensor(self, pe):
        k = self.k
        project_columns(k, pe, k.h, self.x_ready, self.jobs[0:8])
        project_tokens(k, pe, k.h, self.jobs[8:12])
        project_columns(k, pe, k.h, self.x_ready, self.jobs[12:16])

    def scalar(self, act):
        k = self.k
        if self.layer:
            act.wait_ge(*self.bound_shift)
            act.activation(self.small[:, 0:56], self.small[:, 0:56], ACT.Exp).then_inc(self.bound_exp[0], 1)
            act.wait_ge(*self.bound_sums)
            act.activation(self.small[:, 56:72], self.small[:, 56:72], ACT.Ln).then_inc(self.bound_log[0], 1)
        for j in range(4):
            act.wait_ge(*self.jobs[j].full)
            act.activation(self.q[:, 2 * j:2 * j + 2, :], pair(self.jobs[j]), ACT.Silu).then_inc(self.q_ready[j][0], 1)
        for j in range(4):
            act.wait_ge(*self.jobs[4 + j].full)
            act.activation(self.raw[:, 2 * j:2 * j + 2, :], pair(self.jobs[4 + j]), ACT.Identity)\
               .then_inc(self.f_taken[j][0], 1)
            act.wait_ge(*self.f_taken[j])
        k.act.link(act.activation(self.kk, self.raw, ACT.Sigmoid, scale=-1.0))
        k.act.link(act.activation(self.soft, self.raw, ACT.Abs))
        k.act.link(act.activation(self.soft, self.soft, ACT.Exp, scale=-1.0))
        act.activation(self.soft, self.soft, ACT.Ln, bias=k.eps[:, 2:3]).then_inc(self.log1p[0], 1)
        if self.layer:
            act.wait_ge(*self.dist)
            k.act.link(act.activation(self.soft, self.soft, ACT.Abs))
            k.act.link(act.activation(self.soft, self.soft, ACT.Exp, scale=-1.0))
            act.activation(self.soft, self.soft, ACT.Ln, bias=k.eps[:, 2:3]).then_inc(self.log_sum[0], 1)
        for j in range(4):
            act.wait_ge(*self.jobs[8 + j].full)
            act.activation(self.v[:, :, j * 256:(j + 1) * 256], pair(self.jobs[8 + j]), ACT.Identity)\
               .then_inc(self.v_ready[j][0], 1)
        for j in range(4):
            act.wait_ge(*self.jobs[12 + j].full)
            act.activation(self.g[:, 2 * j:2 * j + 2, :], pair(self.jobs[12 + j]), ACT.Silu)\
               .then_inc(self.g_ready[j][0], 1)

    def vector(self, dve):
        k, chain = self.k, self.k.dve
        s = self.small
        logits = [k.v("lb_logits", i * KC, KC) for i in range(4)]
        if self.layer:
            most, rest = s[:, 72:80], s[:, 80:88]
            chain.link(dve.tensor_tensor(rest, logits[1], logits[2], ALU.max))
            chain.link(dve.tensor_tensor(rest, rest, logits[3], ALU.max))
            chain.link(dve.tensor_tensor(most, rest, logits[0], ALU.max))
            for i in range(4):
                ins = dve.tensor_tensor(s[:, i * 8:i * 8 + 8], logits[i], most, ALU.subtract)
            for i in range(1, 4):
                ins = dve.tensor_tensor(s[:, 24 + i * 8:32 + i * 8], logits[i], rest, ALU.subtract)
            ins.then_inc(self.bound_shift[0], 1)
            dve.wait_ge(*self.bound_exp)
            chain.link(dve.tensor_tensor(s[:, 56:64], s[:, 0:8], s[:, 8:16], ALU.add))
            chain.link(dve.tensor_tensor(s[:, 56:64], s[:, 56:64], s[:, 16:24], ALU.add))
            chain.link(dve.tensor_tensor(s[:, 56:64], s[:, 56:64], s[:, 24:32], ALU.add))
            chain.link(dve.reciprocal(s[:, 88:96], s[:, 56:64]))
            chain.link(dve.tensor_tensor(s[:, 64:72], s[:, 32:40], s[:, 40:48], ALU.add))
            dve.tensor_tensor(s[:, 64:72], s[:, 64:72], s[:, 48:56], ALU.add).then_inc(self.bound_sums[0], 1)
            dve.wait_ge(*self.bound_log)
            chain.link(dve.tensor_tensor(s[:, 96:104], s[:, 0:8], s[:, 88:96], ALU.mult))
            chain.link(dve.tensor_tensor(most, most, s[:, 56:64], ALU.add))
            chain.link(dve.tensor_tensor(rest, rest, s[:, 64:72], ALU.add))
            chain.link(dve.tensor_tensor(s[:, 104:112], logits[0], most, ALU.subtract))
            dve.tensor_tensor(s[:, 112:120], rest, most, ALU.subtract).then_inc(self.bound[0], 1)
            dve.wait_ge(*self.bound)
        dve.wait_ge(*self.log1p)
        chain.link(dve.tensor_scalar(self.raw, self.raw, 0.0, None, ALU.min))
        chain.link(dve.tensor_tensor(self.raw, self.raw, self.soft, ALU.subtract))
        if self.layer:
            for c in range(KC):
                ins = dve.tensor_scalar(self.raw[:, c, :], self.raw[:, c, :], s[:, 104 + c:105 + c], None, ALU.add)
                dve.tensor_scalar(self.kk[:, c, :], self.kk[:, c, :], s[:, 96 + c:97 + c], None, ALU.mult)
            chain.link(ins)
            for c in range(KC):
                ins = dve.tensor_scalar(self.soft[:, c, :], self.raw[:, c, :], s[:, 112 + c:113 + c], None,
                                        ALU.subtract)
            ins.then_inc(self.dist[0], 1)
            dve.wait_ge(*self.dist)
            for c in range(KC):
                ins = dve.tensor_scalar(self.raw[:, c, :], self.raw[:, c, :], s[:, 112 + c:113 + c], None, ALU.max)
            chain.link(ins)
            dve.wait_ge(*self.log_sum)
            chain.link(dve.tensor_tensor(self.raw, self.raw, self.soft, ALU.add))
        for c in range(KC):
            ins = dve.tensor_tensor_scan(self.b[:, c, :], k.c("one_row"), self.raw[:, c, :], 0.0, ALU.mult, ALU.add)
        ins.then_inc(self.ready[0], 1)
        dve.wait_ge(*self.ready)


H_LEVELS = [128] + LEVELS[::-1] + [0]


class HgrnAttention(Stage):

    def __init__(self, core, src):
        self.src = src
        super().__init__(core)

    def setup(self):
        k = self.k
        n = len(H_LEVELS)
        self.e = k.area(M_E, 2, KC * T)
        self.att = k.area(M_ATT, HEADS, 3, P)
        self.cleared = k.counter("att_cleared").event()
        self.diff = k.counter("pair_exponents").events(n - 1)
        self.exp = k.counter("pair_exp").events(n - 1)
        self.e_ready = k.counter("pair_operands").events(n)
        self.jobs = []
        self.taken = k.counter("pairs_taken").events(2 + 4 * (n - 1))
        for l in range(n):
            at = 0 if l == 0 else 2 + 4 * (l - 1)
            self.jobs.append([k.job(e) for e in self.taken[at:at + (2 if l == 0 else 4)]])
        self.out_ready = k.counter("mixer_out_copied").events(4)
        self.sq_ready = k.counter("mixer_out_squared").events(4)
        self.out_jobs = [k.job(e) for e in self.sq_ready]
        self.sum_jobs = k.take(4)
        self.root = k.counter("mixer_root").events(4)
        self.ready = k.counter("mixer_ready").events(4)

    def tensor(self, pe):
        k = self.k
        q, kk = self.src.q, self.src.kk
        for l, b in enumerate(H_LEVELS):
            e = self.e[:, l % 2, :].rearrange("p (h t) -> p h t", h=HEADS)
            pe.wait_ge(*self.e_ready[l])
            if l == 0:
                for j, job in enumerate(self.jobs[0]):
                    begin(pe, job)
                    for i in range(4):
                        h = 4 * j + i
                        mm = pe.matmul(job.ap[:, i * P:(i + 1) * P], e[:, h, 0:P], e[:, h, P:T], start=True, stop=True)
                    mm.then_inc(job.full[0], 1)
                continue
            for j, job in enumerate(self.jobs[l]):
                begin(pe, job)
                t = j % 2
                cols = slice(t * P, (t + 1) * P)
                for i in range(4):
                    h = 4 * (j // 2) + i
                    left, right = (e, e) if b else (kk, q)
                    mm = pe.matmul(job.ap[:, i * P:(i + 1) * P], left[:, h, cols], right[:, h, cols],
                                   start=True, stop=True)
                mm.then_inc(job.full[0], 1)
        pe.wait_ge(*self.taken[-1])
        v = self.src.v
        pe.wait_ge(*self.src.v_ready[-1])
        for j, job in enumerate(self.out_jobs):
            begin(pe, job)
            for i in range(2):
                h = 2 * j + i
                pe.matmul(job.ap[:, i * T:(i + 1) * T], v[:, 0, h * P:(h + 1) * P], self.att[:, h, 0:2, :],
                          start=True, stop=False)
                mm = pe.matmul(job.ap[:, i * T + P:(i + 1) * T], v[:, 1, h * P:(h + 1) * P], self.att[:, h, 2, :],
                               start=False, stop=True)
            mm.then_inc(job.full[0], 1)
        for j, job in enumerate(self.sum_jobs):
            begin(pe, job)
            pe.wait_ge(*self.sq_ready[j])
            pe.matmul(job.ap[:, :], k.c("ones"), self.e[:, 0, j * 512:(j + 1) * 512], start=True, stop=True)\
              .then_inc(job.full[0], 1)

    def scalar(self, act):
        k = self.k
        for l in range(len(H_LEVELS) - 1):
            act.wait_ge(*self.diff[l])
            act.activation(self.e[:, l % 2, :], self.e[:, l % 2, :], ACT.Exp).then_inc(self.exp[l][0], 1)
        out = k.area(M_OUT, KC, T)
        sq = self.e[:, 0, :].rearrange("p (c t) -> p c t", t=T)
        for j, job in enumerate(self.out_jobs):
            act.wait_ge(*job.full)
            act.activation(out[:, 2 * j:2 * j + 2, :], pair(job), ACT.Identity).then_inc(self.out_ready[j][0], 1)
            act.activation(sq[:, 2 * j:2 * j + 2, :], pair(job), ACT.Square).then_inc(self.sq_ready[j][0], 1)
        for j, job in enumerate(self.sum_jobs):
            act.wait_ge(*job.full)
            flat = self.e[:, 0, j * 512:(j + 1) * 512]
            act.activation(flat, job.ap[:, :], ACT.Ln, bias=k.eps[:, 0:1], scale=1.0 / P).then_inc(job.free[0], 1)
            act.wait_ge(*job.free)
            act.activation(flat, flat, ACT.Exp, scale=-0.5).then_inc(self.root[j][0], 1)

    def gpsimd(self, pool):
        pool.wait_ge(*self.src.x_ready[-1])
        pool.memset(self.att, 0.0).then_inc(self.cleared[0], 1)

    def vector(self, dve):
        k, chain = self.k, self.k.dve
        b_all = k.area(M_B, KC * T)
        q_all, k_all = k.area(M_Q, KC * T), k.area(M_K, KC * T)
        for e in self.src.q_ready:
            dve.wait_ge(*e)

        def halves(ap, b):
            return ap.rearrange("p (m s b) -> p m s b", s=2, b=b)

        def exponents(l):
            b = H_LEVELS[l]
            if l >= 2:
                dve.wait_ge(*self.jobs[l - 2][-1].full)
            e, src = halves(self.e[:, l % 2, :], b), halves(b_all, b)
            ref = src[:, :, 0, b - 1:b].broadcast_to([P, KC * T // (2 * b), b])
            dve.tensor_tensor(e[:, :, 1, :], src[:, :, 1, :], ref, ALU.subtract)
            dve.tensor_tensor(e[:, :, 0, :], ref, src[:, :, 0, :], ALU.subtract).then_inc(self.diff[l][0], 1)

        n = len(H_LEVELS)
        exponents(0)
        for l, b in enumerate(H_LEVELS):
            if l + 1 < n - 1:
                exponents(l + 1)
            if b:
                dve.wait_ge(*self.exp[l])
                e = halves(self.e[:, l % 2, :], b)
                dve.tensor_tensor(e[:, :, 1, :], e[:, :, 1, :], halves(q_all, b)[:, :, 1, :], ALU.mult)
                dve.tensor_tensor(e[:, :, 0, :], e[:, :, 0, :], halves(k_all, b)[:, :, 0, :], ALU.mult)\
                   .then_inc(self.e_ready[l][0], 1)
            else:
                dve.tensor_copy(k.note[:, 0:1], k.eps[:, 0:1]).then_inc(self.e_ready[l][0], 1)
            if l >= 1:
                self.take(dve, l - 1)
        self.take(dve, n - 1)
        out = k.area(M_OUT, KC, T)
        rs = self.e[:, 0, :].rearrange("p (c t) -> p c t", t=T)
        gain = k.v("hgrn_norm_w", 1 if self.src.layer else 0)
        for j in range(4):
            dve.wait_ge(*self.root[j])
            dve.wait_ge(*self.out_ready[j])
            o = out[:, 2 * j:2 * j + 2, :]
            chain.link(dve.scalar_tensor_tensor(o, o, gain, rs[:, 2 * j:2 * j + 2, :], ALU.mult, ALU.mult))
            dve.wait_ge(*self.src.g_ready[j])
            dve.tensor_tensor(o, o, self.src.g[:, 2 * j:2 * j + 2, :], ALU.mult).then_inc(self.ready[j][0], 1)

    def take(self, dve, l):
        k = self.k
        at = 0 if l == 0 else 2 + 4 * (l - 1)
        if l == 0:
            dve.wait_ge(*self.cleared)
        for j, job in enumerate(self.jobs[l]):
            dve.wait_ge(*job.full)
            data = job.ap[:, :].rearrange("p (h c) -> p h c", c=P)
            if l >= 2:
                dve.wait_ge(*self.taken[at + j - 4])
            if l == 0:
                ins = dve.tensor_copy(self.att[:, 4 * j:4 * j + 4, 1, :], data)
            else:
                b = H_LEVELS[l]
                mask = k.c("upper_pairs", LEVELS.index(b) * P, P) if b else k.c("ident")
                mask = mask.bitcast(U32).unsqueeze(1).broadcast_to([P, 4, P])
                h = 4 * (j // 2)
                ins = dve.copy_predicated(self.att[:, h:h + 4, 2 * (j % 2), :], mask, data)
            ins.then_inc(self.taken[at + j][0], 1)
            if l == len(H_LEVELS) - 1:
                dve.wait_ge(*self.taken[at + j])


def hgrn(layer):
    def make(k):
        src = HgrnIn(k, layer)
        att = HgrnAttention(k, src)
        ready = [att.ready[c // 2] for c in range(KC)]
        return [src, att, OutProjection(k, k.area(M_OUT, KC, T), ready, KC, ln=6 if layer else 0)]
    return make


MIXERS["hgrn0"] = hgrn(0)
MIXERS["hgrn1"] = hgrn(1)


L_PAD = M_E
L_DT = M_E
L_DEN = L_DT + 2 * 3 * P
L_EN = L_DEN + 2 * T
L_SQ = M_K
L_ROWS = M_B


class MlstmIn(Stage):

    def setup(self):
        k = self.k
        self.x_ready = k.h_ready
        self.qk, self.v, self.o = k.area(M_Q, KC, T), k.area(M_V, TT, D), k.area(M_G, KC, T)
        self.pad = k.area(L_PAD, KC, T + CONV_M - 1)
        self.rows = k.area(L_ROWS, 8, T)
        self.gate_taken = k.counter("mlstm_gate_taken").events(2)
        self.gate_jobs = [k.job(e) for e in self.gate_taken]
        self.qk_taken = k.counter("mlstm_qk_taken").events(4)
        self.v_ready = k.counter("mixer_v").events(4)
        self.o_ready = k.counter("mixer_g").events(4)
        self.jobs = [k.job(e) for e in self.qk_taken + self.v_ready + self.o_ready]
        self.edge = k.counter("mlstm_edge").event()
        self.convolved = k.counter("mlstm_conv").events(KC)
        self.qk_ready = k.counter("mlstm_qk").events(KC)
        self.log1p = k.counter("log1p_ready").event()
        self.rows_ready = k.counter("mlstm_rows").event()
        self.a_taken = k.counter("mlstm_a_columns").event()
        self.a_job = k.job(self.a_taken)

    def tensor(self, pe):
        k = self.k
        for job, name in zip(self.gate_jobs, ("mlstm_i_w", "mlstm_f_w")):
            begin(pe, job)
            w = k.v(name, 0, KC * 8).rearrange("p (k c) -> p k c", k=KC)
            for c in range(KC):
                pe.wait_ge(*self.x_ready[c])
                mm = pe.matmul(job.ap[0:8, 0:T], w[:, c, :], k.h[:, c, :], start=(c == 0), stop=(c == KC - 1))
            mm.then_inc(job.full[0], 1)
        project_columns(k, pe, k.h, self.x_ready, self.jobs[0:4])
        project_tokens(k, pe, k.h, self.jobs[4:8])
        project_columns(k, pe, k.h, self.x_ready, self.jobs[8:12])
        begin(pe, self.a_job)
        pe.wait_ge(*self.rows_ready)
        for t in range(TT):
            mm = pe.transpose(self.a_job.ap[:, t * 8:t * 8 + 8], self.rows[0:8, 1, t * P:(t + 1) * P],
                              k.c("ident", 0, 8, rows=8))
        mm.then_inc(self.a_job.full[0], 1)

    def scalar(self, act):
        k = self.k
        r = self.rows
        act.wait_ge(*self.edge)
        act.wait_ge(*self.gate_jobs[0].full)
        act.activation(r[0:8, 0, :], self.gate_jobs[0].ap[0:8, 0:T], ACT.Identity, bias=k.v("mlstm_gate_i", rows=8))\
           .then_inc(self.gate_taken[0][0], 1)
        act.wait_ge(*self.gate_jobs[1].full)
        act.activation(r[0:8, 2, :], self.gate_jobs[1].ap[0:8, 0:T], ACT.Identity, bias=k.v("mlstm_gate_f", rows=8))\
           .then_inc(self.gate_taken[1][0], 1)
        act.wait_ge(*self.gate_taken[1])
        k.act.link(act.activation(r[0:8, 3, :], r[0:8, 2, :], ACT.Abs))
        k.act.link(act.activation(r[0:8, 3, :], r[0:8, 3, :], ACT.Exp, scale=-1.0))
        act.activation(r[0:8, 3, :], r[0:8, 3, :], ACT.Ln, bias=k.eps[0:8, 2:3]).then_inc(self.log1p[0], 1)
        for j in range(4):
            act.wait_ge(*self.jobs[j].full)
            act.activation(self.pad[:, 2 * j:2 * j + 2, 3:3 + T], pair(self.jobs[j]), ACT.Identity)\
               .then_inc(self.qk_taken[j][0], 1)
        for j in range(4):
            act.wait_ge(*self.jobs[4 + j].full)
            act.activation(self.v[:, :, j * 256:(j + 1) * 256], pair(self.jobs[4 + j]), ACT.Identity)\
               .then_inc(self.v_ready[j][0], 1)
        for c in range(KC):
            act.wait_ge(*self.convolved[c])
            act.activation(self.qk[:, c, :], self.qk[:, c, :], ACT.Silu).then_inc(self.qk_ready[c][0], 1)
        for j in range(4):
            act.wait_ge(*self.jobs[8 + j].full)
            act.activation(self.o[:, 2 * j:2 * j + 2, :], pair(self.jobs[8 + j]), ACT.Sigmoid)\
               .then_inc(self.o_ready[j][0], 1)

    def vector(self, dve):
        k, chain, r = self.k, self.k.dve, self.rows
        for e in self.x_ready:
            dve.wait_ge(*e)
        dve.memset(self.pad[:, :, 0:3], 0.0).then_inc(self.edge[0], 1)
        dve.wait_ge(*self.log1p)
        chain.link(dve.tensor_scalar(r[0:8, 2, :], r[0:8, 2, :], 0.0, None, ALU.min))
        chain.link(dve.tensor_tensor(r[0:8, 2, :], r[0:8, 2, :], r[0:8, 3, :], ALU.subtract))
        chain.link(dve.tensor_tensor_scan(r[0:8, 4, :], k.c("one_row", rows=8), r[0:8, 2, :], 0.0, ALU.mult, ALU.add))
        chain.link(dve.tensor_tensor(r[0:8, 1, :], r[0:8, 0, :], r[0:8, 4, :], ALU.subtract))
        chain.link(dve.tensor_tensor_scan(r[0:8, 5, :], r[0:8, 1, :], r[0:8, 1, :], 0.0, ALU.max, ALU.max))
        dve.scalar_tensor_tensor(r[0:8, 6, :], r[0:8, 4, :], -1.0, r[0:8, 5, :], ALU.mult, ALU.subtract)\
           .then_inc(self.rows_ready[0], 1)
        for c in range(KC):
            dve.wait_ge(*self.qk_taken[c // 2])
            for j in range(CONV_M):
                w = k.v("mlstm_conv_w", j * KC + c)
                src, out = self.pad[:, c, j:j + T], self.qk[:, c, :]
                if j == 0:
                    ins = dve.tensor_scalar(out, src, w, None, ALU.mult)
                else:
                    ins = dve.scalar_tensor_tensor(out, src, w, out, ALU.mult, ALU.add)
                if j < CONV_M - 1:
                    chain.link(ins)
            ins.then_inc(self.convolved[c][0], 1)
        dve.wait_ge(*self.a_job.full)
        dve.tensor_copy(k.cols[:, 0, 0:16], self.a_job.ap[:, 0:16]).then_inc(self.a_taken[0], 1)
        dve.wait_ge(*self.a_taken)


class MlstmAttention(Stage):

    def __init__(self, core, src):
        self.src = src
        super().__init__(core)

    def setup(self):
        k = self.k
        n = HEADS
        self.att = k.area(M_ATT, HEADS, 3, P)
        self.dt = k.area(L_DT, 2, 3 * P)
        self.den, self.en = k.area(L_DEN, 2, T), k.area(L_EN, 2, T)
        self.sq = k.area(L_SQ, KC, T)
        self.out = k.area(M_OUT, KC, T)
        self.diff = k.counter("mlstm_exponents").events(n)
        self.en_ready = k.counter("mlstm_floor").events(n)
        self.exp = k.counter("mlstm_decay").events(n)
        self.s_ready = k.counter("mlstm_scores").events(n)
        self.den_ready = k.counter("mlstm_den").events(n)
        self.h_ready = k.counter("mlstm_h").events(n)
        self.row_jobs, self.score_jobs, self.nd_jobs = [], [], []
        for h in range(n + 1):
            if h < n:
                self.row_jobs.append(k.job(self.exp[h]))
                self.score_jobs.append(k.job(self.s_ready[h]))
            if h >= 1:
                self.nd_jobs.append(k.job(self.h_ready[h - 1]))
        self.sq_ready = k.counter("mixer_out_squared").events(4)
        self.sum_jobs = k.take(4)
        self.root = k.counter("mixer_root").events(4)
        self.ready = k.counter("mixer_ready").events(4)

    def tensor(self, pe):
        k, src = self.k, self.src
        pe.wait_ge(*src.a_taken)
        pe.wait_ge(*src.qk_ready[-1])
        pe.wait_ge(*src.v_ready[-1])
        for h in range(HEADS + 1):
            if h < HEADS:
                job = self.row_jobs[h]
                begin(pe, job)
                for i in range(2):
                    mm = pe.matmul(job.ap[:, i * T:(i + 1) * T], k.c("head_rows", h * P, P, rows=8),
                                   src.rows[0:8, 5 + i, :], start=True, stop=True)
                mm.then_inc(job.full[0], 1)
                job = self.score_jobs[h]
                begin(pe, job)
                rows = slice(64 * (h % 2), 64 * (h % 2) + 64)
                q, kk = src.qk[rows, h // 2, :], src.qk[rows, 4 + h // 2, :]
                pe.matmul(job.ap[:, 0:T], kk[:, 0:P], q, start=True, stop=True)
                pe.matmul(job.ap[:, T:T + P], kk[:, P:T], q[:, P:T], start=True, stop=True).then_inc(job.full[0], 1)
            if h >= 1:
                w = h - 1
                job = self.nd_jobs[w]
                begin(pe, job)
                pe.wait_ge(*self.s_ready[w])
                for i in range(2):
                    for t in range(2):
                        left = k.c("ones") if i else src.v[:, t, w * P:(w + 1) * P]
                        right = self.att[:, w, 0:2, :] if t == 0 else self.att[:, w, 2, :]
                        mm = pe.matmul(job.ap[:, i * T + t * P:(i + 1) * T], left, right, start=(t == 0), stop=(t == 1))
                mm.then_inc(job.full[0], 1)
        sq = k.area(L_SQ, KC * T)
        for j, job in enumerate(self.sum_jobs):
            begin(pe, job)
            pe.wait_ge(*self.sq_ready[j])
            pe.matmul(job.ap[:, :], k.c("ones"), sq[:, j * 512:(j + 1) * 512], start=True, stop=True)\
              .then_inc(job.full[0], 1)

    def scalar(self, act):
        k = self.k
        for h in range(HEADS + 1):
            if h < HEADS:
                act.wait_ge(*self.row_jobs[h].full)
                if h >= 2:
                    act.wait_ge(*self.h_ready[h - 2])
                act.activation(self.en[:, h % 2, :], self.row_jobs[h].ap[:, T:2 * T], ACT.Exp)\
                   .then_inc(self.en_ready[h][0], 1)
                act.wait_ge(*self.diff[h])
                act.activation(self.dt[:, h % 2, :], self.dt[:, h % 2, :], ACT.Exp, scale=-1.0)\
                   .then_inc(self.exp[h][0], 1)
            if h >= 1:
                w = h - 1
                act.wait_ge(*self.nd_jobs[w].full)
                act.activation(self.den[:, w % 2, :], self.nd_jobs[w].ap[:, T:2 * T], ACT.Abs)\
                   .then_inc(self.den_ready[w][0], 1)
        sq = k.area(L_SQ, KC * T)
        for j, job in enumerate(self.sum_jobs):
            act.wait_ge(*self.h_ready[2 * j + 1])
            act.activation(self.sq[:, 2 * j:2 * j + 2, :], self.out[:, 2 * j:2 * j + 2, :], ACT.Square)\
               .then_inc(self.sq_ready[j][0], 1)
        for j, job in enumerate(self.sum_jobs):
            act.wait_ge(*job.full)
            flat = sq[:, j * 512:(j + 1) * 512]
            act.activation(flat, job.ap[:, :], ACT.Ln, bias=k.eps[:, 0:1], scale=1.0 / P).then_inc(job.free[0], 1)
            act.wait_ge(*job.free)
            act.activation(flat, flat, ACT.Exp, scale=-0.5).then_inc(self.root[j][0], 1)

    def vector(self, dve):
        k, chain = self.k, self.k.dve
        for h in range(HEADS + 1):
            if h < HEADS:
                dve.wait_ge(*self.row_jobs[h].full)
                dve.wait_ge(*self.en_ready[h])
                if h >= 2:
                    dve.wait_ge(*self.s_ready[h - 2])
                m = self.row_jobs[h].ap
                dve.tensor_scalar(self.dt[:, h % 2, 0:T], m[:, 0:T], k.cols[:, 0, h:h + 1], 0.0,
                                  ALU.subtract, ALU.max)
                dve.tensor_scalar(self.dt[:, h % 2, T:T + P], m[:, P:T], k.cols[:, 0, 8 + h:9 + h], 0.0,
                                  ALU.subtract, ALU.max).then_inc(self.diff[h][0], 1)
            if h >= 1:
                self.divide(dve, h - 1)
            if h < HEADS:
                dve.wait_ge(*self.exp[h])
                dve.wait_ge(*self.score_jobs[h].full)
                att = self.att[:, h, :, :].rearrange("p a b -> p (a b)")
                chain.link(dve.scalar_tensor_tensor(att, self.score_jobs[h].ap[:, 0:3 * P], 0.125,
                                                    self.dt[:, h % 2, :], ALU.mult, ALU.mult))
                both = self.att[:, h, 0:3:2, :]
                dve.tensor_tensor(both, both, k.c("upto").unsqueeze(1).broadcast_to([P, 2, P]), ALU.mult)\
                   .then_inc(self.s_ready[h][0], 1)
        for j in range(4):
            dve.wait_ge(*self.root[j])
            for c in (2 * j, 2 * j + 1):
                ins = dve.scalar_tensor_tensor(self.out[:, c, :], self.out[:, c, :], k.v("mlstm_norm_w", c),
                                               self.sq[:, c, :], ALU.mult, ALU.mult)
            chain.link(ins)
            o = self.out[:, 2 * j:2 * j + 2, :]
            dve.wait_ge(*self.src.o_ready[j])
            dve.tensor_tensor(o, o, self.src.o[:, 2 * j:2 * j + 2, :], ALU.mult).then_inc(self.ready[j][0], 1)

    def divide(self, dve, h):
        k, chain = self.k, self.k.dve
        den = self.den[:, h % 2, :]
        dve.wait_ge(*self.den_ready[h])
        dve.wait_ge(*self.en_ready[h])
        chain.link(dve.tensor_tensor(den, den, self.en[:, h % 2, :], ALU.max))
        chain.link(dve.reciprocal(den, den))
        dve.tensor_tensor(self.out[:, h, :], self.nd_jobs[h].ap[:, 0:T], den, ALU.mult)\
           .then_inc(self.h_ready[h][0], 1)


def mlstm(k):
    src = MlstmIn(k)
    att = MlstmAttention(k, src)
    ready = [att.ready[c // 2] for c in range(KC)]
    return [src, att, OutProjection(k, k.area(M_OUT, KC, T), ready, KC, ln=2)]


MIXERS["mlstm"] = mlstm


S_U = M_Q
S_BC = M_V
S_PH = S_BC + 4096
S_TAB = S_PH + 4 * T
S_T1 = S_TAB + 4 * T
S_T2 = S_T1 + 2 * T
S_G = S_T2 + 2 * T
S_H = S_G + 2 * T
R_DT, R_MAG, R_TH, R_N, R_SIN, R_COS, R_CR, R_CI, R_T1, R_T2, R_T3 = range(11)


class S5In(Stage):

    def setup(self):
        k = self.k
        self.x_ready = k.h_ready
        self.u = k.area(S_U, KC, T)
        self.u_ready = k.counter("s5_u").events(4)
        self.jobs = [k.job(e) for e in self.u_ready]
        self.loaded = k.counter("s5_matrices_loaded")
        self.dt_ready = k.counter("s5_dt").event()
        self.prod_ready = k.counter("s5_products").events(2)
        self.exp_ready = k.counter("s5_exp").event()
        self.sin_ready = k.counter("s5_sin").event()
        self.ready = k.counter("s5_ready").event()

    def tensor(self, pe):
        project_columns(self.k, pe, self.k.h, self.x_ready, self.jobs)

    def scalar(self, act):
        k, c = self.k, self.k.cols
        for e in self.x_ready:
            act.wait_ge(*e)
        act.dma_start(k.area(S_BC, 4096), k.s5_bc).then_inc(self.loaded.sem, 16)
        act.activation(c[:, R_DT, :], k.v("s5_log_dt", 0, S5_TILES), ACT.Exp).then_inc(self.dt_ready[0], 1)
        act.wait_ge(*self.prod_ready[0])
        act.activation(c[:, R_MAG, :], c[:, R_MAG, :], ACT.Exp).then_inc(self.exp_ready[0], 1)
        act.wait_ge(*self.prod_ready[1])
        act.activation(c[:, R_SIN, :], c[:, R_TH, :], ACT.Sin)
        act.activation(c[:, R_COS, :], c[:, R_TH, :], ACT.Sin, scale=0.5).then_inc(self.sin_ready[0], 1)
        for j in range(4):
            act.wait_ge(*self.jobs[j].full)
            act.activation(self.u[:, 2 * j:2 * j + 2, :], pair(self.jobs[j]), ACT.Identity)\
               .then_inc(self.u_ready[j][0], 1)

    def vector(self, dve):
        k, c, link = self.k, self.k.cols, self.k.dve.link
        are, aim = k.v("s5_a_re", 0, S5_TILES), k.v("s5_a_im", 0, S5_TILES)
        mult, add, sub = ALU.mult, ALU.add, ALU.subtract

        def tt(out, a, b, op):
            link(dve.tensor_tensor(c[:, out, :], a, b, op))

        row = lambda i: c[:, i, :]
        dve.wait_ge(*self.dt_ready)
        dve.tensor_tensor(c[:, R_MAG, :], are, row(R_DT), mult).then_inc(self.prod_ready[0][0], 1)
        tt(R_TH, aim, row(R_DT), mult)
        reduce_angle(dve, link, row(R_TH), row(R_N), self.prod_ready[1])
        dve.wait_ge(*self.exp_ready)
        dve.wait_ge(*self.sin_ready)
        tt(R_COS, row(R_COS), row(R_COS), mult)
        link(dve.tensor_scalar(row(R_COS), row(R_COS), -2.0, 1.0, mult, add))
        tt(R_T1, row(R_MAG), row(R_COS), mult)
        link(dve.tensor_scalar(row(R_T1), row(R_T1), -1.0, None, add))
        tt(R_T2, row(R_MAG), row(R_SIN), mult)
        tt(R_T3, are, are, mult)
        tt(R_N, aim, aim, mult)
        tt(R_T3, row(R_T3), row(R_N), add)
        link(dve.reciprocal(row(R_T3), row(R_T3)))
        tt(R_CR, row(R_T1), are, mult)
        tt(R_N, row(R_T2), aim, mult)
        tt(R_CR, row(R_CR), row(R_N), add)
        tt(R_CR, row(R_CR), row(R_T3), mult)
        tt(R_CI, row(R_T2), are, mult)
        tt(R_N, row(R_T1), aim, mult)
        tt(R_CI, row(R_CI), row(R_N), sub)
        tt(R_CI, row(R_CI), row(R_T3), mult)
        dve.wait_ge(self.loaded.sem, 16)
        out = k.area(S_BC + 2048, 2, S5_TILES, 32)
        t1, t2 = k.area(S_PH, S5_TILES, 32), k.area(S_T1, S5_TILES, 32)
        cr = row(R_CR).unsqueeze(2).broadcast_to([P, S5_TILES, 32])
        ci = row(R_CI).unsqueeze(2).broadcast_to([P, S5_TILES, 32])
        link(dve.tensor_tensor(t1, out[:, 0, :, :], ci, mult))
        link(dve.tensor_tensor(t2, out[:, 1, :, :], ci, mult))
        link(dve.tensor_tensor(out[:, 0, :, :], out[:, 0, :, :], cr, mult))
        link(dve.tensor_tensor(out[:, 0, :, :], out[:, 0, :, :], t2, sub))
        link(dve.tensor_tensor(out[:, 1, :, :], out[:, 1, :, :], cr, mult))
        link(dve.tensor_tensor(out[:, 1, :, :], out[:, 1, :, :], t1, add))
        dve.tensor_scalar(out[:, 1, :, :], out[:, 1, :, :], -1.0, None, mult).then_inc(self.ready[0], 1)
        dve.wait_ge(*self.ready)


def reduce_angle(dve, link, x, n, last):
    link(dve.tensor_scalar(n, x, 1.0 / TWO_PI, ROUND, ALU.mult, ALU.add))
    link(dve.tensor_scalar(n, n, ROUND, None, ALU.subtract))
    for part in (PI_1, PI_2, PI_3):
        link(dve.scalar_tensor_tensor(x, n, -part, x, ALU.mult, ALU.add))
    dve.tensor_scalar(x, x, 3.1415925, -3.1415925, ALU.min, ALU.max).then_inc(last[0], 1)
    dve.wait_ge(*last)


class S5Scan(Stage):

    def __init__(self, core, src):
        self.src = src
        super().__init__(core)

    def setup(self):
        k = self.k
        n = S5_TILES
        self.phase = k.area(S_PH, 2, 2, T)
        self.table = k.area(S_TAB, 2, 2, T)
        self.t1, self.t2, self.g = (k.area(at, 2, T) for at in (S_T1, S_T2, S_G))
        self.hs = k.area(S_H, 2, 2, T)
        self.out = k.area(M_OUT, KC, T)
        self.phase_ready = k.counter("s5_phase").events(n)
        self.sin_done = k.counter("s5_table_sin").events(n)
        self.table_ready = k.counter("s5_table").events(n)
        self.bu_used = k.counter("s5_bu_used").events(n)
        self.h_ready = k.counter("s5_state").events(n)
        self.y_ready = k.counter("s5_y").events(KC)
        self.ready = k.counter("mixer_ready_act").events(KC)
        self.bu_jobs, self.y_jobs = [], []
        for i in range(n + 1):
            if i < n:
                self.bu_jobs.append(k.job(self.bu_used[i]))
            if i >= 1 and (i - 1) % 4 == 0:
                self.y_jobs.append(k.job(self.y_ready[(i - 1) // 4]))

    def tensor(self, pe):
        k = self.k
        b = k.area(S_BC, KC * 2, P)
        c = k.area(S_BC + 2048, 2, S5_TILES, 32)
        pe.wait_ge(self.src.loaded.sem, 16)
        pe.wait_ge(*self.src.ready)
        for i in range(S5_TILES + 1):
            if i < S5_TILES:
                j, r = i // 4, i % 4
                rows = slice(32 * r, 32 * r + 32)
                job = self.bu_jobs[i]
                begin(pe, job)
                pe.wait_ge(*self.src.u_ready[j // 2])
                for part in range(2):
                    mm = pe.matmul(job.ap[:, part * T:(part + 1) * T], b[rows, 2 * j + part, :], self.src.u[rows, j, :],
                                   start=True, stop=True, tile_position=(32 * r, 0))
                mm.then_inc(job.full[0], 1)
            if i >= 1:
                w = i - 1
                j, r = w // 4, w % 4
                job = self.y_jobs[j]
                if r == 0:
                    begin(pe, job)
                pe.wait_ge(*self.h_ready[w])
                for part in range(2):
                    mm = pe.matmul(job.ap[32 * r:32 * r + 32, 0:T], c[:, part, w, :], self.hs[:, w % 2, part, :],
                                   start=(part == 0), stop=(part == 1), tile_position=(0, 32 * r))
                mm.then_inc(self.y_sem(w), 1)

    def y_sem(self, w):
        return self.y_jobs[w // 4].full[0] if w % 4 == 3 else self.k.counter("s5_states_used").sem

    def states_used(self, w):
        if w % 4 == 3:
            return self.y_jobs[w // 4].full
        return (self.k.counter("s5_states_used").sem, w - w // 4 + 1)

    def scalar(self, act):
        k = self.k
        for i in range(S5_TILES):
            act.wait_ge(*self.phase_ready[i])
            if i >= 2:
                act.wait_ge(*self.h_ready[i - 2])
            act.activation(self.table[:, i % 2, 1, :], self.phase[:, i % 2, 0, :], ACT.Sin)
            act.activation(self.table[:, i % 2, 0, :], self.phase[:, i % 2, 0, :], ACT.Sin, scale=0.5)\
               .then_inc(self.sin_done[i][0], 1)
            act.wait_ge(*self.sin_done[i])
            k.act.link(act.activation(self.table[:, i % 2, 0, :], self.table[:, i % 2, 0, :], ACT.Square))
            act.activation(self.table[:, i % 2, 0, :], self.table[:, i % 2, 0, :], ACT.Identity,
                           bias=k.eps[:, 2:3], scale=-2.0).then_inc(self.table_ready[i][0], 1)
        for c in range(KC):
            act.wait_ge(*self.y_ready[c])
            act.activation(self.out[:, c, :], self.out[:, c, :], ACT.Gelu_apprx_tanh).then_inc(self.ready[c][0], 1)

    def vector(self, dve):
        k, link = self.k, self.k.dve.link

        def phase(i):
            if i >= 2:
                dve.wait_ge(*self.sin_done[i - 2])
            x, n = self.phase[:, i % 2, 0, :], self.phase[:, i % 2, 1, :]
            link(dve.tensor_scalar(x, k.c("time"), k.cols[:, R_TH, i:i + 1], None, ALU.mult))
            reduce_angle(dve, link, x, n, self.phase_ready[i])

        phase(0)
        for i in range(S5_TILES):
            if i + 1 < S5_TILES:
                phase(i + 1)
            dve.wait_ge(*self.table_ready[i])
            job = self.bu_jobs[i]
            dve.wait_ge(*job.full)
            cos = over_chunks(self.table[:, i % 2, 0, :], 2)
            sin = over_chunks(self.table[:, i % 2, 1, :], 2)
            dve.tensor_tensor(self.t1, pair(job), cos, ALU.mult)
            dve.tensor_tensor(self.t2, pair(job), sin, ALU.mult).then_inc(self.bu_used[i][0], 1)
            dve.wait_ge(*self.bu_used[i])
            dve.tensor_tensor(self.g[:, 0, :], self.t1[:, 0, :], self.t2[:, 1, :], ALU.add)
            link(dve.tensor_tensor(self.g[:, 1, :], self.t1[:, 1, :], self.t2[:, 0, :], ALU.subtract))
            mag = k.cols[:, R_MAG, i:i + 1].broadcast_to([P, T])
            h = self.hs[:, i % 2, :, :]
            if i >= 2:
                dve.wait_ge(*self.states_used(i - 2))
            dve.tensor_tensor_scan(h[:, 0, :], mag, self.g[:, 0, :], 0.0, ALU.mult, ALU.add)
            link(dve.tensor_tensor_scan(h[:, 1, :], mag, self.g[:, 1, :], 0.0, ALU.mult, ALU.add))
            dve.tensor_tensor(self.t1, h, cos, ALU.mult)
            link(dve.tensor_tensor(self.t2, h, sin, ALU.mult))
            dve.tensor_tensor(h[:, 0, :], self.t1[:, 0, :], self.t2[:, 1, :], ALU.subtract)
            dve.tensor_tensor(h[:, 1, :], self.t1[:, 1, :], self.t2[:, 0, :], ALU.add).then_inc(self.h_ready[i][0], 1)
            dve.wait_ge(*self.h_ready[i])
            if i % 4 == 1 and i > 4:
                self.finish(dve, i // 4 - 1)
        self.finish(dve, KC - 1)

    def finish(self, dve, c):
        dve.wait_ge(*self.y_jobs[c].full)
        dve.scalar_tensor_tensor(self.out[:, c, :], self.src.u[:, c, :], self.k.v("s5_d", c),
                                 self.y_jobs[c].ap[:, 0:T], ALU.mult, ALU.add).then_inc(self.y_ready[c][0], 1)


def s5(k):
    src = S5In(k)
    scan = S5Scan(k, src)
    return [src, scan, OutProjection(k, k.area(M_OUT, KC, T), scan.ready, KC, ln=4, glu=True)]


MIXERS["s5"] = s5




def parts(k, which):
    out = [Start(k)]
    a = k.area(AT_A, KC, T)
    for name in which:
        if name == "mod0" or name == "mod1":
            out.append(Modulation(k, int(name[-1])))
        elif name.startswith("ffn_rms"):
            pre = PreNorm(k, k.h[:, :, :], k.h_ready, a, k.coef[:, 3, :], k.mod[:, 3 * KC:4 * KC, 0])
            out += [pre] + feed_forward(k, a, pre.ready, rms_gain=k.coef[:, 4, :])
        elif name.startswith("ffn_ln"):
            out += feed_forward(k, k.h, k.h_ready, ln=2 * int(name[-1]) + 1)
        else:
            out += MIXERS[name](k)
    return out


def program(nc, stream, vec, const, x, ctx_x, s5_bc, out, which):
    n_slabs = stream.shape[0]
    with ExitStack() as ctx:
        k = Core(nc, ctx, vec, const)
        k.eps = ctx.enter_context(nc.sbuf_tensor("epsilons", [P, 4], F32))
        k.note = ctx.enter_context(nc.sbuf_tensor("note", [P, 2], F32))
        k.ctx_x, k.s5_bc = ctx_x, s5_bc
        stages = parts(k, which)
        stored = k.sem("stored")
        eps_ready = k.sem("eps_ready")
        block = ctx.enter_context(nc.Block())

        @block.sync
        def _(sp):
            sp.dma_start(k.const[:, :], const).then_inc(k.consts_loaded, 16)
            sp.dma_start(k.vec[:, :], vec).then_inc(k.consts_loaded, 16)
            sp.dma_start(k.h[:, :, :], x).then_inc(k.consts_loaded, 16)
            sp.dma_start(k.area(H_END, KC, T), ctx_x).then_inc(k.consts_loaded, 16)
            for n in range(n_slabs):
                if n >= RING:
                    sp.wait_ge(k.used, n - RING + 1)
                sp.dma_start(k.ring[:, n % RING, :], stream[n]).then_inc(k.loaded[n % RING], 16)
            for event in k.h_ready:
                sp.wait_ge(*event)
            sp.dma_start(out, k.h[:, :, :]).then_inc(stored, 16)
            sp.wait_ge(stored, 16)

        @block.tensor
        def _(pe):
            for stage in stages:
                stage.tensor(pe)
            assert k.weights.at == n_slabs, (k.weights.at, n_slabs)

        @block.scalar
        def _(act):
            k.act = Chain(act, k.act_chain)
            act.wait_ge(eps_ready, 3)
            for stage in stages:
                stage.scalar(act)

        @block.vector
        def _(dve):
            k.dve = Chain(dve, k.dve_chain)
            dve.memset(k.eps[:, 0:1], EPS).then_inc(eps_ready, 1)
            dve.memset(k.eps[:, 1:2], LN_EPS).then_inc(eps_ready, 1)
            dve.memset(k.eps[:, 2:3], 1.0).then_inc(eps_ready, 1)
            for stage in stages:
                stage.vector(dve)

        @block.gpsimd
        def _(pool):
            k.pool = Chain(pool, k.pool_chain)
            for stage in stages:
                stage.gpsimd(pool)


ORDER = ["mod0", "hybrid", "ffn_rms0", "mod1", "conformer", "ffn_rms1",
         "hgrn0", "ffn_ln0", "mlstm", "ffn_ln1", "s5", "ffn_ln2", "hgrn1", "ffn_ln3"]


def by_columns(w):
    n = w.shape[1]
    return w.reshape(KC, P, n // 256, 256).transpose(2, 1, 0, 3).reshape(n // 256, P, SLAB)


def by_tiles(w):
    rows = w.shape[0] // P
    tiles = w.reshape(rows, P, KC, P).transpose(2, 0, 1, 3).reshape(-1, SLAB_TILES, P, P)
    return tiles.transpose(0, 2, 1, 3).reshape(-1, P, SLAB)


def halves_paired(w):
    n = w.shape[1] // 2
    return w.reshape(w.shape[0], 2, n // P, P).transpose(0, 2, 1, 3).reshape(w.shape[0], 2 * n)


def hyb_columns():
    q = 2064 + np.concatenate([np.r_[j * 64:(j + 1) * 64, (j + 4) * 64:(j + 5) * 64] for j in range(4)])
    return np.r_[0:2048, q, 2576:2832]


def hyb_out_rows():
    return np.r_[0:512, 512 + (hyb_columns()[2048:2560] - 2064)]


def slabs(name, i):
    out = {
        "mod0": lambda: [by_columns(i["w_mod"][0])],
        "mod1": lambda: [by_columns(i["w_mod"][1])],
        "hybrid": lambda: [by_columns(i["hyb_w_in"][0][:, hyb_columns()]),
                           by_columns(i["hyb_w_out"][0][hyb_out_rows()])],
        "conformer": lambda: [by_columns(halves_paired(i["conf_w_in"][0])), by_columns(i["conf_w_out"][0])],
        "mlstm": lambda: [by_columns(i["mlstm_w_in_2"][0][:, :3072]), by_columns(i["mlstm_w_out_2"][0])],
        "s5": lambda: [by_columns(i["s5_w_in_2"][0]), by_columns(halves_paired(i["s5_w_out_2"][0]))],
    }
    for j in range(2):
        out[f"ffn_rms{j}"] = lambda j=j: [by_columns(halves_paired(i["w_ffn_in"][j])), by_tiles(i["w_ffn_out"][j])]
        out[f"hgrn{j}"] = lambda j=j: [by_columns(i["hgrn_w_in_2"][j]), by_columns(i["hgrn_w_out_2"][j])]
    for j in range(4):
        out[f"ffn_ln{j}"] = lambda j=j: [by_columns(halves_paired(i["ffn_w_gate_up_2"][j])),
                                         by_tiles(i["ffn_w_down_2"][j])]
    return out[name]()


def pack_vectors(i):
    def chunks(a):
        return np.asarray(a).reshape(-1, P).T

    def rows(a):
        a = np.asarray(a).reshape(-1)
        return np.pad(a, (0, P - len(a)))[:, None]

    def small(w):
        return np.asarray(w).reshape(KC, P, 8).transpose(1, 0, 2).reshape(P, KC * 8)

    def states(a):
        return np.asarray(a).reshape(S5_TILES, P).T

    v = {n: chunks(i[n]) for n in ("c", "c_ctx", "b_mod", "g_mix_pre", "g_mix_post", "g_ffn_pre", "g_ffn_post",
                                   "hyb_conv_w", "hyb_out_norm", "conf_b_in", "conf_dw_w", "conf_dw_b",
                                   "conf_ln_g", "conf_ln_b", "conf_b_out")}
    v["hyb_q_norm"] = chunks(np.tile(i["hyb_q_norm"][0], 2))
    v["hyb_k_norm"] = chunks(np.tile(i["hyb_k_norm"][0], 2))
    v["hyb_a_log"], v["hyb_dt_bias"] = rows(i["hyb_a_log"]), rows(i["hyb_dt_bias"])
    v["hyb_beta_w"], v["hyb_g_w"] = small(i["hyb_w_in"][0][:, 2048:2056]), small(i["hyb_w_in"][0][:, 2056:2064])
    v["hgrn_norm_w"] = chunks(i["hgrn_norm_w_2"])
    v["lb_logits"] = chunks(i["hgrn_lb_logits_2"])
    v["mlstm_conv_w"] = chunks(i["mlstm_conv_w_2"])
    v["mlstm_gate_i"], v["mlstm_gate_f"] = rows(i["mlstm_gate_b_2"][0, :8]), rows(i["mlstm_gate_b_2"][0, 8:])
    v["mlstm_norm_w"] = chunks(i["mlstm_norm_w_2"])
    v["mlstm_i_w"], v["mlstm_f_w"] = (small(i["mlstm_w_in_2"][0][:, 3072 + 8 * j:3080 + 8 * j]) for j in range(2))
    v["s5_a_re"], v["s5_a_im"] = states(i["s5_a_re_2"]), states(i["s5_a_im_2"])
    v["s5_log_dt"] = states(np.repeat(i["s5_log_dt_2"].reshape(-1), S5_STATE))
    v["s5_d"] = chunks(i["s5_d_2"])
    v["ln_g"], v["ln_b"] = chunks(i["ln_g_2"]), chunks(i["ln_b_2"])
    for name, n in VECTORS:
        assert v[name].shape == (P, n), (name, v[name].shape)
    return np.ascontiguousarray(np.concatenate([v[n] for n, _ in VECTORS], 1))


def pack_s5(i):
    b = np.zeros((P, KC, 2, P), np.float32)
    c = np.zeros((P, 2, S5_TILES, 32), np.float32)
    for part, (wb, wc) in enumerate(((i["s5_b_re_2"][0], i["s5_c_re_2"][0]), (i["s5_b_im_2"][0], i["s5_c_im_2"][0]))):
        for g in range(GROUPS):
            chunk, row = g // 8, (g % 8) * S5_CH
            half = g % 2
            b[row:row + S5_CH, chunk, part, half * 64:half * 64 + 64] = wb[g].T
            c[half * 64:half * 64 + 64, part, g // 2, half * S5_CH:(half + 1) * S5_CH] = wc[g].T
    return np.concatenate([b.reshape(P, -1), c.reshape(P, -1)], 1)


def pack_constants():
    t = np.arange(P)
    c = {"ident": np.eye(P), "mean": np.full((P, P), 1.0 / D), "ones": np.ones((P, P)),
         "ones64": np.kron(np.eye(2), np.ones((64, 64))),
         "upto": t[:, None] <= t[None, :], "from_": t[:, None] >= t[None, :]}
    turn = np.zeros((P, P))
    for base in range(0, P, 32):
        for j in range(16):
            turn[base + 16 + j, base + j] = -1.0
            turn[base + j, base + 16 + j] = 1.0
    c["rope_turn"] = turn
    pairs = []
    for b in LEVELS:
        same = t[:, None] // (2 * b) == t[None, :] // (2 * b)
        pairs.append(same & ((t[:, None] // b) % 2 == 1) & ((t[None, :] // b) % 2 == 0))
    c["lower_pairs"] = np.concatenate(pairs, 1)
    c["upper_pairs"] = np.concatenate([m.T for m in pairs], 1)
    n = np.arange(T)
    freq = 10000.0 ** (-np.arange(16) / 16.0)
    angle = np.concatenate([freq[:, None] * (n // 64), freq[:, None] * (n // 64),
                            freq[:, None] * (n % 64), freq[:, None] * (n % 64)], 0)
    c["cos"], c["sin"] = np.tile(np.cos(angle), (2, 1)), np.tile(np.sin(angle), (2, 1))
    sel = np.zeros((P, HEADS, P))
    for h in range(HEADS):
        sel[h, h, :] = 1.0
    c["head_rows"] = sel.reshape(P, -1)
    c["one_row"] = np.ones((P, T))
    c["time"] = np.tile(np.arange(T), (P, 1))
    for name, size in CONSTANTS:
        assert c[name].shape == (P, size), name
    return np.ascontiguousarray(np.concatenate([c[n] for n, _ in CONSTANTS], 1).astype(np.float32))


def feature_major(a):
    return np.ascontiguousarray(np.asarray(a).reshape(T, KC, P).transpose(2, 1, 0))


def launch_arrays(inputs, which):
    i = {n: np.asarray(a) for n, a in inputs.items()}
    stream = np.concatenate([s for name in which for s in slabs(name, i)], 0)
    return {"stream": stream, "vectors": pack_vectors(i), "constants": pack_constants(),
            "x": feature_major(i["x"][0]), "ctx": feature_major(i["ctx"][0]), "s5_bc": pack_s5(i)}


def build(nc, arrays, which):
    aps = {n: nc.dram_tensor(f"{n}_dram", a.shape, mybir.dt.from_np(a.dtype), kind="ExternalInput").ap()
           for n, a in arrays.items()}
    out = nc.dram_tensor("out_dram", (P, KC, T), F32, kind="ExternalOutput").ap()
    program(nc, aps["stream"], aps["vectors"], aps["constants"], aps["x"], aps["ctx"], aps["s5_bc"], out, which)


def kernel(**inputs):
    import concourse.bacc as _bacc
    from concourse.bass_utils import run_bass_kernel_spmd as _run

    arrays = launch_arrays(inputs, ORDER)
    nc = _bacc.Bacc("TRN2", target_bir_lowering=False, num_devices=1)
    build(nc, arrays, ORDER)
    r = _run(nc, [{f"{n}_dram": a for n, a in arrays.items()}], core_ids=[0])
    got = r.results[0]["out_dram"]
    return np.ascontiguousarray(got.transpose(2, 1, 0).reshape(1, T, D))
```

```python
from contextlib import ExitStack

import numpy as np

import concourse.bass as bass
from concourse import mybir

F32 = mybir.dt.float32
F32R = mybir.dt.float32r
U32 = mybir.dt.uint32
ALU = mybir.AluOpType
ACT = mybir.ActivationFunctionType
AXX = mybir.AxisListType.X

P = 128
D = 1024
KC = D // P
T = 256
TT = T // P
FFN = 2816
FC = FFN // P
COND = 6 * D // P
SLAB = 2048
SLAB_TILES = SLAB // P
RING = 5
SPLITS = 2
BANK = 512
BANKS = 7
MOD_FIRST = 8
MOD_EARLY = 8
A_HEADS = 4
B_PAIRS = 4
DIRS = 2
DH = DIRS * A_HEADS
CONV_A = 5
CONV_C = 31
PAD_C = CONV_C // 2
CONV_M = 4
HEADS = 8
GROUPS = 64
S5_CH = 16
S5_STATE = 64
S5_TILES = GROUPS * S5_STATE // P
EPS = 1e-6
LN_EPS = 1e-5
ALPHA = 8.0 ** 0.25
LEVELS = [1, 2, 4, 8, 16, 32, 64]
TWO_PI = 6.283185307179586
TURN = 6.283185
PI_1 = 6.28125
PI_2 = 0.0019350051879882812
PI_3 = 3.019916050561733e-07
ROUND = 12582912.0

VECTORS = [
    ("c", KC), ("c_ctx", KC), ("b_mod", 2 * COND),
    ("g_mix_pre", 2 * KC), ("g_mix_post", 2 * KC), ("g_ffn_pre", 2 * KC), ("g_ffn_post", 2 * KC),
    ("hyb_conv_w", CONV_A * 12), ("hyb_out_norm", 1), ("hyb_q_norm", 1), ("hyb_k_norm", 1),
    ("hyb_a_log", 1), ("hyb_dt_bias", 1), ("hyb_beta_w", KC * 8), ("hyb_g_w", KC * 8),
    ("conf_b_in", 2 * KC), ("conf_dw_w", CONV_C * KC), ("conf_dw_b", KC),
    ("conf_ln_g", KC), ("conf_ln_b", KC), ("conf_b_out", KC),
    ("hgrn_norm_w", 2), ("lb_logits", 4 * KC),
    ("mlstm_conv_w", CONV_M * KC), ("mlstm_gate_i", 1), ("mlstm_gate_f", 1), ("mlstm_norm_w", KC),
    ("mlstm_i_w", KC * 8), ("mlstm_f_w", KC * 8),
    ("s5_a_re", S5_TILES), ("s5_a_im", S5_TILES), ("s5_log_dt", S5_TILES), ("s5_d", KC),
    ("ln_g", 8 * KC), ("ln_b", 8 * KC),
]
CONSTANTS = [
    ("ident", P), ("mean", P), ("ones", P), ("ones64", P), ("rope_turn", P),
    ("upto", P), ("from_", P), ("lower_pairs", len(LEVELS) * P), ("upper_pairs", len(LEVELS) * P),
    ("cos", T), ("sin", T), ("head_rows", HEADS * P), ("one_row", T),
    ("time", T),
]


def columns_of(table):
    at, out = 0, {}
    for name, n in table:
        out[name] = (at, n)
        at += n
    return out, at


VEC_AT, VEC_N = columns_of(VECTORS)
CONST_AT, CONST_N = columns_of(CONSTANTS)


class Signal:

    def __init__(self, sem):
        self.sem, self.count = sem, 0

    def events(self, n):
        first = self.count + 1
        self.count += n
        return [(self.sem, first + i) for i in range(n)]

    def event(self):
        return self.events(1)[0]


class Chain:

    def __init__(self, eng, sem):
        self.eng, self.sem, self.count = eng, sem, 0

    def link(self, ins):
        self.count += 1
        ins.then_inc(self.sem, 1)
        self.eng.wait_ge(self.sem, self.count)

    def step(self, ins, behind):
        self.count += 1
        ins.then_inc(self.sem, 1)
        if self.count > behind:
            self.eng.wait_ge(self.sem, self.count - behind)


class Job:

    def __init__(self, ap, before, full, free):
        self.ap, self.before, self.full, self.free = ap, before, full, free


class Weights:

    def __init__(self, ring, parts, loaded, used, rounded, split):
        self.ring, self.parts, self.loaded, self.used = ring, parts, loaded, used
        self.rounded, self.split_done = rounded, split
        self.at, self.release = 0, False
        self.split_slabs = []
        self.count = 0
        self.rounded_to = self.split_to = 0

    def reserve(self, n, split):
        first = self.count
        if split:
            self.split_slabs += range(first, first + n)
        self.count += n
        return first

    def next(self, pe):
        i = self.at
        self.release = i > 0
        self.at += 1
        if i in self.split_slabs:
            s = self.split_slabs.index(i)
            pe.wait_ge(self.split_done, s + 1)
            return self.parts[:, s % SPLITS, 0, :], self.parts[:, s % SPLITS, 1, :]
        pe.wait_ge(self.loaded[i % RING], 16 * (i // RING + 1))
        return self.ring[:, i % RING, :],

    def free(self, i):
        if i in self.split_slabs:
            return self.split_done, self.split_slabs.index(i) + 1
        return self.used, i + 1

    def round_through(self, act, last):
        while self.rounded_to < len(self.split_slabs) and self.split_slabs[self.rounded_to] <= last:
            s = self.rounded_to
            i = self.split_slabs[s]
            act.wait_ge(self.loaded[i % RING], 16 * (i // RING + 1))
            if s >= SPLITS:
                act.wait_ge(self.used, self.split_slabs[s - SPLITS] + 1)
            for half in range(2):
                cols = slice(half * SLAB // 2, (half + 1) * SLAB // 2)
                act.activation(self.parts[:, s % SPLITS, 0, cols], self.ring[:, i % RING, cols], ACT.Identity)\
                   .then_inc(self.rounded, 1)
            self.rounded_to += 1

    def split_through(self, dve, last):
        while self.split_to < len(self.split_slabs) and self.split_slabs[self.split_to] <= last:
            s = self.split_to
            i = self.split_slabs[s]
            for half in range(2):
                cols = slice(half * SLAB // 2, (half + 1) * SLAB // 2)
                dve.wait_ge(self.rounded, 2 * s + half + 1)
                ins = dve.tensor_tensor(self.parts[:, s % SPLITS, 1, cols], self.ring[:, i % RING, cols],
                                        self.parts[:, s % SPLITS, 0, cols].bitcast(F32), ALU.subtract)
            ins.then_inc(self.split_done, 1)
            self.split_to += 1

    def matmul(self, pe, *args, **kw):
        mm = pe.matmul(*args, **kw)
        if self.release:
            mm.then_inc(self.used, 1)
            self.release = False
        return mm

    def product(self, pe, out, w, x, start, stop):
        terms = [(w[0], x[0])] if len(w) == 1 else [(w[0], x[0]), (w[0], x[1]), (w[1], x[0])]
        for i, (a, b) in enumerate(terms):
            mm = self.matmul(pe, out, a, b, start=start and i == 0, stop=stop and i == len(terms) - 1)
        return mm


class Core:

    def __init__(self, nc, ctx, vec_dram, const_dram):
        self.nc = nc

        def sb(name, shape, dt=F32):
            return ctx.enter_context(nc.sbuf_tensor(name, shape, dt))

        def sem(name):
            return ctx.enter_context(nc.semaphore(name))

        self.ring = sb("weight_ring", [P, RING, SLAB])
        weight_parts = sb("weight_parts", [P, SPLITS, 2, SLAB], F32R)
        self.vec = sb("vectors", [P, VEC_N])
        self.const = sb("constants", [P, CONST_N])
        self.h = sb("residual", [P, KC, T])
        self.mods = [sb(f"modulation{i}", [P, COND, 2]) for i in range(2)]
        self.coefs = [sb(f"modulation_gains{i}", [P, 5, KC]) for i in range(2)]
        self.row_parts = sb("modulation_rows", [2, 2, 256])
        self.background = None
        self.silu_c = sb("silu_cond", [P, KC, 2])
        self.work_n = 25600
        with nc.sbuf_tensor("work", [P, self.work_n], F32) as work:
            self.work = work
        self.x_parts = sb("input_parts", [P, 2, KC, T], F32R)
        sb("work_middle", [P, AT_PARTS - 2 * KC * T])
        self.hid_parts = sb("hidden_parts", [P, 2, FC, T], F32R)
        sb("work_rest", [P, self.work_n - AT_PARTS - 2 * FC * T])
        self.cols = sb("columns", [P, 12, 32])
        self.psum = ctx.enter_context(nc.psum_tensor("psum", [P, BANKS + 1, BANK], F32))
        self.mod_bank = self.psum[:, BANKS, :]
        self.loaded = [sem(f"slab_loaded{i}") for i in range(RING)]
        self.used = sem("slab_used")
        self.consts_loaded = sem("consts_loaded")
        self.act_chain = sem("act_chain")
        self.dve_chain = sem("dve_chain")
        self.pool_chain = sem("pool_chain")
        self.bank_full = [Signal(sem(f"bank{i}_full")) for i in range(BANKS)]
        self.bank_free = [Signal(sem(f"bank{i}_free")) for i in range(BANKS)]
        self.last_free = [None] * BANKS
        self.jobs = 0
        self.counters = {}
        self.sem = sem
        self.weights = Weights(self.ring, weight_parts, self.loaded, self.used, sem("slab_rounded"),
                               sem("slab_split"))
        self.vec_dram, self.const_dram = vec_dram, const_dram
        self.root_free = None
        self.h_ready = None

    def counter(self, name):
        if name not in self.counters:
            self.counters[name] = Signal(self.sem(name))
        return self.counters[name]

    def job(self, free=None):
        b = self.jobs % BANKS
        self.jobs += 1
        job = Job(self.psum[:, b, :], self.last_free[b], self.bank_full[b].event(),
                  free or self.bank_free[b].event())
        self.last_free[b] = job.free
        return job

    def take(self, n):
        return [self.job() for _ in range(n)]

    def v(self, name, i=0, n=1, rows=P):
        at = VEC_AT[name][0] + i
        return self.vec[0:rows, at:at + n]

    def c(self, name, i=0, n=None, rows=P):
        at, size = CONST_AT[name]
        n = size if n is None else n
        return self.const[0:rows, at + i:at + i + n]

    def area(self, at, *shape):
        n = 1
        for s in shape:
            n *= s
        assert at + n <= self.work_n, (at, shape)
        flat = self.work[:, at:at + n]
        if len(shape) == 1:
            return flat
        if len(shape) == 2:
            return flat.rearrange("p (a b) -> p a b", b=shape[1])
        return flat.rearrange("p (a b c) -> p a b c", b=shape[1], c=shape[2])


def over_chunks(ap, n):
    return ap.unsqueeze(1).broadcast_to([ap.shape[0], n, ap.shape[1]])


def begin(eng, job):
    if job.before:
        eng.wait_ge(*job.before)


class Stage:
    def __init__(self, core):
        self.k = core
        self.setup()

    def setup(self):
        pass

    def tensor(self, pe):
        pass

    def scalar(self, act):
        pass

    def vector(self, dve):
        pass

    def gpsimd(self, pool):
        pass


AT_A = 0
AT_SQ = AT_A + KC * T
AT_Y = AT_SQ + KC * T
AT_RS = AT_Y + KC * T
AT_HID = AT_RS + 2 * T
AT_HID_NEW = AT_HID
AT_PARTS = AT_HID + 2 * T


class Start(Stage):

    def setup(self):
        self.k.h_ready = [(self.k.consts_loaded, 64)] * KC
        self.k.parts_ready = None
        self.silu_ready = self.k.counter("silu_ready").events(2)
        self.k.silu_ready = self.silu_ready[1]

    def tensor(self, pe):
        pe.wait_ge(self.k.consts_loaded, 64)

    def scalar(self, act):
        act.wait_ge(self.k.consts_loaded, 64)
        for i, name in enumerate(("c", "c_ctx")):
            act.activation(self.k.silu_c[:, :, i], self.k.v(name, 0, KC), ACT.Silu)\
               .then_inc(self.silu_ready[i][0], 1)

    def vector(self, dve):
        dve.wait_ge(self.k.consts_loaded, 64)

    def gpsimd(self, pool):
        pool.wait_ge(self.k.consts_loaded, 64)


def mod_columns(k, layer, first, n):
    at = 256 + (layer * COND + first) * 2
    return k.mod_bank[:, at:at + 2 * n]


def mod_rows(k, pe, out, slab, first, n):
    for c in range(first, first + n):
        mm = k.weights.matmul(pe, out, k.silu_c[:, c, :], slab[:, c, :], start=(c == 0), stop=(c == KC - 1))
    return mm


def mod_turn(k, pe, rows, layer, n):
    return pe.matmul(mod_columns(k, layer, n, 1), rows, k.c("ident", 0, 2, rows=2), start=True, stop=True)


def add_bias(k, dve, layer, first, n):
    bias = k.v("b_mod", layer * COND + first, n).unsqueeze(2).broadcast_to([P, n, 2])
    return dve.tensor_tensor(k.mods[layer][:, first:first + n, :],
                             mod_columns(k, layer, first, n).rearrange("p (n c) -> p n c", c=2), bias, ALU.add)


def gain(k, dve, layer, i, part, name, cond, add):
    return dve.scalar_tensor_tensor(k.coefs[layer][:, i, :], k.mods[layer][:, part * KC:(part + 1) * KC, cond], add,
                                    k.v(name, layer * KC, KC), ALU.add, ALU.mult)


def later_gains(k, dve, layer):
    gain(k, dve, layer, 2, 2, "g_mix_post", 0, 0.0)
    gain(k, dve, layer, 3, 4, "g_ffn_pre", 0, 1.0)
    return gain(k, dve, layer, 4, 5, "g_ffn_post", 0, 0.0)


class Modulation(Stage):

    def __init__(self, core, layer, slabs):
        self.layer, self.slabs = layer, slabs
        super().__init__(core)

    def setup(self):
        k = self.k
        self.taken = k.counter("modulation_row").events(self.slabs // 2)
        self.jobs = [k.job(e) for e in self.taken]
        k.weights.reserve(self.slabs, False)
        self.rows = k.area(AT_HID, self.slabs * 256)
        self.turned = k.counter("modulation_turned").event()
        self.biased = k.counter("modulation_biased").event()
        self.ready = k.counter("modulation_ready").event()
        k.mod_bank_free = self.biased

    def tensor(self, pe):
        k = self.k
        pe.wait_ge(*k.silu_ready)

        def turn(j):
            pe.wait_ge(*self.taken[j])
            for n in range(4 * j, 4 * j + 4):
                mm = mod_turn(k, pe, self.rows[0:2, n * P:(n + 1) * P], self.layer, n)
            return mm

        for j, job in enumerate(self.jobs):
            begin(pe, job)
            for half in range(2):
                slab = k.weights.next(pe)[0].rearrange("p (k c) -> p k c", k=KC)
                mm = mod_rows(k, pe, job.ap[0:2, half * 256:(half + 1) * 256], slab, 0, KC)
            mm.then_inc(job.full[0], 1)
            if j:
                turn(j - 1)
        turn(len(self.jobs) - 1).then_inc(self.turned[0], 1)

    def scalar(self, act):
        for j, job in enumerate(self.jobs):
            act.wait_ge(*job.full)
            act.activation(self.rows[0:2, j * BANK:(j + 1) * BANK], job.ap[0:2, :], ACT.Identity)\
               .then_inc(self.taken[j][0], 1)

    def vector(self, dve):
        k = self.k
        dve.wait_ge(*self.turned)
        add_bias(k, dve, self.layer, 0, 2 * self.slabs).then_inc(self.biased[0], 1)
        dve.wait_ge(*self.biased)
        if self.slabs == COND // 2:
            later_gains(k, dve, self.layer)
        gain(k, dve, self.layer, 0, 1, "g_mix_pre", 0, 1.0)
        gain(k, dve, self.layer, 1, 1, "g_mix_pre", 1, 1.0).then_inc(self.ready[0], 1)
        dve.wait_ge(*self.ready)


class BackgroundModulation:

    def __init__(self, core):
        self.k = core
        self.work = [(0, n) for n in range(MOD_FIRST, COND // 2)] + [(1, n) for n in range(COND // 2)]
        self.full = core.counter("background_row").events(len(self.work))
        self.taken = core.counter("background_row_taken").events(len(self.work))
        self.done = core.counter("modulation_turned").event()
        self.biased = core.counter("modulation_biased").events(2)
        self.ready = core.counter("modulation_ready").event()
        self.bank_free = core.mod_bank_free
        self.at = self.act_at = 0
        core.background = self

    def turn(self, pe, i):
        layer, n = self.work[i]
        pe.wait_ge(*self.taken[i])
        for c in range(2):
            mm = mod_turn(self.k, pe, self.k.row_parts[0:2, i % 2, c * P:(c + 1) * P], layer, 2 * n + c)
        return mm

    def fill(self, pe, pieces, last=None):
        k = self.k
        last = len(self.work) if last is None else last
        while pieces and self.at < 2 * last:
            i, half = divmod(self.at, 2)
            if half == 0:
                if i == 0:
                    pe.wait_ge(*self.bank_free)
                else:
                    self.turn(pe, i - 1)
                self.slab = k.weights.next(pe)[0].rearrange("p (k c) -> p k c", k=KC)
            mm = mod_rows(k, pe, k.mod_bank[0:2, 0:256], self.slab, half * KC // 2, KC // 2)
            if half:
                mm.then_inc(self.full[i][0], 1)
            self.at += 1
            pieces -= 1

    def finish(self, pe):
        self.fill(pe, 2 * len(self.work))
        self.turn(pe, len(self.work) - 1).then_inc(self.done[0], 1)

    def take(self, act, pieces, last=None):
        end = min(self.act_at + pieces, 2 * (len(self.work) if last is None else last))
        for i in range(self.act_at // 2, end // 2):
            act.wait_ge(*self.full[i])
            act.activation(self.k.row_parts[0:2, i % 2, :], self.k.mod_bank[0:2, 0:256], ACT.Identity)\
               .then_inc(self.taken[i][0], 1)
        self.act_at = max(self.act_at, end)

    def vector(self, dve):
        k = self.k
        dve.wait_ge(*self.done)
        add_bias(k, dve, 0, 2 * MOD_FIRST, COND - 2 * MOD_FIRST).then_inc(self.biased[0][0], 1)
        add_bias(k, dve, 1, 0, COND).then_inc(self.biased[1][0], 1)
        dve.wait_ge(*self.biased[1])
        later_gains(k, dve, 0)
        gain(k, dve, 1, 0, 1, "g_mix_pre", 0, 1.0)
        later_gains(k, dve, 1).then_inc(self.ready[0], 1)
        dve.wait_ge(*self.ready)


def root_inverse(act, chain, out, sums, eps, free=None):
    ins = act.activation(out, sums, ACT.Ln, bias=eps)
    if free is None:
        chain.link(ins)
    else:
        ins.then_inc(free[0], 1)
        act.wait_ge(*free)
    return act.activation(out, out, ACT.Exp, scale=-0.5)


def round_normed(act, hi, x, gain, shift, hi_ready):
    for c in range(KC):
        act.activation(hi[:, c, :], x[:, c, :], ACT.Identity, scale=gain[:, c:c + 1], bias=shift[:, c:c + 1])\
           .then_inc(hi_ready[c][0], 1)


def split_normed(k, dve, out, parts, x, gain, shift, hi_ready, ready, out_ready=None):
    out_ready = out_ready or k.counter("normed_whole").events(KC)
    for c in range(KC):
        dve.tensor_scalar(out[:, c, :], x[:, c, :], gain[:, c:c + 1], shift[:, c:c + 1], ALU.mult, ALU.add)\
           .then_inc(out_ready[c][0], 1)
    for c in range(KC):
        dve.wait_ge(*out_ready[c])
        dve.wait_ge(*hi_ready[c])
        dve.tensor_tensor(parts[1][:, c, :], out[:, c, :], parts[0][:, c, :].bitcast(F32), ALU.subtract)\
           .then_inc(ready[c][0], 1)
    dve.wait_ge(*ready[-1])


class PreNorm(Stage):

    def __init__(self, core, x, x_ready, out, gain, shift, split=False, sq_at=AT_SQ):
        self.x, self.x_ready, self.out, self.gain, self.shift = x, x_ready, out, gain, shift
        self.split, self.sq_at = split, sq_at
        super().__init__(core)

    def setup(self):
        k = self.k
        self.sq = k.area(self.sq_at, KC, T)
        self.rs = k.area(AT_RS, T)
        self.squared = k.counter("squared").events(KC)
        self.job = k.job()
        self.root = k.counter("root_ready").event()
        self.next_slab = k.weights.count
        if self.split:
            self.hi_ready = k.counter("input_rounded").events(KC)
            self.scaled = k.counter("norm_scaled").event()
            self.parts = k.x_parts[:, 0], k.x_parts[:, 1]
        self.ready = k.counter("normed_ready").events(KC)
        self.root_free, k.root_free = k.root_free, self.ready[-1]

    def scalar(self, act):
        for c in range(KC):
            act.wait_ge(*self.x_ready[c])
            act.activation(self.sq[:, c, :], self.x[:, c, :], ACT.Square).then_inc(self.squared[c][0], 1)
        act.wait_ge(*self.job.full)
        if self.root_free:
            act.wait_ge(*self.root_free)
        root_inverse(act, self.k.act, self.rs, self.job.ap[:, 0:T], self.k.eps[:, 0:1], self.job.free)\
            .then_inc(self.root[0], 1)
        self.k.weights.round_through(act, self.next_slab)
        if self.split:
            act.wait_ge(*self.scaled)
            round_normed(act, self.parts[0], self.out, self.gain, self.shift, self.hi_ready)

    def tensor(self, pe):
        begin(pe, self.job)
        for c in range(KC):
            pe.wait_ge(*self.squared[c])
            mm = pe.matmul(self.job.ap[:, 0:T], self.k.c("mean"), self.sq[:, c, :],
                           start=(c == 0), stop=(c == KC - 1))
        mm.then_inc(self.job.full[0], 1)

    def vector(self, dve):
        k = self.k
        dve.wait_ge(*self.root)
        if self.split:
            dve.tensor_tensor(self.out, self.x, over_chunks(self.rs, KC), ALU.mult).then_inc(self.scaled[0], 1)
            dve.wait_ge(*self.scaled)
            split_normed(k, dve, k.area(AT_PARTS, KC, T), self.parts, self.out, self.gain, self.shift, self.hi_ready,
                         self.ready)
            k.weights.split_through(dve, self.next_slab)
            return
        k.dve.link(dve.tensor_tensor(self.out, self.x, over_chunks(self.rs, KC), ALU.mult))
        for c in range(KC):
            dve.tensor_scalar(self.out[:, c, :], self.out[:, c, :], self.gain[:, c:c + 1],
                              self.shift[:, c:c + 1], ALU.mult, ALU.add).then_inc(self.ready[c][0], 1)
        dve.wait_ge(*self.ready[-1])


class OutProjection(Stage):

    def __init__(self, core, x, x_ready, chunks, rms_gain=None, bias=None, ln=None, glu=False, split=False):
        self.x, self.x_ready, self.chunks = x if isinstance(x, tuple) else (x,), x_ready, chunks
        self.split = split
        self.rms_gain, self.bias, self.ln, self.glu = rms_gain, bias, ln, glu
        super().__init__(core)

    def setup(self):
        k = self.k
        self.y = k.area(AT_Y, KC, T)
        self.sq = k.area(AT_SQ, KC, T)
        self.rs = k.area(AT_RS, T)
        self.gate = k.area(AT_RS, 2, T)
        self.y_ready = k.counter("y_ready_act" if self.ln is None else "y_ready").events(KC)
        self.y_squared = k.counter("y_squared").events(KC)
        if self.glu:
            self.gate_used = k.counter("out_gate_used").events(KC)
            self.out_jobs = [k.job(free) for free in self.gate_used]
        else:
            self.out_jobs = [k.job(free) for free in (self.y_squared if self.ln is None else self.y_ready)[1::2]]
        self.sum_job = k.job()
        if self.ln is not None:
            self.var_job = k.job()
            self.centred = k.counter("centred").event()
        if self.glu:
            self.gated = k.counter("out_gate").events(KC)
        self.root = k.counter("root_ready").event()
        slabs = (2 if self.glu else 1) * self.chunks * KC // SLAB_TILES
        self.slab0 = k.weights.reserve(slabs, len(self.x) == 2)
        self.next_slab = k.weights.count
        self.last_slab = [self.slab0 + (j + 1) * slabs // len(self.out_jobs) - 1 +
                          (1 if (j + 1) * slabs % len(self.out_jobs) else 0) for j in range(len(self.out_jobs))]
        self.h_new = k.counter("residual_ready").events(KC)
        if self.split:
            if self.ln is not None:
                self.scaled = k.counter("norm_scaled").event()
            self.hi_ready = k.counter("input_rounded").events(KC)
            self.parts = k.x_parts[:, 0], k.x_parts[:, 1]
            self.parts_ready = k.counter("normed_ready").events(KC)
            k.parts_ready = self.parts_ready
        k.h_ready = self.h_new
        self.root_free, k.root_free = k.root_free, self.h_new[-1]

    def columns(self, pe, job, n, tiles):
        k = self.k
        out = job.ap[:, tiles * T:(tiles + 1) * T]
        for c in range(self.chunks):
            if self.chunks == KC:
                if n % 2 == 0 and c == 0:
                    self.slab = [s.rearrange("p (k c) -> p k c", k=KC) for s in k.weights.next(pe)]
                w = [s[:, c, (n % 2) * P:(n % 2 + 1) * P] for s in self.slab]
            else:
                i = n * self.chunks + c
                if i % SLAB_TILES == 0:
                    self.slab = [s.rearrange("p (t c) -> p t c", c=P) for s in k.weights.next(pe)]
                w = [s[:, i % SLAB_TILES, :] for s in self.slab]
            if n == 0:
                pe.wait_ge(*self.x_ready[c])
            mm = k.weights.product(pe, out, w, [x[:, c, :] for x in self.x], c == 0, c == self.chunks - 1)
        return mm

    def tensor(self, pe):
        for j, job in enumerate(self.out_jobs):
            begin(pe, job)
            self.columns(pe, job, 2 * j, 0)
            self.columns(pe, job, 2 * j + 1, 1).then_inc(job.full[0], 1)
        begin(pe, self.sum_job)
        rms = self.ln is None
        for c in range(KC):
            pe.wait_ge(*(self.y_squared if rms else self.y_ready)[c])
            mm = pe.matmul(self.sum_job.ap[:, 0:T], self.k.c("mean"), (self.sq if rms else self.y)[:, c, :],
                           start=(c == 0), stop=(c == KC - 1))
        mm.then_inc(self.sum_job.full[0], 1)
        if not rms:
            begin(pe, self.var_job)
            for c in range(KC):
                pe.wait_ge(*self.y_squared[c])
                mm = pe.matmul(self.var_job.ap[:, 0:T], self.k.c("mean"), self.sq[:, c, :],
                               start=(c == 0), stop=(c == KC - 1))
            mm.then_inc(self.var_job.full[0], 1)

    def scalar(self, act):
        k = self.k
        if self.ln is None:
            for j, job in enumerate(self.out_jobs):
                k.weights.round_through(act, self.last_slab[j] + 1)
                act.wait_ge(*job.full)
                for t in range(2):
                    c = 2 * j + t
                    b = self.bias[:, c:c + 1] if self.bias is not None else 0.0
                    ins = act.activation(self.y[:, c, :], job.ap[:, t * T:(t + 1) * T], ACT.Identity, bias=b)
                    ins.then_inc(self.y_ready[c][0], 1)
                    ins = act.activation(self.sq[:, c, :], job.ap[:, t * T:(t + 1) * T], ACT.Square, bias=b)
                    ins.then_inc(self.y_squared[c][0], 1)
            act.wait_ge(*self.sum_job.full)
            if self.root_free:
                act.wait_ge(*self.root_free)
            root_inverse(act, k.act, self.rs, self.sum_job.ap[:, 0:T], k.eps[:, 0:1], self.sum_job.free)\
                .then_inc(self.root[0], 1)
            if self.split:
                for c in range(KC):
                    act.wait_ge(*self.h_new[c])
                    act.activation(self.parts[0][:, c, :], k.h[:, c, :], ACT.Identity)\
                       .then_inc(self.hi_ready[c][0], 1)
            return
        if self.glu:
            for c, job in enumerate(self.out_jobs):
                k.weights.round_through(act, self.last_slab[c] + 1)
                act.wait_ge(*job.full)
                if c >= 2:
                    act.wait_ge(*self.gate_used[c - 2])
                act.activation(self.gate[:, c % 2, :], job.ap[:, T:2 * T], ACT.Sigmoid)\
                   .then_inc(self.gated[c][0], 1)
        k.weights.round_through(act, self.next_slab)
        act.wait_ge(*self.centred)
        for c in range(KC):
            act.activation(self.sq[:, c, :], self.y[:, c, :], ACT.Square).then_inc(self.y_squared[c][0], 1)
        act.wait_ge(*self.var_job.full)
        root_inverse(act, k.act, self.rs, self.var_job.ap[:, 0:T], k.eps[:, 1:2], self.var_job.free)\
            .then_inc(self.root[0], 1)
        if self.split:
            act.wait_ge(*self.scaled)
            gain, shift = (k.v(n, self.ln * KC, KC) for n in ("ln_g", "ln_b"))
            round_normed(act, self.parts[0], self.y, gain, shift, self.hi_ready)

    def vector(self, dve):
        k = self.k
        if self.ln is None:
            for last in self.last_slab:
                k.weights.split_through(dve, last + 1)
            dve.wait_ge(*self.root)
            k.dve.link(dve.tensor_tensor(self.y, self.y, over_chunks(self.rs, KC), ALU.mult))
            for c in range(KC):
                dve.scalar_tensor_tensor(k.h[:, c, :], self.y[:, c, :], self.rms_gain[:, c:c + 1], k.h[:, c, :],
                                         ALU.mult, ALU.add).then_inc(self.h_new[c][0], 1)
            dve.wait_ge(*self.h_new[-1])
            if self.split:
                for c in range(KC):
                    dve.wait_ge(*self.hi_ready[c])
                    dve.tensor_tensor(self.parts[1][:, c, :], k.h[:, c, :], self.parts[0][:, c, :].bitcast(F32),
                                      ALU.subtract).then_inc(self.parts_ready[c][0], 1)
                dve.wait_ge(*self.parts_ready[-1])
            return
        if self.glu:
            for c, job in enumerate(self.out_jobs):
                k.weights.split_through(dve, self.last_slab[c] + 1)
                dve.wait_ge(*self.gated[c])
                dve.tensor_tensor(self.y[:, c, :], job.ap[:, 0:T], self.gate[:, c % 2, :], ALU.mult)\
                   .then_inc(self.gate_used[c][0], 1)
                dve.wait_ge(*self.gate_used[c])
                dve.scalar_tensor_tensor(self.y[:, c, :], k.h[:, c, :], ALPHA, self.y[:, c, :], ALU.mult, ALU.add)\
                   .then_inc(self.y_ready[c][0], 1)
        else:
            for j, job in enumerate(self.out_jobs):
                k.weights.split_through(dve, self.last_slab[j] + 1)
                dve.wait_ge(*job.full)
                for t in range(2):
                    c = 2 * j + t
                    dve.scalar_tensor_tensor(self.y[:, c, :], k.h[:, c, :], ALPHA, job.ap[:, t * T:(t + 1) * T],
                                             ALU.mult, ALU.add).then_inc(self.y_ready[c][0], 1)
        dve.wait_ge(*self.sum_job.full)
        dve.tensor_copy(self.rs, self.sum_job.ap[:, 0:T]).then_inc(self.sum_job.free[0], 1)
        dve.wait_ge(*self.sum_job.free)
        dve.tensor_tensor(self.y, self.y, over_chunks(self.rs, KC), ALU.subtract).then_inc(self.centred[0], 1)
        dve.wait_ge(*self.root)
        gain, shift = (k.v(n, self.ln * KC, KC) for n in ("ln_g", "ln_b"))
        if self.split:
            dve.tensor_tensor(self.y, self.y, over_chunks(self.rs, KC), ALU.mult).then_inc(self.scaled[0], 1)
            dve.wait_ge(*self.scaled)
            split_normed(k, dve, k.h, self.parts, self.y, gain, shift, self.hi_ready, self.parts_ready, self.h_new)
            return
        k.dve.link(dve.tensor_tensor(self.y, self.y, over_chunks(self.rs, KC), ALU.mult))
        for c in range(KC):
            dve.tensor_scalar(k.h[:, c, :], self.y[:, c, :], gain[:, c:c + 1], shift[:, c:c + 1],
                              ALU.mult, ALU.add).then_inc(self.h_new[c][0], 1)
        dve.wait_ge(*self.h_new[-1])


class GateUp(Stage):

    def __init__(self, core, x, x_ready):
        self.x, self.x_ready = x, x_ready
        super().__init__(core)

    def setup(self):
        k = self.k
        self.hid = k.area(AT_HID_NEW, 2, T)
        self.parts = k.hid_parts[:, 0], k.hid_parts[:, 1]
        self.slab0 = k.weights.reserve(FC, True)
        self.silu = k.counter("gate_ready").events(FC)
        self.whole = k.counter("hidden_whole").events(FC)
        self.rounded = k.counter("hidden_rounded").events(FC)
        self.ready = k.counter("hidden_ready").events(FC)
        self.jobs = [k.job(free) for free in self.whole]

    def tensor(self, pe):
        k = self.k
        for j, job in enumerate(self.jobs):
            begin(pe, job)
            slab = [s.rearrange("p (k c) -> p k c", k=KC) for s in k.weights.next(pe)]
            for half in range(2):
                for c in range(KC):
                    if j == 0:
                        pe.wait_ge(*self.x_ready[c])
                    mm = k.weights.product(pe, job.ap[:, half * T:(half + 1) * T],
                                           [s[:, c, half * P:(half + 1) * P] for s in slab],
                                           [x[:, c, :] for x in self.x], c == 0, c == KC - 1)
            mm.then_inc(job.full[0], 1)

    def scalar(self, act):
        for j, job in enumerate(self.jobs):
            self.k.weights.round_through(act, self.slab0 + j + 1)
            act.wait_ge(*job.full)
            if j >= 2:
                act.wait_ge(*self.ready[j - 2])
            act.activation(self.hid[:, j % 2, :], job.ap[:, 0:T], ACT.Silu).then_inc(self.silu[j][0], 1)

    def vector(self, dve):
        for j, job in enumerate(self.jobs):
            self.k.weights.split_through(dve, self.slab0 + j + 1)
            dve.wait_ge(*self.silu[j])
            hid, (hi, lo) = self.hid[:, j % 2, :], (part[:, j, :] for part in self.parts)
            dve.tensor_tensor(hid, hid, job.ap[:, T:2 * T], ALU.mult).then_inc(self.whole[j][0], 1)
            dve.wait_ge(*self.whole[j])
            dve.tensor_copy(hi, hid).then_inc(self.rounded[j][0], 1)
            dve.wait_ge(*self.rounded[j])
            dve.tensor_tensor(lo, hid, hi.bitcast(F32), ALU.subtract).then_inc(self.ready[j][0], 1)


def feed_forward(k, x, x_ready, **residual):
    up = GateUp(k, x, x_ready)
    return [up, OutProjection(k, up.parts, up.ready, FC, **residual)]


MIXERS = {}
SPLIT_MIXERS = ("hgrn0", "hgrn1", "mlstm")
T2 = 2 * T
N4 = A_HEADS * P
H_A = 0
H_Q = 6656
H_K = H_Q + A_HEADS * T
H_V = H_K + A_HEADS * T2
H_Z = H_V + A_HEADS * T2
H_QB = H_Z + A_HEADS * T
H_KB = H_QB + B_PAIRS * T
H_VB = H_KB + T2
H_PAD = H_VB + T2
H_GATE = H_PAD + 3 * 2 * (T + CONV_A - 1)
H_MIX = H_GATE + 3 * T2
H_END = H_MIX + KC * T
H_P = 0
H_PT = H_P + 2 * T2
H_VT = H_PT + 2 * 4 * T
H_GB = 0
H_L = H_GB + 16 * P
H_X = H_L + 16 * P
H_XT = H_QB
H_QS = H_XT + 16 * P
H_KT = H_END
H_VTOK = H_KT + 8 * P
H_S = H_VTOK + 8 * P
H_LM = H_S + 2 * DH * P
SEQS = 2


class HybridProjection(Stage):

    def setup(self):
        k = self.k
        self.a = k.area(H_A, KC, T2)
        self.norms = [PreNorm(k, k.area(H_END, KC, T), [(k.consts_loaded, 64)] * KC, self.a[:, :, 0:T],
                              k.coef[:, 1, :], k.mod[:, 0:KC, 1], sq_at=AT_Y),
                      PreNorm(k, k.h[:, :, :], k.h_ready, self.a[:, :, T:T2],
                              k.coef[:, 0, :], k.mod[:, 0:KC, 0], sq_at=AT_Y)]
        self.gate_jobs = k.take(2)
        self.beta = k.area(H_GATE, T2)[0:8, :]
        self.g = k.area(H_GATE + T2, T2)[0:8, :]
        self.g_abs = k.area(H_GATE + 2 * T2, T2)[0:8, :]
        lat = slice(T, T2)
        q, kk, v = k.area(H_Q, A_HEADS, T), k.area(H_K, A_HEADS, T2), k.area(H_V, A_HEADS, T2)
        z, qb = k.area(H_Z, A_HEADS, T), k.area(H_QB, B_PAIRS, T)
        every = slice(0, T2)
        self.chunks = [(q[:, h, :], lat, "conv") for h in range(4)] + [(kk[:, h, :], every, "conv") for h in range(4)]
        self.chunks += [(v[:, h, :], every, "conv") for h in range(4)] + [(z[:, h, :], lat, "silu") for h in range(4)]
        self.chunks += [(qb[:, h, :], lat, "copy") for h in range(4)]
        self.chunks += [(k.area(H_KB, T2), every, "copy"), (k.area(H_VB, T2), every, "copy")]
        k.weights.reserve(len(self.chunks) // 2, False)
        self.taken = k.counter("projection_taken").events(len(self.chunks))
        self.jobs = [k.job(free) for free in self.taken]
        self.pad = k.area(H_PAD, 3, SEQS, T + CONV_A - 1)
        self.pad_clear = k.counter("pad_clear").event()
        self.convolved = k.counter("convolved").events(12)
        self.conv_ready = k.counter("conv_ready").events(12)
        self.gate_exp = k.counter("gate_exp").event()
        self.gate_linear = k.counter("gate_linear").event()
        self.k.gates_ready = k.counter("gates_ready").events(2)
        self.heads = [(self.chunks[h][0], "ones", 1.0) for h in range(8)]
        self.heads += [(self.chunks[h][0], "ones64", 1.0 / 64) for h in range(16, 21)]
        self.squared = k.counter("head_squared").events(len(self.heads))
        self.log_ready = k.counter("head_log").events(len(self.heads))
        self.sum_jobs = [k.job(e) for e in self.log_ready]
        self.normed = k.counter("head_normed").events(len(self.heads))
        self.turn_jobs = k.take(5)
        self.turned = k.counter("rope_done").events(5)
        starts = [sum(x.shape[1] for x, _, _ in self.heads[:i]) for i in range(len(self.heads) + 1)]
        self.rs = [k.area(at, x.shape[1]) for at, (x, _, _) in zip(starts, self.heads)]
        self.batches = [(range(0, 8), k.area(0, starts[8])), (range(8, 13), k.area(starts[8], starts[13] - starts[8]))]
        self.root_exp = k.counter("head_root").events(2)
        self.sq = k.area(starts[-1], 2, T2)
        k.hyb = self

    def tensor(self, pe):
        k = self.k
        for norm in self.norms:
            norm.tensor(pe)
        k.background.fill(pe, 2 * MOD_EARLY, MOD_EARLY)
        for norm in self.norms:
            pe.wait_ge(*norm.ready[-1])
        for job, name in zip(self.gate_jobs, ("hyb_beta_w", "hyb_g_w")):
            begin(pe, job)
            w = k.v(name, 0, KC * 8).rearrange("p (k c) -> p k c", k=KC)
            for c in range(KC):
                mm = pe.matmul(job.ap[0:8, 0:T2], w[:, c, :], self.a[:, c, :], start=(c == 0), stop=(c == KC - 1))
            mm.then_inc(job.full[0], 1)
        for n, (job, (_, tokens, _)) in enumerate(zip(self.jobs, self.chunks)):
            begin(pe, job)
            if n % 2 == 0:
                slab = k.weights.next(pe)[0].rearrange("p (k c) -> p k c", k=KC)
            out = job.ap[:, 0:tokens.stop - tokens.start]
            for c in range(KC):
                mm = k.weights.matmul(pe, out, slab[:, c, (n % 2) * P:(n % 2 + 1) * P], self.a[:, c, tokens],
                                      start=(c == 0), stop=(c == KC - 1))
            mm.then_inc(job.full[0], 1)
        for i, (x, ones, _) in enumerate(self.heads):
            n = x.shape[1]
            begin(pe, self.sum_jobs[i])
            pe.wait_ge(*self.squared[i])
            pe.matmul(self.sum_jobs[i].ap[:, 0:n], k.c(ones), self.sq[:, i % 2, 0:n], start=True, stop=True)\
              .then_inc(self.sum_jobs[i].full[0], 1)
        for i in range(5):
            x = self.heads[8 + i][0]
            x = x[:, x.shape[1] - T:]
            begin(pe, self.turn_jobs[i])
            pe.wait_ge(*self.normed[8 + i])
            pe.matmul(self.turn_jobs[i].ap[:, 0:T], k.c("rope_turn"), x, start=True, stop=True)\
              .then_inc(self.turn_jobs[i].full[0], 1)

    def scalar(self, act):
        k = self.k
        for norm in self.norms:
            norm.scalar(act)
        k.background.take(act, 2 * MOD_EARLY, MOD_EARLY)
        beta_job, g_job = self.gate_jobs
        act.wait_ge(*beta_job.full)
        act.activation(self.beta, beta_job.ap[0:8, 0:T2], ACT.Sigmoid).then_inc(beta_job.free[0], 1)
        act.wait_ge(*g_job.full)
        dt_bias = k.v("hyb_dt_bias", rows=8)
        k.act.link(act.activation(self.g_abs, g_job.ap[0:8, 0:T2], ACT.Abs, bias=dt_bias))
        act.activation(self.g, g_job.ap[0:8, 0:T2], ACT.Identity, bias=dt_bias).then_inc(g_job.free[0], 1)
        act.wait_ge(*g_job.free)
        act.activation(k.cols[0:8, 0, 0:1], k.v("hyb_a_log", rows=8), ACT.Exp).then_inc(self.gate_linear[0], 1)
        k.act.link(act.activation(self.g_abs, self.g_abs, ACT.Exp, scale=-1.0))
        act.activation(self.g_abs, self.g_abs, ACT.Ln, bias=k.eps[0:8, 2:3]).then_inc(self.gate_exp[0], 1)
        act.wait_ge(*self.pad_clear)

        def silu(n):
            act.wait_ge(*self.convolved[n])
            x = self.chunks[n][0]
            act.activation(x, x, ACT.Silu).then_inc(self.conv_ready[n][0], 1)

        for n, (job, (x, tokens, kind)) in enumerate(zip(self.jobs, self.chunks)):
            act.wait_ge(*job.full)
            seqs = (tokens.stop - tokens.start) // T
            if kind == "conv":
                if n >= 3:
                    act.wait_ge(*self.convolved[n - 3])
                act.activation(self.pad[:, n % 3, 0:seqs, 2:2 + T],
                               job.ap[:, 0:seqs * T].rearrange("p (s t) -> p s t", t=T), ACT.Identity)\
                   .then_inc(self.taken[n][0], 1)
            else:
                act.activation(x, job.ap[:, 0:seqs * T], ACT.Silu if kind == "silu" else ACT.Identity)\
                   .then_inc(self.taken[n][0], 1)
            if 1 <= n <= 12:
                silu(n - 1)
        for i, (x, _, scale) in enumerate(self.heads):
            n = x.shape[1]
            if i < 8:
                act.wait_ge(*self.conv_ready[i])
            else:
                act.wait_ge(*self.taken[8 + i])
            if i >= 2:
                act.wait_ge(*self.sum_jobs[i - 2].full)
            act.activation(self.sq[:, i % 2, 0:n], x, ACT.Square).then_inc(self.squared[i][0], 1)
            act.wait_ge(*self.sum_jobs[i].full)
            act.activation(self.rs[i], self.sum_jobs[i].ap[:, 0:n], ACT.Ln, bias=k.eps[:, 0:1],
                           scale=scale).then_inc(self.log_ready[i][0], 1)
            for b, (members, roots) in enumerate(self.batches):
                if i == members[-1]:
                    act.wait_ge(*self.log_ready[i])
                    act.activation(roots, roots, ACT.Exp, scale=-0.5).then_inc(self.root_exp[b][0], 1)

    def vector(self, dve):
        k = self.k
        chain = k.dve
        dve.memset(self.pad[:, :, :, 0:2], 0.0)
        dve.memset(self.pad[:, :, :, 2 + T:4 + T], 0.0).then_inc(self.pad_clear[0], 1)
        for norm in self.norms:
            norm.vector(dve)
        dve.wait_ge(*self.gate_linear)
        chain.link(dve.tensor_scalar(self.g, self.g, 0.0, None, ALU.max))
        dve.wait_ge(*self.gate_exp)
        chain.link(dve.tensor_tensor(self.g, self.g, self.g_abs, ALU.add))
        dve.tensor_scalar(self.g, self.g, k.cols[0:8, 0, 0:1], -1.0, ALU.mult, ALU.mult)\
           .then_inc(k.gates_ready[0][0], 1)
        dve.wait_ge(*k.gates_ready[0])
        for n in range(12):
            x, tokens, _ = self.chunks[n]
            seqs = (tokens.stop - tokens.start) // T
            x = x.rearrange("p (s t) -> p s t", t=T)
            dve.wait_ge(*self.taken[n])
            for j in range(CONV_A):
                w = k.v("hyb_conv_w", j * 12 + n)
                src = self.pad[:, n % 3, 0:seqs, j:j + T]
                if j == 0:
                    ins = dve.tensor_scalar(x, src, w, None, ALU.mult)
                else:
                    ins = dve.scalar_tensor_tensor(x, src, w, x, ALU.mult, ALU.add)
                if j < CONV_A - 1:
                    chain.link(ins)
            ins.then_inc(self.convolved[n][0], 1)
        for i, (x, _, _) in enumerate(self.heads):
            n = x.shape[1]
            dve.wait_ge(*self.root_exp[0 if i < 8 else 1])
            gain = (P ** -0.5 if i < 4 else 1.0) if i < 8 else k.v("hyb_q_norm" if i < 12 else "hyb_k_norm")
            dve.scalar_tensor_tensor(x, x, gain, self.rs[i], ALU.mult, ALU.mult)\
               .then_inc(self.normed[i][0], 1)
        for i in range(5):
            x = self.heads[8 + i][0]
            x = x[:, x.shape[1] - T:]
            turned = self.sq[:, i % 2, 0:T]
            dve.wait_ge(*self.normed[8 + i])
            dve.wait_ge(*self.turn_jobs[i].full)
            dve.tensor_tensor(turned, self.turn_jobs[i].ap[:, 0:T], k.c("sin"), ALU.mult)\
               .then_inc(self.turn_jobs[i].free[0], 1)
            chain.link(dve.tensor_tensor(x, x, k.c("cos"), ALU.mult))
            dve.wait_ge(*self.turn_jobs[i].free)
            dve.tensor_tensor(x, x, turned, ALU.add).then_inc(self.turned[i][0], 1)


class HybridAttention(Stage):

    def setup(self):
        k = self.k
        self.q, self.kb, self.vb = k.area(H_QB, B_PAIRS, T), k.area(H_KB, T2), k.area(H_VB, T2)
        self.probs = k.area(H_P, 2, T2)
        self.pt = k.area(H_PT, 2, 4, T)
        self.vt = k.area(H_VT, 4, P)
        self.out = k.area(H_MIX + A_HEADS * T, B_PAIRS, T)
        self.vt_ready = k.counter("values_by_token").event()
        self.vt_job = k.job(self.vt_ready)
        self.units = [(j, half, t) for j in range(B_PAIRS) for half in range(2) for t in range(TT)]
        n = len(self.units)
        self.score_jobs, self.turn_jobs, self.pv_jobs = [], [], []
        self.peak = k.counter("score_peak").events(n)
        self.exp_done = k.counter("exp_done").events(n)
        self.probs_ready = k.counter("probs_ready").events(n)
        self.pt_ready = k.counter("probs_turned").events(n)
        self.out_ready = k.counter("attention_out").events(n // 2)
        for u in range(n + 1):
            if u < n:
                self.score_jobs.append(k.job(self.exp_done[u]))
            if u >= 1:
                self.turn_jobs.append(k.job(self.pt_ready[u - 1]))
                if u % 2 == 0:
                    self.pv_jobs.append(k.job(self.out_ready[u // 2 - 1]))
        k.attention_out = self.out_ready

    def tensor(self, pe):
        k = self.k
        begin(pe, self.vt_job)
        pe.wait_ge(*k.hyb.taken[21])
        for s in range(4):
            mm = pe.transpose(self.vt_job.ap[:, s * P:(s + 1) * P], self.vb[:, s * P:(s + 1) * P], k.c("ident"))
        mm.then_inc(self.vt_job.full[0], 1)
        pe.wait_ge(*k.hyb.turned[4])
        for u in range(len(self.units) + 1):
            if u < len(self.units):
                j, half, t = self.units[u]
                rows = slice(64 * half, 64 * half + 64)
                begin(pe, self.score_jobs[u])
                pe.matmul(self.score_jobs[u].ap[:, :], self.q[rows, j, t * P:(t + 1) * P], self.kb[rows, :],
                          start=True, stop=True).then_inc(self.score_jobs[u].full[0], 1)
            k.background.fill(pe, 2)
            if u >= 1:
                w = u - 1
                begin(pe, self.turn_jobs[w])
                pe.wait_ge(*self.probs_ready[w])
                for s in range(4):
                    mm = pe.transpose(self.turn_jobs[w].ap[:, s * P:(s + 1) * P],
                                      self.probs[:, w % 2, s * P:(s + 1) * P], k.c("ident"))
                mm.then_inc(self.turn_jobs[w].full[0], 1)
                if w % 2 == 1:
                    m = w // 2
                    begin(pe, self.pv_jobs[m])
                    if m == 0:
                        pe.wait_ge(*self.vt_ready)
                    pe.wait_ge(*self.pt_ready[w])
                    for s in range(4):
                        mm = pe.matmul(self.pv_jobs[m].ap[:, 0:T], self.vt[:, s, :], self.pt[:, m % 2, s, :],
                                       start=(s == 0), stop=(s == 3))
                    mm.then_inc(self.pv_jobs[m].full[0], 1)

    def scalar(self, act):
        k = self.k
        act.wait_ge(*self.vt_job.full)
        act.activation(self.vt, self.vt_job.ap[:, :].rearrange("p (s c) -> p s c", s=4), ACT.Identity)\
           .then_inc(self.vt_ready[0], 1)
        for u in range(len(self.units) + 1):
            if u < len(self.units):
                act.wait_ge(*self.peak[u])
                if u >= 2:
                    act.wait_ge(*self.turn_jobs[u - 2].full)
                act.activation(self.probs[:, u % 2, :], self.score_jobs[u].ap[:, :], ACT.Exp,
                               bias=k.cols[:, 1, u:u + 1], scale=0.125, accum_out=k.cols[:, 2, u:u + 1])\
                   .then_inc(self.exp_done[u][0], 1)
            if u >= 1:
                w = u - 1
                act.wait_ge(*self.turn_jobs[w].full)
                m = w // 2
                if m >= 2:
                    act.wait_ge(*self.pv_jobs[m - 2].full)
                t = w % 2
                act.activation(self.pt[:, m % 2, :, t * P:(t + 1) * P],
                               self.turn_jobs[w].ap[:, :].rearrange("p (s c) -> p s c", s=4), ACT.Identity)\
                   .then_inc(self.pt_ready[w][0], 1)
            k.background.take(act, 2)

    def vector(self, dve):
        k = self.k
        for u in range(len(self.units) + 1):
            if u < len(self.units):
                dve.wait_ge(*self.score_jobs[u].full)
                k.dve.link(dve.reduce_max(k.cols[:, 3, u:u + 1], self.score_jobs[u].ap[:, :], AXX))
                dve.tensor_scalar(k.cols[:, 1, u:u + 1], k.cols[:, 3, u:u + 1], -0.125, None, ALU.mult)\
                   .then_inc(self.peak[u][0], 1)
                dve.wait_ge(*self.exp_done[u])
                k.dve.link(dve.reciprocal(k.cols[:, 3, u:u + 1], k.cols[:, 2, u:u + 1]))
                dve.tensor_scalar(self.probs[:, u % 2, :], self.probs[:, u % 2, :], k.cols[:, 3, u:u + 1],
                                  None, ALU.mult).then_inc(self.probs_ready[u][0], 1)
            if u >= 2 and u % 2 == 0:
                m = u // 2 - 1
                j, half, _ = self.units[u - 1]
                rows = slice(64 * half, 64 * half + 64)
                dve.wait_ge(*self.pv_jobs[m].full)
                dve.tensor_copy(self.out[rows, j, :], self.pv_jobs[m].ap[rows, 0:T]).then_inc(self.out_ready[m][0], 1)


C_BETA, C_G, C_GC, C_BEG, C_TAIL, C_LAST = 4, 5, 6, 7, 8, 9


class DeltaColumns(Stage):

    def setup(self):
        k = self.k
        self.turned = k.counter("gates_by_token").event()
        self.job = k.job(self.turned)
        self.summed = k.counter("gates_summed").event()
        self.sum_job = k.job(self.summed)
        self.exp = k.counter("gates_exp").event()
        self.ready = k.counter("delta_columns").event()

    def tensor(self, pe):
        k = self.k
        begin(pe, self.job)
        pe.wait_ge(*k.gates_ready[0])
        for n in range(4):
            for i, x in enumerate((k.hyb.beta, k.hyb.g)):
                mm = pe.transpose(self.job.ap[:, i * 32 + n * 8:i * 32 + n * 8 + 8], x[:, n * P:(n + 1) * P],
                                  k.c("ident", 0, 8, rows=8))
        mm.then_inc(self.job.full[0], 1)
        begin(pe, self.sum_job)
        pe.wait_ge(*self.turned)
        for n in range(4):
            for d, tri in enumerate(("upto", "from_")):
                at = n * 8 + d * 4
                mm = pe.matmul(self.sum_job.ap[:, at:at + 4], k.c(tri), k.cols[:, C_G, at:at + 4],
                               start=True, stop=True)
        mm.then_inc(self.sum_job.full[0], 1)

    def scalar(self, act):
        k = self.k
        act.wait_ge(*self.summed)
        act.activation(k.cols[:, C_BEG, :], k.cols[:, C_GC, :], ACT.Exp).then_inc(self.exp[0], 1)

    def vector(self, dve):
        k = self.k
        dve.wait_ge(*self.job.full)
        dve.tensor_copy(k.cols[:, C_BETA:C_G + 1, :], self.job.ap[:, 0:64].rearrange("p (a b) -> p a b", a=2))\
           .then_inc(self.turned[0], 1)
        dve.wait_ge(*self.sum_job.full)
        dve.tensor_copy(k.cols[:, C_GC, :], self.sum_job.ap[:, 0:32]).then_inc(self.summed[0], 1)
        dve.wait_ge(*self.exp)
        dve.wait_ge(*self.turned)
        dve.tensor_tensor(k.cols[:, C_BEG, :], k.cols[:, C_BEG, :], k.cols[:, C_BETA, :], ALU.mult)\
           .then_inc(self.ready[0], 1)
        dve.wait_ge(*self.ready)


class Delta(Stage):

    def __init__(self, core, seq):
        self.seq = seq
        super().__init__(core)

    def setup(self):
        k = self.k
        s = self.seq
        self.gb, self.l, self.x, self.xt, self.qs = (
            k.area(at, 4, A_HEADS, P) for at in (H_GB, H_L, H_X, H_XT, H_QS))
        self.lm = k.area(H_LM, 2, A_HEADS, P)
        self.kt, self.vt = k.area(H_KT, TT, A_HEADS, P), k.area(H_VTOK, TT, A_HEADS, P)
        self.state = k.area(H_S, 2, DH, P)
        self.kf = k.area(H_K, A_HEADS, T2)
        self.vf = k.area(H_V, A_HEADS, T2)
        self.qf = k.area(H_Q, A_HEADS, T)
        self.groups = [(d, t) for d in range(DIRS) for t in range(TT)]
        self.tok_ready = k.counter("delta_by_token").events(4)
        self.tok_jobs = [k.job(e) for e in self.tok_ready]
        self.gb_ready = k.counter("decay_rows").events(4)
        self.gb_jobs = [k.job(e) for e in self.gb_ready]
        self.diff = k.counter("decay_difference").events(4)
        self.decay = k.counter("decay_ready").events(4)
        self.l_ready = k.counter("lower_ready").events(4)
        self.kk_jobs = [k.job(e) for e in self.l_ready]
        self.masked = k.counter("pairs_masked").events(4 * len(LEVELS))
        self.q_ready = k.counter("inverse_q").events(4 * len(LEVELS))
        self.x_ready = k.counter("inverse_x").events(4 * len(LEVELS))
        self.xt_ready = k.counter("inverse_xt").events(4 * len(LEVELS))
        self.level_jobs = {}
        for l in range(len(LEVELS)):
            for g in range(4):
                self.level_jobs[l, g, "q"] = k.job(self.q_ready[4 * l + g])
            for g in range(4):
                self.level_jobs[l, g, "x"] = k.job(self.x_ready[4 * l + g])
                self.level_jobs[l, g, "xt"] = k.job(self.xt_ready[4 * l + g])
        self.rhs = k.counter("delta_rhs").events(4)
        self.w_ready = k.counter("delta_w").events(4)
        self.u_ready = k.counter("delta_u").events(4)
        self.w_jobs, self.u_jobs = [], []
        for g in range(4):
            self.w_jobs.append(k.job(self.w_ready[g]))
            self.u_jobs.append(k.job(self.u_ready[g]))
        self.tail_diff = k.counter("tail_difference").event()
        self.tail_exp = k.counter("tail_exp").event()
        self.tail_ready = k.counter("tail_ready").events(4)
        if s == 1:
            self.intra_diff = k.counter("intra_difference").events(4)
            self.intra_exp = k.counter("intra_exp").events(4)
            self.intra_ready = k.counter("intra_ready").events(4)
            self.kq_jobs = [k.job(e) for e in self.intra_ready]
            self.qd_exp = k.counter("query_decay_exp").events(4)
            self.qd_ready = k.counter("query_decay").events(4)
        self.v_new = k.counter("value_new").events(4)
        self.s_new = k.counter("state_new").events(4)
        self.steps = [(0, 0, 0), (0, 1, 1), (1, 0, 1), (1, 1, 0)]
        self.ws_jobs, self.kv_jobs = [], []
        for i, (step, _, _) in enumerate(self.steps):
            zero = s == 0 and step == 0
            last = s == 1 and step == 1
            self.ws_jobs.append(None if zero else k.job(self.v_new[i]))
            self.kv_jobs.append(None if last else k.job(self.s_new[i]))
        if s == 1:
            self.out_jobs = k.take(TT)

    def tensor(self, pe):
        k, s = self.k, self.seq
        if s == 0:
            pe.wait_ge(*k.hyb.conv_ready[11])
            pe.wait_ge(*k.hyb.normed[7])
        for i, (job, src) in enumerate(zip(self.tok_jobs, (self.kf, self.kf, self.vf, self.vf))):
            begin(pe, job)
            at = s * T + (i % 2) * P
            for h in range(A_HEADS):
                mm = pe.transpose(job.ap[:, h * P:(h + 1) * P], src[:, h, at:at + P], k.c("ident"))
            mm.then_inc(job.full[0], 1)
        for g, (d, t) in enumerate(self.groups):
            begin(pe, self.gb_jobs[g])
            for h in range(A_HEADS):
                col = k.cols[:, C_G, (s * TT + t) * 8 + d * 4 + h:(s * TT + t) * 8 + d * 4 + h + 1]
                mm = pe.matmul(self.gb_jobs[g].ap[:, h * P:(h + 1) * P], col.broadcast_to([P, P]),
                               k.c(("upto", "from_")[d]), start=True, stop=True)
            mm.then_inc(self.gb_jobs[g].full[0], 1)
        for g, (d, t) in enumerate(self.groups):
            begin(pe, self.kk_jobs[g])
            for h in range(A_HEADS):
                kt = self.kf[:, h, s * T + t * P:s * T + (t + 1) * P]
                mm = pe.matmul(self.kk_jobs[g].ap[:, h * P:(h + 1) * P], kt, kt, start=True, stop=True)
            mm.then_inc(self.kk_jobs[g].full[0], 1)
        for l in range(len(LEVELS)):
            for g in range(4):
                job = self.level_jobs[l, g, "q"]
                begin(pe, job)
                pe.wait_ge(*self.masked[4 * l + g])
                if l > 0:
                    pe.wait_ge(*self.xt_ready[4 * (l - 1) + g])
                for h in range(A_HEADS):
                    mm = pe.matmul(job.ap[:, h * P:(h + 1) * P], self.lm[:, g % 2, h, :], self.xt[:, g, h, :],
                                   start=True, stop=True)
                mm.then_inc(job.full[0], 1)
                if g % 2:
                    k.background.fill(pe, 1)
            for g in range(4):
                pe.wait_ge(*self.q_ready[4 * l + g])
                if l > 0:
                    pe.wait_ge(*self.x_ready[4 * (l - 1) + g])
                for which, left, right in (("x", self.qs, self.x), ("xt", self.x, self.qs)):
                    job = self.level_jobs[l, g, which]
                    begin(pe, job)
                    for h in range(A_HEADS):
                        mm = pe.matmul(job.ap[:, h * P:(h + 1) * P], left[:, g, h, :], right[:, g, h, :],
                                       start=True, stop=True)
                    mm.then_inc(job.full[0], 1)
        for g in range(4):
            pe.wait_ge(*self.rhs[g])
            begin(pe, self.w_jobs[g])
            for h in range(A_HEADS):
                mm = pe.matmul(self.w_jobs[g].ap[:, h * P:(h + 1) * P], self.l[:, g, h, :], self.xt[:, g, h, :],
                               start=True, stop=True)
            mm.then_inc(self.w_jobs[g].full[0], 1)
            begin(pe, self.u_jobs[g])
            for h in range(A_HEADS):
                mm = pe.matmul(self.u_jobs[g].ap[:, h * P:(h + 1) * P], self.xt[:, g, h, :], self.x[:, g, h, :],
                               start=True, stop=True)
            mm.then_inc(self.u_jobs[g].full[0], 1)
        if s == 1:
            for g, (d, t) in enumerate(self.groups):
                begin(pe, self.kq_jobs[g])
                for h in range(A_HEADS):
                    mm = pe.matmul(self.kq_jobs[g].ap[:, h * P:(h + 1) * P],
                                   self.kf[:, h, T + t * P:T + (t + 1) * P], self.qf[:, h, t * P:(t + 1) * P],
                                   start=True, stop=True)
                mm.then_inc(self.kq_jobs[g].full[0], 1)
        for i, (step, d, t) in enumerate(self.steps):
            g = d * TT + t
            if self.ws_jobs[i] is not None:
                begin(pe, self.ws_jobs[i])
                pe.wait_ge(*self.w_ready[g])
                if i >= 2:
                    pe.wait_ge(*self.s_new[i - 2])
                for h in range(A_HEADS):
                    mm = pe.matmul(self.ws_jobs[i].ap[:, h * P:(h + 1) * P], self.qs[:, g, h, :],
                                   self.state[:, self.state_of(step), d * 4 + h, :], start=True, stop=True)
                mm.then_inc(self.ws_jobs[i].full[0], 1)
            if self.kv_jobs[i] is not None:
                begin(pe, self.kv_jobs[i])
                pe.wait_ge(*self.v_new[i])
                pe.wait_ge(*self.tail_ready[g])
                for h in range(A_HEADS):
                    mm = pe.matmul(self.kv_jobs[i].ap[:, h * P:(h + 1) * P], self.l[:, g, h, :], self.x[:, g, h, :],
                                   start=True, stop=True)
                mm.then_inc(self.kv_jobs[i].full[0], 1)
        if s == 1:
            pe.wait_ge(*self.v_new[3])
            for t in range(TT):
                begin(pe, self.out_jobs[t])
                for h in range(A_HEADS):
                    out = self.out_jobs[t].ap[:, h * P:(h + 1) * P]
                    for d in range(DIRS):
                        g, step = d * TT + t, (t if d == 0 else 1 - t)
                        if h == 0:
                            pe.wait_ge(*self.qd_ready[g])
                            pe.wait_ge(*self.intra_ready[g])
                        pe.matmul(out, self.state[:, step, d * 4 + h, :], self.gb[:, g, h, :],
                                  start=(d == 0), stop=False)
                        mm = pe.matmul(out, self.x[:, g, h, :], self.xt[:, g, h, :], start=False, stop=(d == 1))
                mm.then_inc(self.out_jobs[t].full[0], 1)

    def state_of(self, step):
        return step if self.seq == 1 else 0

    def scalar(self, act):
        k, s = self.k, self.seq

        def banked(job):
            return job.ap[:, :].rearrange("p (h c) -> p h c", c=P)

        for i, job in enumerate(self.tok_jobs):
            act.wait_ge(*job.full)
            dst = (self.kt, self.vt)[i // 2][:, i % 2, :, :]
            act.activation(dst, banked(job), ACT.Identity).then_inc(self.tok_ready[i][0], 1)
        for g in range(4):
            act.wait_ge(*self.gb_jobs[g].full)
            act.activation(self.gb[:, g, :, :], banked(self.gb_jobs[g]), ACT.Identity)\
               .then_inc(self.gb_ready[g][0], 1)
        for g in range(4):
            act.wait_ge(*self.diff[g])
            act.activation(self.l[:, g, :, :], self.l[:, g, :, :], ACT.Exp, scale=-1.0).then_inc(self.decay[g][0], 1)
        for l in range(len(LEVELS)):
            for g in range(4):
                n = 4 * l + g
                job = self.level_jobs[l, g, "q"]
                act.wait_ge(*job.full)
                if l > 0:
                    act.wait_ge(*self.level_jobs[l - 1, g, "xt"].full)
                act.activation(self.qs[:, g, :, :], banked(job), ACT.Identity).then_inc(self.q_ready[n][0], 1)
                if g % 2:
                    k.background.take(act, 1)
        for g in range(4):
            act.wait_ge(*self.w_jobs[g].full)
            act.wait_ge(*self.level_jobs[len(LEVELS) - 1, g, "xt"].full)
            act.activation(self.qs[:, g, :, :], banked(self.w_jobs[g]), ACT.Copy, scale=-1.0)\
               .then_inc(self.w_ready[g][0], 1)
            act.wait_ge(*self.u_jobs[g].full)
            act.activation(self.x[:, g, :, :], banked(self.u_jobs[g]), ACT.Identity).then_inc(self.u_ready[g][0], 1)
        act.wait_ge(*self.tail_diff)
        k.act.link(act.activation(k.cols[:, C_TAIL, 0:16], k.cols[:, C_TAIL, 0:16], ACT.Exp))
        act.activation(k.cols[:, C_LAST, 0:16], k.cols[:, C_LAST, 0:16], ACT.Exp).then_inc(self.tail_exp[0], 1)
        if s == 1:
            for g in range(4):
                act.wait_ge(*self.intra_diff[g])
                act.activation(self.xt[:, g, :, :], self.xt[:, g, :, :], ACT.Exp).then_inc(self.intra_exp[g][0], 1)
                act.activation(self.gb[:, g, :, :], self.gb[:, g, :, :], ACT.Exp).then_inc(self.qd_exp[g][0], 1)

    def vector(self, dve):
        k, s, chain = self.k, self.seq, self.k.dve

        def banked(job):
            return job.ap[:, :].rearrange("p (h c) -> p h c", c=P)

        def col(row, g, h):
            d, t = self.groups[g]
            at = (s * TT + t) * 8 + d * 4 + h
            return k.cols[:, row, at:at + 1]

        def four(mask):
            return mask.unsqueeze(1).broadcast_to([P, A_HEADS, P])

        for g in range(4):
            dve.wait_ge(*self.gb_ready[g])
            for h in range(A_HEADS):
                ins = dve.tensor_scalar(self.l[:, g, h, :], self.gb[:, g, h, :], col(C_GC, g, h), 0.0,
                                        ALU.subtract, ALU.max)
            ins.then_inc(self.diff[g][0], 1)
        for g in range(4):
            dve.wait_ge(*self.decay[g])
            dve.wait_ge(*self.kk_jobs[g].full)
            for h in range(A_HEADS):
                ins = dve.scalar_tensor_tensor(self.l[:, g, h, :], self.kk_jobs[g].ap[:, h * P:(h + 1) * P],
                                               col(C_BETA, g, h), self.l[:, g, h, :], ALU.mult, ALU.mult)
            ins.then_inc(self.l_ready[g][0], 1)
            for x in (self.x, self.xt):
                ins = dve.tensor_copy(x[:, g, :, :], four(k.c("ident")))
            chain.link(ins)
            dve.wait_ge(*self.l_ready[g])

        def mask(l, g):
            d = self.groups[g][0]
            if 4 * l + g >= 2:
                m = 4 * l + g - 2
                dve.wait_ge(*self.level_jobs[m // 4, m % 4, "q"].full)
            pairs = k.c(("lower_pairs", "upper_pairs")[d], l * P, P)
            dve.tensor_tensor(self.lm[:, g % 2, :, :], self.l[:, g, :, :], four(pairs), ALU.mult)\
               .then_inc(self.masked[4 * l + g][0], 1)

        mask(0, 0)
        mask(0, 1)
        for l in range(len(LEVELS)):
            mask(l, 2)
            mask(l, 3)
            for g in range(4):
                for which, x, ready in (("x", self.x, self.x_ready), ("xt", self.xt, self.xt_ready)):
                    job = self.level_jobs[l, g, which]
                    dve.wait_ge(*job.full)
                    if which == "x":
                        dve.wait_ge(*self.level_jobs[l, g, "xt"].full)
                    dve.tensor_tensor(x[:, g, :, :], x[:, g, :, :], banked(job), ALU.subtract)\
                       .then_inc(ready[4 * l + g][0], 1)
                if g >= 2 and l + 1 < len(LEVELS):
                    mask(l + 1, g - 2)
        dve.wait_ge(*self.xt_ready[-1])
        for i in range(4):
            dve.wait_ge(*self.tok_ready[i])
        for g, (d, t) in enumerate(self.groups):
            for h in range(A_HEADS):
                dve.tensor_scalar(self.l[:, g, h, :], self.kt[:, t, h, :], col(C_BEG, g, h), None, ALU.mult)
                ins = dve.tensor_scalar(self.x[:, g, h, :], self.vt[:, t, h, :], col(C_BETA, g, h), None, ALU.mult)
            ins.then_inc(self.rhs[g][0], 1)
        for g, (d, t) in enumerate(self.groups):
            last = (P - 1) * (1 - d)
            at = (s * TT + t) * 8 + d * 4
            dve.tensor_tensor(k.cols[:, C_TAIL, g * 4:g * 4 + 4], self.gb[:, g, :, last],
                              k.cols[:, C_GC, at:at + 4], ALU.subtract)
            ins = dve.tensor_copy(k.cols[:, C_LAST, g * 4:g * 4 + 4], self.gb[:, g, :, last])
        ins.then_inc(self.tail_diff[0], 1)
        dve.wait_ge(*self.tail_exp)
        for g, (d, t) in enumerate(self.groups):
            dve.wait_ge(*self.w_jobs[g].full)
            for h in range(A_HEADS):
                ins = dve.tensor_scalar(self.l[:, g, h, :], self.kt[:, t, h, :],
                                        k.cols[:, C_TAIL, g * 4 + h:g * 4 + h + 1], None, ALU.mult)
            ins.then_inc(self.tail_ready[g][0], 1)
        if s == 1:
            for g, (d, t) in enumerate(self.groups):
                dve.wait_ge(*self.u_jobs[g].full)
                for h in range(A_HEADS):
                    ins = dve.tensor_scalar(self.xt[:, g, h, :], self.gb[:, g, h, :], col(C_GC, g, h), 0.0,
                                            ALU.subtract, ALU.min)
                ins.then_inc(self.intra_diff[g][0], 1)
            for g, (d, t) in enumerate(self.groups):
                dve.wait_ge(*self.intra_exp[g])
                chain.link(dve.tensor_tensor(self.xt[:, g, :, :], self.xt[:, g, :, :],
                                             four(k.c(("upto", "from_")[d])), ALU.mult))
                dve.wait_ge(*self.kq_jobs[g].full)
                dve.tensor_tensor(self.xt[:, g, :, :], self.xt[:, g, :, :], banked(self.kq_jobs[g]), ALU.mult)\
                   .then_inc(self.intra_ready[g][0], 1)
                dve.wait_ge(*self.qd_exp[g])
                dve.tensor_tensor(self.gb[:, g, :, :], self.gb[:, g, :, :], self.qf[:, :, t * P:(t + 1) * P],
                                  ALU.mult).then_inc(self.qd_ready[g][0], 1)
        for i, (step, d, t) in enumerate(self.steps):
            g = d * TT + t
            dve.wait_ge(*self.u_ready[g])
            if self.ws_jobs[i] is not None:
                dve.wait_ge(*self.ws_jobs[i].full)
                ins = dve.tensor_tensor(self.x[:, g, :, :], self.x[:, g, :, :], banked(self.ws_jobs[i]), ALU.add)
            else:
                ins = dve.tensor_copy(k.cols[:, 10, 0:1], k.cols[:, C_LAST, 0:1])
            ins.then_inc(self.v_new[i][0], 1)
            dve.wait_ge(*self.v_new[i])
            if self.kv_jobs[i] is not None:
                dve.wait_ge(*self.kv_jobs[i].full)
                if i >= 2:
                    dve.wait_ge(*self.s_new[i - 2])
                src = self.state_of(step)
                dst = 0 if s == 0 else step + 1
                for h in range(A_HEADS):
                    ps = self.kv_jobs[i].ap[:, h * P:(h + 1) * P]
                    out = self.state[:, dst, d * 4 + h, :]
                    if self.ws_jobs[i] is None:
                        ins = dve.tensor_copy(out, ps)
                    else:
                        ins = dve.scalar_tensor_tensor(out, self.state[:, src, d * 4 + h, :],
                                                       k.cols[:, C_LAST, g * 4 + h:g * 4 + h + 1], ps,
                                                       ALU.mult, ALU.add)
                ins.then_inc(self.s_new[i][0], 1)


class DeltaReadout(Stage):

    def __init__(self, core, delta):
        self.delta = delta
        super().__init__(core)

    def setup(self):
        k = self.k
        self.copied = k.counter("readout_copied").events(TT)
        self.squared = k.counter("readout_squared").events(TT)
        self.o = k.area(H_K, TT, A_HEADS, P)
        self.sq = k.area(H_V, TT, A_HEADS, P)
        self.jobs = k.take(TT)
        self.root = k.counter("readout_root").events(TT)
        self.ready = k.counter("readout_ready").events(TT)

    def tensor(self, pe):
        for t in range(TT):
            begin(pe, self.jobs[t])
            pe.wait_ge(*self.squared[t])
            pe.matmul(self.jobs[t].ap[:, :], self.k.c("ones"), self.sq[:, t, :, :].rearrange("p h c -> p (h c)"),
                      start=True, stop=True).then_inc(self.jobs[t].full[0], 1)

    def scalar(self, act):
        for t in range(TT):
            job = self.delta.out_jobs[t]
            act.wait_ge(*job.full)
            act.activation(self.o[:, t, :, :].rearrange("p h c -> p (h c)"), job.ap[:, :], ACT.Identity)\
               .then_inc(self.copied[t][0], 1)
            act.activation(self.sq[:, t, :, :].rearrange("p h c -> p (h c)"), job.ap[:, :], ACT.Square)\
               .then_inc(self.squared[t][0], 1)
            act.wait_ge(*self.squared[t])
            act.wait_ge(*self.jobs[t].full)
            flat = self.sq[:, t, :, :].rearrange("p h c -> p (h c)")
            act.activation(flat, self.jobs[t].ap[:, :], ACT.Ln, bias=self.k.eps[:, 0:1], scale=1.0 / P)\
               .then_inc(self.jobs[t].free[0], 1)
            act.wait_ge(*self.jobs[t].free)
            act.activation(flat, flat, ACT.Exp, scale=-0.5).then_inc(self.root[t][0], 1)

    def vector(self, dve):
        k = self.k
        z = k.area(H_Z, A_HEADS, T)
        mix = k.area(H_MIX, KC, T)
        for t in range(TT):
            dve.wait_ge(*self.root[t])
            dve.wait_ge(*self.copied[t])
            dve.tensor_copy(k.cols[:, 10, 1:2], k.cols[:, C_LAST, 0:1]).then_inc(self.delta.out_jobs[t].free[0], 1)
            k.dve.link(dve.scalar_tensor_tensor(self.o[:, t, :, :], self.o[:, t, :, :], k.v("hyb_out_norm"),
                                                self.sq[:, t, :, :], ALU.mult, ALU.mult))
            dve.tensor_tensor(mix[:, 0:A_HEADS, t * P:(t + 1) * P], self.o[:, t, :, :],
                              z[:, :, t * P:(t + 1) * P], ALU.mult).then_inc(self.ready[t][0], 1)
        dve.wait_ge(*self.ready[-1])


class BackgroundEnd(Stage):

    def tensor(self, pe):
        self.k.background.finish(pe)

    def vector(self, dve):
        self.k.background.vector(dve)

    def scalar(self, act):
        self.k.background.take(act, 2 * len(self.k.background.work))


def hybrid(k):
    background = BackgroundModulation(k)
    k.weights.reserve(MOD_EARLY, False)
    projection = HybridProjection(k)
    k.weights.reserve(len(background.work) - MOD_EARLY, False)
    stages = [projection, HybridAttention(k), DeltaColumns(k), Delta(k, 0), Delta(k, 1)]
    stages += [DeltaReadout(k, stages[-1]), BackgroundEnd(k)]
    mix_ready = [stages[-2].ready[-1]] * A_HEADS + [k.attention_out[-1]] * B_PAIRS
    return stages + [OutProjection(k, k.area(H_MIX, KC, T), mix_ready, KC, rms_gain=k.coef[:, 2, :])]


MIXERS["hybrid"] = hybrid


F_U = AT_HID
F_C = F_U + KC * (T + 2 * PAD_C)
F_G = F_C + KC * T


POOL_TAPS = 7


class ConformerIn(Stage):

    def __init__(self, core, x, x_ready):
        self.x, self.x_ready = x, x_ready
        super().__init__(core)

    def setup(self):
        k = self.k
        self.u = k.area(F_U, KC, T + 2 * PAD_C)
        self.conv = k.area(F_C, KC, T)
        self.gate = k.area(F_G, 2, T)
        k.weights.reserve(KC, False)
        self.odd = k.area(F_G + 2 * T, T)
        self.pool_sum = k.area(F_G + 3 * T, 2, T)
        self.tap = k.area(F_G + 5 * T, 2, T)
        self.pool_ready = k.counter("pool_conv").events(KC)
        self.edges = k.counter("pad_clear").event()
        self.gated = k.counter("conf_gate").events(KC)
        self.ready = k.counter("conf_u").events(KC)
        self.conv_ready = k.counter("convolved").events(KC)
        self.jobs = [k.job(e) for e in self.ready]

    def tensor(self, pe):
        k = self.k
        for j, job in enumerate(self.jobs):
            begin(pe, job)
            slab = k.weights.next(pe)[0].rearrange("p (k c) -> p k c", k=KC)
            for half in range(2):
                for c in range(KC):
                    if j == 0:
                        pe.wait_ge(*self.x_ready[c])
                    mm = k.weights.matmul(pe, job.ap[:, half * T:(half + 1) * T],
                                          slab[:, c, half * P:(half + 1) * P], self.x[:, c, :],
                                          start=(c == 0), stop=(c == KC - 1))
            mm.then_inc(job.full[0], 1)

    def scalar(self, act):
        k = self.k
        for j, job in enumerate(self.jobs):
            act.wait_ge(*job.full)
            if j >= 2:
                act.wait_ge(*self.ready[j - 2])
            act.activation(self.gate[:, j % 2, :], job.ap[:, T:2 * T], ACT.Sigmoid,
                           bias=k.v("conf_b_in", KC + j)).then_inc(self.gated[j][0], 1)

    def gpsimd(self, pool):
        k = self.k
        for c in range(KC):
            pool.wait_ge(*self.ready[c])
            if c >= 2:
                pool.wait_ge(*self.conv_ready[c - 2])
            acc = self.pool_sum[:, c % 2, :]
            for i in range(POOL_TAPS):
                j = CONV_C - POOL_TAPS + i
                src, w = self.u[:, c, j:j + T], k.v("conf_dw_w", j * KC + c).broadcast_to([P, T])
                if i == 0:
                    k.pool.step(pool.tensor_tensor(acc, src, w, ALU.mult), behind=1)
                else:
                    tap = self.tap[:, i % 2, :]
                    k.pool.link(pool.tensor_tensor(tap, src, w, ALU.mult))
                    ins = pool.tensor_tensor(acc, acc, tap, ALU.add)
                    if i < POOL_TAPS - 1:
                        k.pool.step(ins, behind=1)
            ins.then_inc(self.pool_ready[c][0], 1)

    def vector(self, dve):
        k = self.k
        dve.memset(self.u[:, :, 0:PAD_C], 0.0)
        dve.memset(self.u[:, :, PAD_C + T:], 0.0).then_inc(self.edges[0], 1)
        dve.wait_ge(*self.edges)
        for c in range(KC):
            job = self.jobs[c]
            dve.wait_ge(*self.gated[c])
            dve.scalar_tensor_tensor(self.u[:, c, PAD_C:PAD_C + T], job.ap[:, 0:T], k.v("conf_b_in", c),
                                     self.gate[:, c % 2, :], ALU.add, ALU.mult).then_inc(self.ready[c][0], 1)
            dve.wait_ge(*self.ready[c])
            sums = (self.conv[:, c, :], self.odd)
            for j in range(CONV_C - POOL_TAPS):
                w = k.v("conf_dw_w", j * KC + c)
                src, acc = self.u[:, c, j:j + T], sums[j % 2]
                if j == 0:
                    ins = dve.tensor_scalar(acc, src, w, k.v("conf_dw_b", c), ALU.mult, ALU.add)
                elif j == 1:
                    ins = dve.tensor_scalar(acc, src, w, None, ALU.mult)
                else:
                    ins = dve.scalar_tensor_tensor(acc, src, w, acc, ALU.mult, ALU.add)
                k.dve.step(ins, behind=0 if j == CONV_C - POOL_TAPS - 1 else 1)
            k.dve.link(dve.tensor_tensor(sums[0], sums[0], sums[1], ALU.add))
            dve.wait_ge(*self.pool_ready[c])
            dve.tensor_tensor(sums[0], sums[0], self.pool_sum[:, c % 2, :], ALU.add)\
               .then_inc(self.conv_ready[c][0], 1)
            dve.wait_ge(*self.conv_ready[c])


class ConformerNorm(Stage):

    def __init__(self, core, x, x_ready):
        self.x, self.x_ready = x, x_ready
        super().__init__(core)

    def setup(self):
        k = self.k
        self.sq, self.rs = k.area(AT_SQ, KC, T), k.area(AT_RS, T)
        self.mean_job = k.job()
        self.var_job = k.job()
        self.centred = k.counter("centred").event()
        self.squared = k.counter("squared").events(KC)
        self.root = k.counter("root_ready").event()
        self.scaled = k.counter("norm_scaled").event()
        self.ready = k.counter("conf_act").events(KC)
        self.root_free, k.root_free = k.root_free, self.scaled

    def tensor(self, pe):
        for job, src, ready in ((self.mean_job, self.x, self.x_ready), (self.var_job, self.sq, self.squared)):
            begin(pe, job)
            for c in range(KC):
                pe.wait_ge(*ready[c])
                mm = pe.matmul(job.ap[:, 0:T], self.k.c("mean"), src[:, c, :], start=(c == 0), stop=(c == KC - 1))
            mm.then_inc(job.full[0], 1)

    def scalar(self, act):
        k = self.k
        act.wait_ge(*self.centred)
        for c in range(KC):
            act.activation(self.sq[:, c, :], self.x[:, c, :], ACT.Square).then_inc(self.squared[c][0], 1)
        act.wait_ge(*self.var_job.full)
        root_inverse(act, k.act, self.rs, self.var_job.ap[:, 0:T], k.eps[:, 0:1], self.var_job.free)\
            .then_inc(self.root[0], 1)
        act.wait_ge(*self.scaled)
        for c in range(KC):
            act.activation(self.x[:, c, :], self.x[:, c, :], ACT.Silu, bias=k.v("conf_ln_b", c),
                           scale=k.v("conf_ln_g", c)).then_inc(self.ready[c][0], 1)

    def vector(self, dve):
        dve.wait_ge(*self.mean_job.full)
        for c in range(KC):
            dve.wait_ge(*self.x_ready[c])
        dve.tensor_copy(self.rs, self.mean_job.ap[:, 0:T]).then_inc(self.mean_job.free[0], 1)
        dve.wait_ge(*self.mean_job.free)
        dve.tensor_tensor(self.x, self.x, over_chunks(self.rs, KC), ALU.subtract).then_inc(self.centred[0], 1)
        dve.wait_ge(*self.root)
        dve.tensor_tensor(self.x, self.x, over_chunks(self.rs, KC), ALU.mult).then_inc(self.scaled[0], 1)


def conformer(k):
    a = k.area(AT_A, KC, T)
    pre = PreNorm(k, k.h[:, :, :], k.h_ready, a, k.coef[:, 0, :], k.mod[:, 0:KC, 0])
    conv = ConformerIn(k, a, pre.ready)
    norm = ConformerNorm(k, conv.conv, conv.conv_ready)
    return [pre, conv, norm, OutProjection(k, conv.conv, norm.ready, KC, rms_gain=k.coef[:, 2, :],
                                           bias=k.v("conf_b_out", 0, KC))]


MIXERS["conformer"] = conformer


M_OUT = AT_A
M_Q = AT_HID
M_K = M_Q + KC * T
M_B = M_K + KC * T
M_V = M_B + KC * T
M_G = M_V + TT * D
M_E = M_G + KC * T
M_ATT = M_E + 2 * KC * T


def project_columns(k, pe, x, x_ready, jobs):
    for j, job in enumerate(jobs):
        begin(pe, job)
        slab = [s.rearrange("p (k c) -> p k c", k=KC) for s in k.weights.next(pe)]
        for half in range(2):
            for c in range(KC):
                if j == 0:
                    pe.wait_ge(*x_ready[c])
                mm = k.weights.product(pe, job.ap[:, half * T:(half + 1) * T],
                                       [s[:, c, half * P:(half + 1) * P] for s in slab],
                                       [part[:, c, :] for part in x], c == 0, c == KC - 1)
        mm.then_inc(job.full[0], 1)


def project_tokens(k, pe, x, jobs):
    for job in jobs:
        begin(pe, job)
        slab = [s.rearrange("p (k c) -> p k c", k=KC) for s in k.weights.next(pe)]
        for t in range(TT):
            for c in range(KC):
                mm = k.weights.product(pe, job.ap[:, t * 256:(t + 1) * 256],
                                       [part[:, c, t * P:(t + 1) * P] for part in x],
                                       [s[:, c, :] for s in slab], c == 0, c == KC - 1)
        mm.then_inc(job.full[0], 1)


def pair(job):
    return job.ap[:, :].rearrange("p (a t) -> p a t", a=2)


class HgrnIn(Stage):

    def __init__(self, core, layer):
        self.layer = layer
        super().__init__(core)

    def setup(self):
        k = self.k
        self.x_ready = k.parts_ready
        self.slab0 = k.weights.reserve(16, True)
        self.q, self.kk, self.b = (k.area(at, KC, T) for at in (M_Q, M_K, M_B))
        self.v, self.g = k.area(M_V, TT, D), k.area(M_G, KC, T)
        self.raw, self.soft = k.area(M_E, KC, T), k.area(M_E + KC * T, KC, T)
        self.q_ready = k.counter("mixer_q").events(4)
        self.f_taken = k.counter("forget_taken").events(4)
        self.v_ready = k.counter("mixer_v").events(4)
        self.g_ready = k.counter("mixer_g").events(4)
        self.jobs = [k.job(e) for e in self.q_ready + self.f_taken + self.v_ready + self.g_ready]
        if self.layer:
            self.bound_shift = k.counter("bound_shift").event()
            self.bound_log = k.counter("bound_log").event()
            self.bound_sums = k.counter("bound_sums").event()
            self.bound_exp = k.counter("bound_exp").event()
            self.bound = k.counter("bound_ready").event()
            self.dist = k.counter("log_distance").event()
            self.log_sum = k.counter("log_sum").event()
        self.k_exp = k.counter("k_sigmoid").event()
        self.log1p = k.counter("log1p_ready").event()
        self.ready = k.counter("decay_cumulated").event()
        self.small = k.cols[:, :, :].rearrange("p a b -> p (a b)")

    def tensor(self, pe):
        k = self.k
        x = k.x_parts[:, 0], k.x_parts[:, 1]
        project_columns(k, pe, x, self.x_ready, self.jobs[0:8])
        project_tokens(k, pe, x, self.jobs[8:12])
        project_columns(k, pe, x, self.x_ready, self.jobs[12:16])

    def scalar(self, act):
        k = self.k

        def round_to(n):
            k.weights.round_through(act, self.slab0 + n)

        if self.layer:
            act.wait_ge(*self.bound_shift)
            act.activation(self.small[:, 0:56], self.small[:, 0:56], ACT.Exp).then_inc(self.bound_exp[0], 1)
            act.wait_ge(*self.bound_sums)
            act.activation(self.small[:, 56:72], self.small[:, 56:72], ACT.Ln).then_inc(self.bound_log[0], 1)
        for j in range(4):
            round_to(j + 1)
            act.wait_ge(*self.jobs[j].full)
            act.activation(self.q[:, 2 * j:2 * j + 2, :], pair(self.jobs[j]), ACT.Silu).then_inc(self.q_ready[j][0], 1)
        for j in range(4):
            round_to(4 + j + 1)
            act.wait_ge(*self.jobs[4 + j].full)
            act.activation(self.raw[:, 2 * j:2 * j + 2, :], pair(self.jobs[4 + j]), ACT.Identity)\
               .then_inc(self.f_taken[j][0], 1)
            act.wait_ge(*self.f_taken[j])
        k.act.link(act.activation(self.kk, self.raw, ACT.Sigmoid, scale=-1.0))
        round_to(9)
        k.act.link(act.activation(self.soft, self.raw, ACT.Abs))
        k.act.link(act.activation(self.soft, self.soft, ACT.Exp, scale=-1.0))
        round_to(10)
        act.activation(self.soft, self.soft, ACT.Ln, bias=k.eps[:, 2:3]).then_inc(self.log1p[0], 1)
        round_to(11)
        if self.layer:
            act.wait_ge(*self.dist)
            k.act.link(act.activation(self.soft, self.soft, ACT.Abs))
            k.act.link(act.activation(self.soft, self.soft, ACT.Exp, scale=-1.0))
            round_to(12)
            act.activation(self.soft, self.soft, ACT.Ln, bias=k.eps[:, 2:3]).then_inc(self.log_sum[0], 1)
        for j in range(4):
            round_to(8 + j + 1)
            act.wait_ge(*self.jobs[8 + j].full)
            act.activation(self.v[:, :, j * 256:(j + 1) * 256], pair(self.jobs[8 + j]), ACT.Identity)\
               .then_inc(self.v_ready[j][0], 1)
        for j in range(4):
            round_to(12 + j + 1)
            act.wait_ge(*self.jobs[12 + j].full)
            act.activation(self.g[:, 2 * j:2 * j + 2, :], pair(self.jobs[12 + j]), ACT.Silu)\
               .then_inc(self.g_ready[j][0], 1)

    def vector(self, dve):
        k, chain = self.k, self.k.dve
        s = self.small
        logits = [k.v("lb_logits", i * KC, KC) for i in range(4)]
        if self.layer:
            most, rest = s[:, 72:80], s[:, 80:88]
            chain.link(dve.tensor_tensor(rest, logits[1], logits[2], ALU.max))
            chain.link(dve.tensor_tensor(rest, rest, logits[3], ALU.max))
            chain.link(dve.tensor_tensor(most, rest, logits[0], ALU.max))
            for i in range(4):
                ins = dve.tensor_tensor(s[:, i * 8:i * 8 + 8], logits[i], most, ALU.subtract)
            for i in range(1, 4):
                ins = dve.tensor_tensor(s[:, 24 + i * 8:32 + i * 8], logits[i], rest, ALU.subtract)
            ins.then_inc(self.bound_shift[0], 1)
            dve.wait_ge(*self.bound_exp)
            chain.link(dve.tensor_tensor(s[:, 56:64], s[:, 0:8], s[:, 8:16], ALU.add))
            chain.link(dve.tensor_tensor(s[:, 56:64], s[:, 56:64], s[:, 16:24], ALU.add))
            chain.link(dve.tensor_tensor(s[:, 56:64], s[:, 56:64], s[:, 24:32], ALU.add))
            chain.link(dve.reciprocal(s[:, 88:96], s[:, 56:64]))
            chain.link(dve.tensor_tensor(s[:, 64:72], s[:, 32:40], s[:, 40:48], ALU.add))
            dve.tensor_tensor(s[:, 64:72], s[:, 64:72], s[:, 48:56], ALU.add).then_inc(self.bound_sums[0], 1)
            dve.wait_ge(*self.bound_log)
            chain.link(dve.tensor_tensor(s[:, 96:104], s[:, 0:8], s[:, 88:96], ALU.mult))
            chain.link(dve.tensor_tensor(most, most, s[:, 56:64], ALU.add))
            chain.link(dve.tensor_tensor(rest, rest, s[:, 64:72], ALU.add))
            chain.link(dve.tensor_tensor(s[:, 104:112], logits[0], most, ALU.subtract))
            dve.tensor_tensor(s[:, 112:120], rest, most, ALU.subtract).then_inc(self.bound[0], 1)
            dve.wait_ge(*self.bound)
        def split_to(n):
            k.weights.split_through(dve, self.slab0 + n)

        split_to(10)
        dve.wait_ge(*self.log1p)
        chain.link(dve.tensor_scalar(self.raw, self.raw, 0.0, None, ALU.min))
        chain.link(dve.tensor_tensor(self.raw, self.raw, self.soft, ALU.subtract))
        split_to(11)
        if self.layer:
            for c in range(KC):
                ins = dve.tensor_scalar(self.raw[:, c, :], self.raw[:, c, :], s[:, 104 + c:105 + c], None, ALU.add)
                dve.tensor_scalar(self.kk[:, c, :], self.kk[:, c, :], s[:, 96 + c:97 + c], None, ALU.mult)
            chain.link(ins)
            for c in range(KC):
                ins = dve.tensor_scalar(self.soft[:, c, :], self.raw[:, c, :], s[:, 112 + c:113 + c], None,
                                        ALU.subtract)
            ins.then_inc(self.dist[0], 1)
            dve.wait_ge(*self.dist)
            for c in range(KC):
                ins = dve.tensor_scalar(self.raw[:, c, :], self.raw[:, c, :], s[:, 112 + c:113 + c], None, ALU.max)
            chain.link(ins)
            split_to(12)
            dve.wait_ge(*self.log_sum)
            chain.link(dve.tensor_tensor(self.raw, self.raw, self.soft, ALU.add))
        for c in range(KC):
            if c == KC // 2:
                split_to(13)
            ins = dve.tensor_tensor_scan(self.b[:, c, :], k.c("one_row"), self.raw[:, c, :], 0.0, ALU.mult, ALU.add)
        ins.then_inc(self.ready[0], 1)
        dve.wait_ge(*self.ready)
        split_to(16)


H_LEVELS = [128] + LEVELS[::-1] + [0]


class HgrnAttention(Stage):

    def __init__(self, core, src):
        self.src = src
        super().__init__(core)

    def setup(self):
        k = self.k
        n = len(H_LEVELS)
        self.e = k.area(M_E, 2, KC * T)
        self.att = k.area(M_ATT, HEADS, 3, P)
        self.cleared = k.counter("att_cleared").event()
        self.diff = k.counter("pair_exponents").events(n - 1)
        self.exp = k.counter("pair_exp").events(n - 1)
        self.e_ready = k.counter("pair_operands").events(n)
        self.jobs = []
        self.taken = k.counter("pairs_taken").events(2 + 4 * (n - 1))
        for l in range(n):
            at = 0 if l == 0 else 2 + 4 * (l - 1)
            self.jobs.append([k.job(e) for e in self.taken[at:at + (2 if l == 0 else 4)]])
        self.out_ready = k.counter("mixer_out_copied").events(4)
        self.sq_ready = k.counter("mixer_out_squared").events(4)
        self.out_jobs = [k.job(e) for e in self.sq_ready]
        self.sum_jobs = k.take(4)
        self.root = k.counter("mixer_root").events(4)
        self.ready = k.counter("mixer_ready").events(4)

    def tensor(self, pe):
        k = self.k
        q, kk = self.src.q, self.src.kk
        for l, b in enumerate(H_LEVELS):
            e = self.e[:, l % 2, :].rearrange("p (h t) -> p h t", h=HEADS)
            pe.wait_ge(*self.e_ready[l])
            if l == 0:
                for j, job in enumerate(self.jobs[0]):
                    begin(pe, job)
                    for i in range(4):
                        h = 4 * j + i
                        mm = pe.matmul(job.ap[:, i * P:(i + 1) * P], e[:, h, 0:P], e[:, h, P:T], start=True, stop=True)
                    mm.then_inc(job.full[0], 1)
                continue
            for j, job in enumerate(self.jobs[l]):
                begin(pe, job)
                t = j % 2
                cols = slice(t * P, (t + 1) * P)
                for i in range(4):
                    h = 4 * (j // 2) + i
                    left, right = (e, e) if b else (kk, q)
                    mm = pe.matmul(job.ap[:, i * P:(i + 1) * P], left[:, h, cols], right[:, h, cols],
                                   start=True, stop=True)
                mm.then_inc(job.full[0], 1)
        pe.wait_ge(*self.taken[-1])
        v = self.src.v
        pe.wait_ge(*self.src.v_ready[-1])
        for j, job in enumerate(self.out_jobs):
            begin(pe, job)
            for i in range(2):
                h = 2 * j + i
                pe.matmul(job.ap[:, i * T:(i + 1) * T], v[:, 0, h * P:(h + 1) * P], self.att[:, h, 0:2, :],
                          start=True, stop=False)
                mm = pe.matmul(job.ap[:, i * T + P:(i + 1) * T], v[:, 1, h * P:(h + 1) * P], self.att[:, h, 2, :],
                               start=False, stop=True)
            mm.then_inc(job.full[0], 1)
        for j, job in enumerate(self.sum_jobs):
            begin(pe, job)
            pe.wait_ge(*self.sq_ready[j])
            pe.matmul(job.ap[:, :], k.c("ones"), self.e[:, 0, j * 512:(j + 1) * 512], start=True, stop=True)\
              .then_inc(job.full[0], 1)

    def scalar(self, act):
        k = self.k
        for l in range(len(H_LEVELS) - 1):
            act.wait_ge(*self.diff[l])
            act.activation(self.e[:, l % 2, :], self.e[:, l % 2, :], ACT.Exp).then_inc(self.exp[l][0], 1)
        out = k.area(M_OUT, KC, T)
        sq = self.e[:, 0, :].rearrange("p (c t) -> p c t", t=T)
        for j, job in enumerate(self.out_jobs):
            act.wait_ge(*job.full)
            act.activation(out[:, 2 * j:2 * j + 2, :], pair(job), ACT.Identity).then_inc(self.out_ready[j][0], 1)
            act.activation(sq[:, 2 * j:2 * j + 2, :], pair(job), ACT.Square).then_inc(self.sq_ready[j][0], 1)
        for j, job in enumerate(self.sum_jobs):
            act.wait_ge(*job.full)
            flat = self.e[:, 0, j * 512:(j + 1) * 512]
            act.activation(flat, job.ap[:, :], ACT.Ln, bias=k.eps[:, 0:1], scale=1.0 / P).then_inc(job.free[0], 1)
        for j, job in enumerate(self.sum_jobs):
            act.wait_ge(*job.free)
            flat = self.e[:, 0, j * 512:(j + 1) * 512]
            act.activation(flat, flat, ACT.Exp, scale=-0.5).then_inc(self.root[j][0], 1)

    def gpsimd(self, pool):
        pool.wait_ge(*self.src.x_ready[-1])
        pool.memset(self.att, 0.0).then_inc(self.cleared[0], 1)

    def vector(self, dve):
        k, chain = self.k, self.k.dve
        b_all = k.area(M_B, KC * T)
        q_all, k_all = k.area(M_Q, KC * T), k.area(M_K, KC * T)
        for e in self.src.q_ready:
            dve.wait_ge(*e)

        def halves(ap, b):
            return ap.rearrange("p (m s b) -> p m s b", s=2, b=b)

        def exponents(l):
            b = H_LEVELS[l]
            if l >= 2:
                dve.wait_ge(*self.jobs[l - 2][-1].full)
            e, src = halves(self.e[:, l % 2, :], b), halves(b_all, b)
            ref = src[:, :, 0, b - 1:b].broadcast_to([P, KC * T // (2 * b), b])
            dve.tensor_tensor(e[:, :, 1, :], src[:, :, 1, :], ref, ALU.subtract)
            dve.tensor_tensor(e[:, :, 0, :], ref, src[:, :, 0, :], ALU.subtract).then_inc(self.diff[l][0], 1)

        n = len(H_LEVELS)
        exponents(0)
        for l, b in enumerate(H_LEVELS):
            if l + 1 < n - 1:
                exponents(l + 1)
            if b:
                dve.wait_ge(*self.exp[l])
                e = halves(self.e[:, l % 2, :], b)
                dve.tensor_tensor(e[:, :, 1, :], e[:, :, 1, :], halves(q_all, b)[:, :, 1, :], ALU.mult)
                dve.tensor_tensor(e[:, :, 0, :], e[:, :, 0, :], halves(k_all, b)[:, :, 0, :], ALU.mult)\
                   .then_inc(self.e_ready[l][0], 1)
            else:
                dve.tensor_copy(k.note[:, 0:1], k.eps[:, 0:1]).then_inc(self.e_ready[l][0], 1)
            if l >= 1:
                self.take(dve, l - 1)
        self.take(dve, n - 1)
        out = k.area(M_OUT, KC, T)
        rs = self.e[:, 0, :].rearrange("p (c t) -> p c t", t=T)
        gain = k.v("hgrn_norm_w", 1 if self.src.layer else 0)
        for j in range(4):
            dve.wait_ge(*self.root[j])
            dve.wait_ge(*self.out_ready[j])
            o = out[:, 2 * j:2 * j + 2, :]
            chain.link(dve.scalar_tensor_tensor(o, o, gain, rs[:, 2 * j:2 * j + 2, :], ALU.mult, ALU.mult))
            dve.wait_ge(*self.src.g_ready[j])
            dve.tensor_tensor(o, o, self.src.g[:, 2 * j:2 * j + 2, :], ALU.mult).then_inc(self.ready[j][0], 1)

    def take(self, dve, l):
        k = self.k
        at = 0 if l == 0 else 2 + 4 * (l - 1)
        if l == 0:
            dve.wait_ge(*self.cleared)
        for j, job in enumerate(self.jobs[l]):
            dve.wait_ge(*job.full)
            data = job.ap[:, :].rearrange("p (h c) -> p h c", c=P)
            if l >= 2:
                dve.wait_ge(*self.taken[at + j - 4])
            if l == 0:
                ins = dve.tensor_copy(self.att[:, 4 * j:4 * j + 4, 1, :], data)
            else:
                b = H_LEVELS[l]
                mask = k.c("upper_pairs", LEVELS.index(b) * P, P) if b else k.c("ident")
                mask = mask.bitcast(U32).unsqueeze(1).broadcast_to([P, 4, P])
                h = 4 * (j // 2)
                ins = dve.copy_predicated(self.att[:, h:h + 4, 2 * (j % 2), :], mask, data)
            ins.then_inc(self.taken[at + j][0], 1)
            if l == len(H_LEVELS) - 1:
                dve.wait_ge(*self.taken[at + j])


def hgrn(layer):
    def make(k):
        src = HgrnIn(k, layer)
        att = HgrnAttention(k, src)
        ready = [att.ready[c // 2] for c in range(KC)]
        return [src, att, OutProjection(k, k.area(M_OUT, KC, T), ready, KC, ln=6 if layer else 0, split=True)]
    return make


MIXERS["hgrn0"] = hgrn(0)
MIXERS["hgrn1"] = hgrn(1)


L_PAD = M_E
L_DT = M_E
L_DEN = L_DT + 2 * 3 * P
L_EN = L_DEN + 2 * T
L_SQ = M_K
L_ROWS = M_B


class MlstmIn(Stage):

    def setup(self):
        k = self.k
        self.x_ready = k.parts_ready
        self.slab0 = k.weights.reserve(12, True)
        self.qk, self.v, self.o = k.area(M_Q, KC, T), k.area(M_V, TT, D), k.area(M_G, KC, T)
        self.pad = k.area(L_PAD, KC, T + CONV_M - 1)
        self.rows = k.area(L_ROWS, 8, T)
        self.gate_taken = k.counter("mlstm_gate_taken").events(2)
        self.gate_jobs = [k.job(e) for e in self.gate_taken]
        self.qk_taken = k.counter("mixer_q").events(4)
        self.v_ready = k.counter("mixer_v").events(4)
        self.o_ready = k.counter("mixer_g").events(4)
        self.jobs = [k.job(e) for e in self.qk_taken + self.v_ready + self.o_ready]
        self.edge = k.counter("pad_clear").event()
        self.convolved = k.counter("convolved").events(KC)
        self.qk_ready = k.counter("mlstm_qk").events(KC)
        self.log1p = k.counter("log1p_ready").event()
        self.rows_ready = k.counter("mlstm_rows").event()
        self.a_taken = k.counter("mlstm_a_columns").event()
        self.a_job = k.job(self.a_taken)

    def tensor(self, pe):
        k = self.k
        for job, name in zip(self.gate_jobs, ("mlstm_i_w", "mlstm_f_w")):
            begin(pe, job)
            w = k.v(name, 0, KC * 8).rearrange("p (k c) -> p k c", k=KC)
            for c in range(KC):
                pe.wait_ge(*self.x_ready[c])
                mm = pe.matmul(job.ap[0:8, 0:T], w[:, c, :], k.h[:, c, :], start=(c == 0), stop=(c == KC - 1))
            mm.then_inc(job.full[0], 1)
        x = k.x_parts[:, 0], k.x_parts[:, 1]
        project_columns(k, pe, x, self.x_ready, self.jobs[0:4])
        project_tokens(k, pe, x, self.jobs[4:8])
        project_columns(k, pe, x, self.x_ready, self.jobs[8:12])
        begin(pe, self.a_job)
        pe.wait_ge(*self.rows_ready)
        for t in range(TT):
            mm = pe.transpose(self.a_job.ap[:, t * 8:t * 8 + 8], self.rows[0:8, 1, t * P:(t + 1) * P],
                              k.c("ident", 0, 8, rows=8))
        mm.then_inc(self.a_job.full[0], 1)

    def scalar(self, act):
        k = self.k
        r = self.rows
        act.wait_ge(*self.edge)
        act.wait_ge(*self.gate_jobs[0].full)
        act.activation(r[0:8, 0, :], self.gate_jobs[0].ap[0:8, 0:T], ACT.Identity, bias=k.v("mlstm_gate_i", rows=8))\
           .then_inc(self.gate_taken[0][0], 1)
        act.wait_ge(*self.gate_jobs[1].full)
        act.activation(r[0:8, 2, :], self.gate_jobs[1].ap[0:8, 0:T], ACT.Identity, bias=k.v("mlstm_gate_f", rows=8))\
           .then_inc(self.gate_taken[1][0], 1)
        act.wait_ge(*self.gate_taken[1])
        k.act.link(act.activation(r[0:8, 3, :], r[0:8, 2, :], ACT.Abs))
        k.act.link(act.activation(r[0:8, 3, :], r[0:8, 3, :], ACT.Exp, scale=-1.0))
        act.activation(r[0:8, 3, :], r[0:8, 3, :], ACT.Ln, bias=k.eps[0:8, 2:3]).then_inc(self.log1p[0], 1)
        for j in range(4):
            k.weights.round_through(act, self.slab0 + j + 1)
            act.wait_ge(*self.jobs[j].full)
            act.activation(self.pad[:, 2 * j:2 * j + 2, 3:3 + T], pair(self.jobs[j]), ACT.Identity)\
               .then_inc(self.qk_taken[j][0], 1)
        for j in range(4):
            k.weights.round_through(act, self.slab0 + 4 + j + 1)
            act.wait_ge(*self.jobs[4 + j].full)
            act.activation(self.v[:, :, j * 256:(j + 1) * 256], pair(self.jobs[4 + j]), ACT.Identity)\
               .then_inc(self.v_ready[j][0], 1)
        for c in range(KC):
            act.wait_ge(*self.convolved[c])
            act.activation(self.qk[:, c, :], self.qk[:, c, :], ACT.Silu).then_inc(self.qk_ready[c][0], 1)
        for j in range(4):
            k.weights.round_through(act, self.slab0 + 8 + j + 1)
            act.wait_ge(*self.jobs[8 + j].full)
            act.activation(self.o[:, 2 * j:2 * j + 2, :], pair(self.jobs[8 + j]), ACT.Sigmoid)\
               .then_inc(self.o_ready[j][0], 1)

    def vector(self, dve):
        k, chain, r = self.k, self.k.dve, self.rows
        for e in self.x_ready:
            dve.wait_ge(*e)
        dve.memset(self.pad[:, :, 0:3], 0.0).then_inc(self.edge[0], 1)
        dve.wait_ge(*self.log1p)
        chain.link(dve.tensor_scalar(r[0:8, 2, :], r[0:8, 2, :], 0.0, None, ALU.min))
        chain.link(dve.tensor_tensor(r[0:8, 2, :], r[0:8, 2, :], r[0:8, 3, :], ALU.subtract))
        chain.link(dve.tensor_tensor_scan(r[0:8, 4, :], k.c("one_row", rows=8), r[0:8, 2, :], 0.0, ALU.mult, ALU.add))
        chain.link(dve.tensor_tensor(r[0:8, 1, :], r[0:8, 0, :], r[0:8, 4, :], ALU.subtract))
        chain.link(dve.tensor_tensor_scan(r[0:8, 5, :], r[0:8, 1, :], r[0:8, 1, :], 0.0, ALU.max, ALU.max))
        dve.scalar_tensor_tensor(r[0:8, 6, :], r[0:8, 4, :], -1.0, r[0:8, 5, :], ALU.mult, ALU.subtract)\
           .then_inc(self.rows_ready[0], 1)
        for c in range(KC):
            k.weights.split_through(dve, self.slab0 + c // 2 + 1)
            dve.wait_ge(*self.qk_taken[c // 2])
            for j in range(CONV_M):
                w = k.v("mlstm_conv_w", j * KC + c)
                src, out = self.pad[:, c, j:j + T], self.qk[:, c, :]
                if j == 0:
                    ins = dve.tensor_scalar(out, src, w, None, ALU.mult)
                else:
                    ins = dve.scalar_tensor_tensor(out, src, w, out, ALU.mult, ALU.add)
                if j < CONV_M - 1:
                    chain.link(ins)
            ins.then_inc(self.convolved[c][0], 1)
        k.weights.split_through(dve, self.slab0 + 12)
        dve.wait_ge(*self.a_job.full)
        dve.tensor_copy(k.cols[:, 0, 0:16], self.a_job.ap[:, 0:16]).then_inc(self.a_taken[0], 1)
        dve.wait_ge(*self.a_taken)


class MlstmAttention(Stage):

    def __init__(self, core, src):
        self.src = src
        super().__init__(core)

    def setup(self):
        k = self.k
        n = HEADS
        self.att = k.area(M_ATT, HEADS, 3, P)
        self.dt = k.area(L_DT, 2, 3 * P)
        self.den, self.en = k.area(L_DEN, 2, T), k.area(L_EN, 2, T)
        self.sq = k.area(L_SQ, KC, T)
        self.out = k.area(M_OUT, KC, T)
        self.diff = k.counter("pair_exponents").events(n)
        self.en_ready = k.counter("mlstm_floor").events(n)
        self.exp = k.counter("pair_exp").events(n)
        self.s_ready = k.counter("mlstm_scores").events(n)
        self.den_ready = k.counter("mlstm_den").events(n)
        self.h_ready = k.counter("mlstm_h").events(n)
        self.row_jobs, self.score_jobs, self.nd_jobs = [], [], []
        for h in range(n + 1):
            if h < n:
                self.row_jobs.append(k.job(self.exp[h]))
                self.score_jobs.append(k.job(self.s_ready[h]))
            if h >= 1:
                self.nd_jobs.append(k.job(self.h_ready[h - 1]))
        self.sq_ready = k.counter("mixer_out_squared").events(4)
        self.sum_jobs = k.take(4)
        self.root = k.counter("mixer_root").events(4)
        self.ready = k.counter("mixer_ready").events(4)

    def tensor(self, pe):
        k, src = self.k, self.src
        pe.wait_ge(*src.a_taken)
        pe.wait_ge(*src.qk_ready[-1])
        pe.wait_ge(*src.v_ready[-1])
        for h in range(HEADS + 1):
            if h < HEADS:
                job = self.row_jobs[h]
                begin(pe, job)
                for i in range(2):
                    mm = pe.matmul(job.ap[:, i * T:(i + 1) * T], k.c("head_rows", h * P, P, rows=8),
                                   src.rows[0:8, 5 + i, :], start=True, stop=True)
                mm.then_inc(job.full[0], 1)
                job = self.score_jobs[h]
                begin(pe, job)
                rows = slice(64 * (h % 2), 64 * (h % 2) + 64)
                q, kk = src.qk[rows, h // 2, :], src.qk[rows, 4 + h // 2, :]
                pe.matmul(job.ap[:, 0:T], kk[:, 0:P], q, start=True, stop=True)
                pe.matmul(job.ap[:, T:T + P], kk[:, P:T], q[:, P:T], start=True, stop=True).then_inc(job.full[0], 1)
            if h >= 1:
                w = h - 1
                job = self.nd_jobs[w]
                begin(pe, job)
                pe.wait_ge(*self.s_ready[w])
                for i in range(2):
                    for t in range(2):
                        left = k.c("ones") if i else src.v[:, t, w * P:(w + 1) * P]
                        right = self.att[:, w, 0:2, :] if t == 0 else self.att[:, w, 2, :]
                        mm = pe.matmul(job.ap[:, i * T + t * P:(i + 1) * T], left, right, start=(t == 0), stop=(t == 1))
                mm.then_inc(job.full[0], 1)
        sq = k.area(L_SQ, KC * T)
        for j, job in enumerate(self.sum_jobs):
            begin(pe, job)
            pe.wait_ge(*self.sq_ready[j])
            pe.matmul(job.ap[:, :], k.c("ones"), sq[:, j * 512:(j + 1) * 512], start=True, stop=True)\
              .then_inc(job.full[0], 1)

    def scalar(self, act):
        k = self.k
        for h in range(HEADS + 1):
            if h < HEADS:
                act.wait_ge(*self.row_jobs[h].full)
                if h >= 2:
                    act.wait_ge(*self.h_ready[h - 2])
                act.activation(self.en[:, h % 2, :], self.row_jobs[h].ap[:, T:2 * T], ACT.Exp)\
                   .then_inc(self.en_ready[h][0], 1)
                act.wait_ge(*self.diff[h])
                act.activation(self.dt[:, h % 2, :], self.dt[:, h % 2, :], ACT.Exp, scale=-1.0)\
                   .then_inc(self.exp[h][0], 1)
            if h >= 1:
                w = h - 1
                act.wait_ge(*self.nd_jobs[w].full)
                act.activation(self.den[:, w % 2, :], self.nd_jobs[w].ap[:, T:2 * T], ACT.Abs)\
                   .then_inc(self.den_ready[w][0], 1)
        sq = k.area(L_SQ, KC * T)
        for j, job in enumerate(self.sum_jobs):
            act.wait_ge(*self.h_ready[2 * j + 1])
            act.activation(self.sq[:, 2 * j:2 * j + 2, :], self.out[:, 2 * j:2 * j + 2, :], ACT.Square)\
               .then_inc(self.sq_ready[j][0], 1)
        for j, job in enumerate(self.sum_jobs):
            act.wait_ge(*job.full)
            flat = sq[:, j * 512:(j + 1) * 512]
            act.activation(flat, job.ap[:, :], ACT.Ln, bias=k.eps[:, 0:1], scale=1.0 / P).then_inc(job.free[0], 1)
        for j, job in enumerate(self.sum_jobs):
            act.wait_ge(*job.free)
            flat = sq[:, j * 512:(j + 1) * 512]
            act.activation(flat, flat, ACT.Exp, scale=-0.5).then_inc(self.root[j][0], 1)

    def vector(self, dve):
        k, chain = self.k, self.k.dve
        for h in range(HEADS + 1):
            if h < HEADS:
                dve.wait_ge(*self.row_jobs[h].full)
                dve.wait_ge(*self.en_ready[h])
                if h >= 2:
                    dve.wait_ge(*self.s_ready[h - 2])
                m = self.row_jobs[h].ap
                dve.tensor_scalar(self.dt[:, h % 2, 0:T], m[:, 0:T], k.cols[:, 0, h:h + 1], 0.0,
                                  ALU.subtract, ALU.max)
                dve.tensor_scalar(self.dt[:, h % 2, T:T + P], m[:, P:T], k.cols[:, 0, 8 + h:9 + h], 0.0,
                                  ALU.subtract, ALU.max).then_inc(self.diff[h][0], 1)
            if h >= 1:
                self.divide(dve, h - 1)
            if h < HEADS:
                dve.wait_ge(*self.exp[h])
                dve.wait_ge(*self.score_jobs[h].full)
                att = self.att[:, h, :, :].rearrange("p a b -> p (a b)")
                chain.link(dve.scalar_tensor_tensor(att, self.score_jobs[h].ap[:, 0:3 * P], 0.125,
                                                    self.dt[:, h % 2, :], ALU.mult, ALU.mult))
                both = self.att[:, h, 0:3:2, :]
                dve.tensor_tensor(both, both, k.c("upto").unsqueeze(1).broadcast_to([P, 2, P]), ALU.mult)\
                   .then_inc(self.s_ready[h][0], 1)
        for j in range(4):
            dve.wait_ge(*self.root[j])
            for c in (2 * j, 2 * j + 1):
                ins = dve.scalar_tensor_tensor(self.out[:, c, :], self.out[:, c, :], k.v("mlstm_norm_w", c),
                                               self.sq[:, c, :], ALU.mult, ALU.mult)
            chain.link(ins)
            o = self.out[:, 2 * j:2 * j + 2, :]
            dve.wait_ge(*self.src.o_ready[j])
            dve.tensor_tensor(o, o, self.src.o[:, 2 * j:2 * j + 2, :], ALU.mult).then_inc(self.ready[j][0], 1)

    def divide(self, dve, h):
        k, chain = self.k, self.k.dve
        den = self.den[:, h % 2, :]
        dve.wait_ge(*self.den_ready[h])
        dve.wait_ge(*self.en_ready[h])
        chain.link(dve.tensor_tensor(den, den, self.en[:, h % 2, :], ALU.max))
        chain.link(dve.reciprocal(den, den))
        dve.tensor_tensor(self.out[:, h, :], self.nd_jobs[h].ap[:, 0:T], den, ALU.mult)\
           .then_inc(self.h_ready[h][0], 1)


def mlstm(k):
    src = MlstmIn(k)
    att = MlstmAttention(k, src)
    ready = [att.ready[c // 2] for c in range(KC)]
    return [src, att, OutProjection(k, k.area(M_OUT, KC, T), ready, KC, ln=2, split=True)]


MIXERS["mlstm"] = mlstm


S_U = M_Q
S_BC = M_V
S_PH = S_BC + 4096
S_TAB = S_PH + 4 * T
S_T1 = S_TAB + 4 * T
S_T2 = S_T1 + 2 * T
S_G = S_T2 + 2 * T
S_H = S_G + 2 * T
R_DT, R_MAG, R_TH, R_N, R_SIN, R_COS, R_CR, R_CI, R_T1, R_T2, R_T3 = range(11)


class S5In(Stage):

    def setup(self):
        k = self.k
        self.x_ready = k.h_ready
        self.slab0 = k.weights.reserve(4, False)
        self.u = k.area(S_U, KC, T)
        self.u_ready = k.counter("mixer_q").events(4)
        self.jobs = [k.job(e) for e in self.u_ready]
        self.loaded = k.counter("s5_matrices_loaded")
        self.dt_ready = k.counter("s5_dt").event()
        self.prod_ready = k.counter("s5_products").events(2)
        self.exp_ready = k.counter("s5_exp").event()
        self.sin_ready = k.counter("s5_sin").event()
        self.ready = k.counter("decay_cumulated").event()

    def tensor(self, pe):
        project_columns(self.k, pe, (self.k.h,), self.x_ready, self.jobs)

    def scalar(self, act):
        k, c = self.k, self.k.cols
        for e in self.x_ready:
            act.wait_ge(*e)
        act.dma_start(k.area(S_BC, 4096), k.s5_bc).then_inc(self.loaded.sem, 16)
        act.activation(c[:, R_DT, :], k.v("s5_log_dt", 0, S5_TILES), ACT.Exp).then_inc(self.dt_ready[0], 1)
        act.wait_ge(*self.prod_ready[0])
        act.activation(c[:, R_MAG, :], c[:, R_MAG, :], ACT.Exp).then_inc(self.exp_ready[0], 1)
        act.wait_ge(*self.prod_ready[1])
        act.activation(c[:, R_SIN, :], c[:, R_TH, :], ACT.Sin)
        act.activation(c[:, R_COS, :], c[:, R_TH, :], ACT.Sin, scale=0.5).then_inc(self.sin_ready[0], 1)
        for j in range(4):
            act.wait_ge(*self.jobs[j].full)
            act.activation(self.u[:, 2 * j:2 * j + 2, :], pair(self.jobs[j]), ACT.Identity)\
               .then_inc(self.u_ready[j][0], 1)

    def vector(self, dve):
        k, c, link = self.k, self.k.cols, self.k.dve.link
        are, aim = k.v("s5_a_re", 0, S5_TILES), k.v("s5_a_im", 0, S5_TILES)
        mult, add, sub = ALU.mult, ALU.add, ALU.subtract

        def tt(out, a, b, op):
            link(dve.tensor_tensor(c[:, out, :], a, b, op))

        row = lambda i: c[:, i, :]
        dve.wait_ge(*self.dt_ready)
        dve.tensor_tensor(c[:, R_MAG, :], are, row(R_DT), mult).then_inc(self.prod_ready[0][0], 1)
        tt(R_TH, aim, row(R_DT), mult)
        reduce_angle(dve, link, row(R_TH), row(R_N), self.prod_ready[1])
        link(dve.tensor_scalar(row(R_DT), row(R_TH), 1.0 / TWO_PI, None, mult))
        dve.wait_ge(*self.exp_ready)
        dve.wait_ge(*self.sin_ready)
        tt(R_COS, row(R_COS), row(R_COS), mult)
        link(dve.tensor_scalar(row(R_COS), row(R_COS), -2.0, 1.0, mult, add))
        tt(R_T1, row(R_MAG), row(R_COS), mult)
        link(dve.tensor_scalar(row(R_T1), row(R_T1), -1.0, None, add))
        tt(R_T2, row(R_MAG), row(R_SIN), mult)
        tt(R_T3, are, are, mult)
        tt(R_N, aim, aim, mult)
        tt(R_T3, row(R_T3), row(R_N), add)
        link(dve.reciprocal(row(R_T3), row(R_T3)))
        tt(R_CR, row(R_T1), are, mult)
        tt(R_N, row(R_T2), aim, mult)
        tt(R_CR, row(R_CR), row(R_N), add)
        tt(R_CR, row(R_CR), row(R_T3), mult)
        tt(R_CI, row(R_T2), are, mult)
        tt(R_N, row(R_T1), aim, mult)
        tt(R_CI, row(R_CI), row(R_N), sub)
        tt(R_CI, row(R_CI), row(R_T3), mult)
        dve.wait_ge(self.loaded.sem, 16)
        out = k.area(S_BC + 2048, 2, S5_TILES, 32)
        t1, t2 = k.area(S_PH, S5_TILES, 32), k.area(S_T1, S5_TILES, 32)
        cr = row(R_CR).unsqueeze(2).broadcast_to([P, S5_TILES, 32])
        ci = row(R_CI).unsqueeze(2).broadcast_to([P, S5_TILES, 32])
        link(dve.tensor_tensor(t1, out[:, 0, :, :], ci, mult))
        link(dve.tensor_tensor(t2, out[:, 1, :, :], ci, mult))
        link(dve.tensor_tensor(out[:, 0, :, :], out[:, 0, :, :], cr, mult))
        link(dve.tensor_tensor(out[:, 0, :, :], out[:, 0, :, :], t2, sub))
        link(dve.tensor_tensor(out[:, 1, :, :], out[:, 1, :, :], cr, mult))
        link(dve.tensor_tensor(out[:, 1, :, :], out[:, 1, :, :], t1, add))
        dve.tensor_scalar(out[:, 1, :, :], out[:, 1, :, :], -1.0, None, mult).then_inc(self.ready[0], 1)
        dve.wait_ge(*self.ready)


def reduce_angle(dve, link, x, n, last):
    link(dve.tensor_scalar(n, x, 1.0 / TWO_PI, ROUND, ALU.mult, ALU.add))
    link(dve.tensor_scalar(n, n, ROUND, None, ALU.subtract))
    for part in (PI_1, PI_2, PI_3):
        link(dve.scalar_tensor_tensor(x, n, -part, x, ALU.mult, ALU.add))
    dve.tensor_scalar(x, x, 3.1415925, -3.1415925, ALU.min, ALU.max).then_inc(last[0], 1)
    dve.wait_ge(*last)


class S5Scan(Stage):

    def __init__(self, core, src):
        self.src = src
        super().__init__(core)

    def setup(self):
        k = self.k
        n = S5_TILES
        self.phase = k.area(S_PH, 2, 2, T)
        self.table = k.area(S_TAB, 2, 2, T)
        self.t1, self.t2, self.g = (k.area(at, 2, T) for at in (S_T1, S_T2, S_G))
        self.hs = k.area(S_H, 2, 2, T)
        self.out = k.area(M_OUT, KC, T)
        self.phase_ready = k.counter("s5_phase").events(n)
        self.sin_done = k.counter("pair_exp").events(n)
        self.table_ready = k.counter("pair_operands").events(n)
        self.bu_used = k.counter("s5_bu_used").events(n)
        self.h_ready = k.counter("s5_state").events(n)
        self.y_ready = k.counter("s5_y").events(KC)
        self.ready = k.counter("mixer_ready_act").events(KC)
        self.bu_jobs, self.y_jobs = [], []
        for i in range(n + 1):
            if i < n:
                self.bu_jobs.append(k.job(self.bu_used[i]))
            if i >= 1 and (i - 1) % 4 == 0:
                self.y_jobs.append(k.job(self.y_ready[(i - 1) // 4]))

    def tensor(self, pe):
        k = self.k
        b = k.area(S_BC, KC * 2, P)
        c = k.area(S_BC + 2048, 2, S5_TILES, 32)
        pe.wait_ge(self.src.loaded.sem, 16)
        pe.wait_ge(*self.src.ready)
        for i in range(S5_TILES + 1):
            if i < S5_TILES:
                j, r = i // 4, i % 4
                rows = slice(32 * r, 32 * r + 32)
                job = self.bu_jobs[i]
                begin(pe, job)
                pe.wait_ge(*self.src.u_ready[j // 2])
                for part in range(2):
                    mm = pe.matmul(job.ap[:, part * T:(part + 1) * T], b[rows, 2 * j + part, :], self.src.u[rows, j, :],
                                   start=True, stop=True, tile_position=(32 * r, 0))
                mm.then_inc(job.full[0], 1)
            if i >= 1:
                w = i - 1
                j, r = w // 4, w % 4
                job = self.y_jobs[j]
                if r == 0:
                    begin(pe, job)
                pe.wait_ge(*self.h_ready[w])
                for part in range(2):
                    mm = pe.matmul(job.ap[32 * r:32 * r + 32, 0:T], c[:, part, w, :], self.hs[:, w % 2, part, :],
                                   start=(part == 0), stop=(part == 1), tile_position=(0, 32 * r))
                mm.then_inc(self.y_sem(w), 1)

    def y_sem(self, w):
        return self.y_jobs[w // 4].full[0] if w % 4 == 3 else self.k.counter("s5_states_used").sem

    def states_used(self, w):
        if w % 4 == 3:
            return self.y_jobs[w // 4].full
        return (self.k.counter("s5_states_used").sem, w - w // 4 + 1)

    def scalar(self, act):
        k = self.k
        for i in range(S5_TILES):
            act.wait_ge(*self.phase_ready[i])
            if i >= 2:
                act.wait_ge(*self.h_ready[i - 2])
            act.activation(self.table[:, i % 2, 1, :], self.phase[:, i % 2, 0, :], ACT.Sin, scale=TURN)
            act.activation(self.table[:, i % 2, 0, :], self.phase[:, i % 2, 0, :], ACT.Sin, scale=0.5 * TURN)\
               .then_inc(self.sin_done[i][0], 1)
            act.wait_ge(*self.sin_done[i])
            k.act.link(act.activation(self.table[:, i % 2, 0, :], self.table[:, i % 2, 0, :], ACT.Square))
            act.activation(self.table[:, i % 2, 0, :], self.table[:, i % 2, 0, :], ACT.Identity,
                           bias=k.eps[:, 2:3], scale=-2.0).then_inc(self.table_ready[i][0], 1)
        for c in range(KC):
            act.wait_ge(*self.y_ready[c])
            act.activation(self.out[:, c, :], self.out[:, c, :], ACT.Gelu_apprx_tanh).then_inc(self.ready[c][0], 1)

    def gpsimd(self, pool):
        k = self.k
        pool.wait_ge(*self.src.ready)
        for i in range(S5_TILES):
            if i >= 2:
                pool.wait_ge(*self.sin_done[i - 2])
            x, n = self.phase[:, i % 2, 0, :], self.phase[:, i % 2, 1, :]
            turns = k.cols[:, R_DT, i:i + 1].broadcast_to([P, T])
            k.pool.link(pool.tensor_tensor(x, k.c("time"), turns, ALU.mult))
            k.pool.link(pool.tensor_scalar(n, x, ROUND, ROUND, ALU.add, ALU.subtract))
            pool.tensor_tensor(x, x, n, ALU.subtract).then_inc(self.phase_ready[i][0], 1)

    def vector(self, dve):
        k, link = self.k, self.k.dve.link
        for i in range(S5_TILES):
            dve.wait_ge(*self.table_ready[i])
            job = self.bu_jobs[i]
            dve.wait_ge(*job.full)
            cos = over_chunks(self.table[:, i % 2, 0, :], 2)
            sin = over_chunks(self.table[:, i % 2, 1, :], 2)
            dve.tensor_tensor(self.t1, pair(job), cos, ALU.mult)
            dve.tensor_tensor(self.t2, pair(job), sin, ALU.mult).then_inc(self.bu_used[i][0], 1)
            dve.wait_ge(*self.bu_used[i])
            dve.tensor_tensor(self.g[:, 0, :], self.t1[:, 0, :], self.t2[:, 1, :], ALU.add)
            link(dve.tensor_tensor(self.g[:, 1, :], self.t1[:, 1, :], self.t2[:, 0, :], ALU.subtract))
            mag = k.cols[:, R_MAG, i:i + 1].broadcast_to([P, T])
            h = self.hs[:, i % 2, :, :]
            if i >= 2:
                dve.wait_ge(*self.states_used(i - 2))
            dve.tensor_tensor_scan(h[:, 0, :], mag, self.g[:, 0, :], 0.0, ALU.mult, ALU.add)
            link(dve.tensor_tensor_scan(h[:, 1, :], mag, self.g[:, 1, :], 0.0, ALU.mult, ALU.add))
            dve.tensor_tensor(self.t1, h, cos, ALU.mult)
            link(dve.tensor_tensor(self.t2, h, sin, ALU.mult))
            dve.tensor_tensor(h[:, 0, :], self.t1[:, 0, :], self.t2[:, 1, :], ALU.subtract)
            dve.tensor_tensor(h[:, 1, :], self.t1[:, 1, :], self.t2[:, 0, :], ALU.add).then_inc(self.h_ready[i][0], 1)
            dve.wait_ge(*self.h_ready[i])
            if i % 4 == 1 and i > 4:
                self.finish(dve, i // 4 - 1)
        self.finish(dve, KC - 1)

    def finish(self, dve, c):
        dve.wait_ge(*self.y_jobs[c].full)
        dve.scalar_tensor_tensor(self.out[:, c, :], self.src.u[:, c, :], self.k.v("s5_d", c),
                                 self.y_jobs[c].ap[:, 0:T], ALU.mult, ALU.add).then_inc(self.y_ready[c][0], 1)


def s5(k):
    src = S5In(k)
    scan = S5Scan(k, src)
    return [src, scan, OutProjection(k, k.area(M_OUT, KC, T), scan.ready, KC, ln=4, glu=True, split=True)]


MIXERS["s5"] = s5




def parts(k, which):
    out = [Start(k)]
    a = k.area(AT_A, KC, T)
    for name, follower in zip(which, list(which[1:]) + [None]):
        if name == "mod0" or name == "mod1":
            layer = int(name[-1])
            k.mod, k.coef = k.mods[layer], k.coefs[layer]
            if "hybrid" not in which:
                out.append(Modulation(k, layer, COND // 2))
            elif layer == 0:
                out.append(Modulation(k, 0, MOD_FIRST))
        elif name.startswith("ffn_rms"):
            pre = PreNorm(k, k.h[:, :, :], k.h_ready, k.area(AT_Y, KC, T), k.coef[:, 3, :], k.mod[:, 3 * KC:4 * KC, 0],
                          split=True)
            out += [pre] + feed_forward(k, pre.parts, pre.ready, rms_gain=k.coef[:, 4, :],
                                        split=follower in SPLIT_MIXERS)
        elif name.startswith("ffn_ln"):
            out += feed_forward(k, (k.x_parts[:, 0], k.x_parts[:, 1]), k.parts_ready, ln=2 * int(name[-1]) + 1,
                                split=follower in SPLIT_MIXERS)
        else:
            out += MIXERS[name](k)
    return out


def program(nc, stream, vec, const, x, ctx_x, s5_bc, out, which):
    n_slabs = stream.shape[0]
    with ExitStack() as ctx:
        k = Core(nc, ctx, vec, const)
        k.eps = ctx.enter_context(nc.sbuf_tensor("epsilons", [P, 4], F32))
        k.note = ctx.enter_context(nc.sbuf_tensor("note", [P, 2], F32))
        k.ctx_x, k.s5_bc = ctx_x, s5_bc
        stages = parts(k, which)
        stored = k.sem("stored")
        eps_ready = k.sem("eps_ready")
        block = ctx.enter_context(nc.Block())

        @block.sync
        def _(sp):
            sp.dma_start(k.const[:, :], const).then_inc(k.consts_loaded, 16)
            sp.dma_start(k.vec[:, :], vec).then_inc(k.consts_loaded, 16)
            sp.dma_start(k.h[:, :, :], x).then_inc(k.consts_loaded, 16)
            sp.dma_start(k.area(H_END, KC, T), ctx_x).then_inc(k.consts_loaded, 16)
            for n in range(n_slabs):
                if n >= RING:
                    sp.wait_ge(*k.weights.free(n - RING))
                sp.dma_start(k.ring[:, n % RING, :], stream[n]).then_inc(k.loaded[n % RING], 16)
            for event in k.h_ready:
                sp.wait_ge(*event)
            sp.dma_start(out, k.h[:, :, :]).then_inc(stored, 16)
            sp.wait_ge(stored, 16)

        @block.tensor
        def _(pe):
            for stage in stages:
                stage.tensor(pe)
            assert k.weights.at == n_slabs, (k.weights.at, n_slabs)

        @block.scalar
        def _(act):
            k.act = Chain(act, k.act_chain)
            act.wait_ge(eps_ready, 3)
            for stage in stages:
                stage.scalar(act)

        @block.vector
        def _(dve):
            k.dve = Chain(dve, k.dve_chain)
            dve.memset(k.eps[:, 0:1], EPS).then_inc(eps_ready, 1)
            dve.memset(k.eps[:, 1:2], LN_EPS).then_inc(eps_ready, 1)
            dve.memset(k.eps[:, 2:3], 1.0).then_inc(eps_ready, 1)
            for stage in stages:
                stage.vector(dve)

        @block.gpsimd
        def _(pool):
            k.pool = Chain(pool, k.pool_chain)
            for stage in stages:
                stage.gpsimd(pool)


ORDER = ["mod0", "hybrid", "ffn_rms0", "mod1", "conformer", "ffn_rms1",
         "hgrn0", "ffn_ln0", "mlstm", "ffn_ln1", "s5", "ffn_ln2", "hgrn1", "ffn_ln3"]


def by_columns(w):
    n = w.shape[1]
    return w.reshape(KC, P, n // 256, 256).transpose(2, 1, 0, 3).reshape(n // 256, P, SLAB)


def by_tiles(w):
    rows = w.shape[0] // P
    tiles = w.reshape(rows, P, KC, P).transpose(2, 0, 1, 3).reshape(-1, SLAB_TILES, P, P)
    return tiles.transpose(0, 2, 1, 3).reshape(-1, P, SLAB)


def halves_paired(w):
    n = w.shape[1] // 2
    return w.reshape(w.shape[0], 2, n // P, P).transpose(0, 2, 1, 3).reshape(w.shape[0], 2 * n)


def hyb_columns():
    q = 2064 + np.concatenate([np.r_[j * 64:(j + 1) * 64, (j + 4) * 64:(j + 5) * 64] for j in range(4)])
    return np.r_[0:2048, q, 2576:2832]


def hyb_out_rows():
    return np.r_[0:512, 512 + (hyb_columns()[2048:2560] - 2064)]


def slabs(name, i, which):
    beside = "hybrid" in which
    end = MOD_FIRST + MOD_EARLY
    out = {
        "mod0": lambda: [by_columns(i["w_mod"][0])[:MOD_FIRST if beside else COND // 2]],
        "mod1": lambda: [by_columns(i["w_mod"][1])[:0 if beside else COND // 2]],
        "hybrid": lambda: [by_columns(i["w_mod"][0])[MOD_FIRST:end],
                           by_columns(i["hyb_w_in"][0][:, hyb_columns()]),
                           by_columns(i["w_mod"][0])[end:], by_columns(i["w_mod"][1]),
                           by_columns(i["hyb_w_out"][0][hyb_out_rows()])],
        "conformer": lambda: [by_columns(halves_paired(i["conf_w_in"][0])), by_columns(i["conf_w_out"][0])],
        "mlstm": lambda: [by_columns(i["mlstm_w_in_2"][0][:, :3072]), by_columns(i["mlstm_w_out_2"][0])],
        "s5": lambda: [by_columns(i["s5_w_in_2"][0]), by_columns(halves_paired(i["s5_w_out_2"][0]))],
    }
    for j in range(2):
        out[f"ffn_rms{j}"] = lambda j=j: [by_columns(halves_paired(i["w_ffn_in"][j])), by_tiles(i["w_ffn_out"][j])]
        out[f"hgrn{j}"] = lambda j=j: [by_columns(i["hgrn_w_in_2"][j]), by_columns(i["hgrn_w_out_2"][j])]
    for j in range(4):
        out[f"ffn_ln{j}"] = lambda j=j: [by_columns(halves_paired(i["ffn_w_gate_up_2"][j])),
                                         by_tiles(i["ffn_w_down_2"][j])]
    return out[name]()


def pack_vectors(i):
    def chunks(a):
        return np.asarray(a).reshape(-1, P).T

    def rows(a):
        a = np.asarray(a).reshape(-1)
        return np.pad(a, (0, P - len(a)))[:, None]

    def small(w):
        return np.asarray(w).reshape(KC, P, 8).transpose(1, 0, 2).reshape(P, KC * 8)

    def states(a):
        return np.asarray(a).reshape(S5_TILES, P).T

    v = {n: chunks(i[n]) for n in ("c", "c_ctx", "b_mod", "g_mix_pre", "g_mix_post", "g_ffn_pre", "g_ffn_post",
                                   "hyb_conv_w", "hyb_out_norm", "conf_b_in", "conf_dw_w", "conf_dw_b",
                                   "conf_ln_g", "conf_ln_b", "conf_b_out")}
    v["hyb_q_norm"] = chunks(np.tile(i["hyb_q_norm"][0], 2))
    v["hyb_k_norm"] = chunks(np.tile(i["hyb_k_norm"][0], 2))
    v["hyb_a_log"], v["hyb_dt_bias"] = rows(i["hyb_a_log"]), rows(i["hyb_dt_bias"])
    v["hyb_beta_w"], v["hyb_g_w"] = small(i["hyb_w_in"][0][:, 2048:2056]), small(i["hyb_w_in"][0][:, 2056:2064])
    v["hgrn_norm_w"] = chunks(i["hgrn_norm_w_2"])
    v["lb_logits"] = chunks(i["hgrn_lb_logits_2"])
    v["mlstm_conv_w"] = chunks(i["mlstm_conv_w_2"])
    v["mlstm_gate_i"], v["mlstm_gate_f"] = rows(i["mlstm_gate_b_2"][0, :8]), rows(i["mlstm_gate_b_2"][0, 8:])
    v["mlstm_norm_w"] = chunks(i["mlstm_norm_w_2"])
    v["mlstm_i_w"], v["mlstm_f_w"] = (small(i["mlstm_w_in_2"][0][:, 3072 + 8 * j:3080 + 8 * j]) for j in range(2))
    v["s5_a_re"], v["s5_a_im"] = states(i["s5_a_re_2"]), states(i["s5_a_im_2"])
    v["s5_log_dt"] = states(np.repeat(i["s5_log_dt_2"].reshape(-1), S5_STATE))
    v["s5_d"] = chunks(i["s5_d_2"])
    v["ln_g"], v["ln_b"] = chunks(i["ln_g_2"]), chunks(i["ln_b_2"])
    for name, n in VECTORS:
        assert v[name].shape == (P, n), (name, v[name].shape)
    return np.ascontiguousarray(np.concatenate([v[n] for n, _ in VECTORS], 1))


def pack_s5(i):
    b = np.zeros((P, KC, 2, P), np.float32)
    c = np.zeros((P, 2, S5_TILES, 32), np.float32)
    for part, (wb, wc) in enumerate(((i["s5_b_re_2"][0], i["s5_c_re_2"][0]), (i["s5_b_im_2"][0], i["s5_c_im_2"][0]))):
        for g in range(GROUPS):
            chunk, row = g // 8, (g % 8) * S5_CH
            half = g % 2
            b[row:row + S5_CH, chunk, part, half * 64:half * 64 + 64] = wb[g].T
            c[half * 64:half * 64 + 64, part, g // 2, half * S5_CH:(half + 1) * S5_CH] = wc[g].T
    return np.concatenate([b.reshape(P, -1), c.reshape(P, -1)], 1)


def pack_constants():
    t = np.arange(P)
    c = {"ident": np.eye(P), "mean": np.full((P, P), 1.0 / D), "ones": np.ones((P, P)),
         "ones64": np.kron(np.eye(2), np.ones((64, 64))),
         "upto": t[:, None] <= t[None, :], "from_": t[:, None] >= t[None, :]}
    turn = np.zeros((P, P))
    for base in range(0, P, 32):
        for j in range(16):
            turn[base + 16 + j, base + j] = -1.0
            turn[base + j, base + 16 + j] = 1.0
    c["rope_turn"] = turn
    pairs = []
    for b in LEVELS:
        same = t[:, None] // (2 * b) == t[None, :] // (2 * b)
        pairs.append(same & ((t[:, None] // b) % 2 == 1) & ((t[None, :] // b) % 2 == 0))
    c["lower_pairs"] = np.concatenate(pairs, 1)
    c["upper_pairs"] = np.concatenate([m.T for m in pairs], 1)
    n = np.arange(T)
    freq = 10000.0 ** (-np.arange(16) / 16.0)
    angle = np.concatenate([freq[:, None] * (n // 64), freq[:, None] * (n // 64),
                            freq[:, None] * (n % 64), freq[:, None] * (n % 64)], 0)
    c["cos"], c["sin"] = np.tile(np.cos(angle), (2, 1)), np.tile(np.sin(angle), (2, 1))
    sel = np.zeros((P, HEADS, P))
    for h in range(HEADS):
        sel[h, h, :] = 1.0
    c["head_rows"] = sel.reshape(P, -1)
    c["one_row"] = np.ones((P, T))
    c["time"] = np.tile(np.arange(T), (P, 1))
    for name, size in CONSTANTS:
        assert c[name].shape == (P, size), name
    return np.ascontiguousarray(np.concatenate([c[n] for n, _ in CONSTANTS], 1).astype(np.float32))


def feature_major(a):
    return np.ascontiguousarray(np.asarray(a).reshape(T, KC, P).transpose(2, 1, 0))


def launch_arrays(inputs, which):
    i = {n: np.asarray(a) for n, a in inputs.items()}
    stream = np.concatenate([s for name in which for s in slabs(name, i, which)], 0)
    return {"stream": stream, "vectors": pack_vectors(i), "constants": pack_constants(),
            "x": feature_major(i["x"][0]), "ctx": feature_major(i["ctx"][0]), "s5_bc": pack_s5(i)}


def build(nc, arrays, which):
    aps = {n: nc.dram_tensor(f"{n}_dram", a.shape, mybir.dt.from_np(a.dtype), kind="ExternalInput").ap()
           for n, a in arrays.items()}
    out = nc.dram_tensor("out_dram", (P, KC, T), F32, kind="ExternalOutput").ap()
    program(nc, aps["stream"], aps["vectors"], aps["constants"], aps["x"], aps["ctx"], aps["s5_bc"], out, which)


def kernel(**inputs):
    import concourse.bacc as _bacc
    from concourse.bass_utils import run_bass_kernel_spmd as _run

    arrays = launch_arrays(inputs, ORDER)
    nc = _bacc.Bacc("TRN2", target_bir_lowering=False, num_devices=1)
    build(nc, arrays, ORDER)
    r = _run(nc, [{f"{n}_dram": a for n, a in arrays.items()}], core_ids=[0])
    got = r.results[0]["out_dram"]
    return np.ascontiguousarray(got.transpose(2, 1, 0).reshape(1, T, D))
```
